# Optimizing a Trainium2 kernel written in Bass

```python
import jax, jax.numpy as jnp
from jax import lax
import numpy as np

D_MODEL = 2048
BATCH = 1
SEQ = 512
DEPTH = 1

CONV_WIDTH = D_MODEL // 2
CONV_K = 3
MLSTM_WIDTH = D_MODEL - CONV_WIDTH
MLSTM_HEADS = 4
MLSTM_V = MLSTM_WIDTH // MLSTM_HEADS
MLSTM_QK = MLSTM_V // 2
MLSTM_CHUNK = 64
N_GATE_COLS = 2 * 2 * MLSTM_HEADS
IN_SIZES = [CONV_WIDTH, CONV_WIDTH, CONV_WIDTH,
            MLSTM_HEADS * MLSTM_QK, MLSTM_HEADS * MLSTM_QK,
            MLSTM_WIDTH, MLSTM_WIDTH, N_GATE_COLS]
IN_COLS = sum(IN_SIZES)
PEER_HEADS = 8
N_KEYS = 128
N_EXPERTS = N_KEYS * N_KEYS
PEER_TOPK = 16
PEER_KEY_DIM = 256
PEER_BLOCK = 128
LN_EPS = 1e-5
ALPHA = (2 * DEPTH) ** 0.25
BETA = (8 * DEPTH) ** -0.25

kernel_name = 'hybrid_conv_mlstm_peer_deepnorm_adaln'

def _ln_stats(x):
    xf = x.astype(jnp.float32)
    mu = jnp.mean(xf, -1, keepdims=True)
    var = jnp.mean(jnp.square(xf - mu), -1, keepdims=True)
    return (xf - mu) * lax.rsqrt(var + LN_EPS)

def _modulate(x, shift, scale):
    return (_ln_stats(x) * (1.0 + scale[:, None, :].astype(jnp.float32))
            + shift[:, None, :].astype(jnp.float32)).astype(x.dtype)

def _post_norm(z, w, b):
    return (_ln_stats(z) * w.astype(jnp.float32) + b.astype(jnp.float32)).astype(z.dtype)

def _short_conv(z, w, b):
    ch = z.shape[-1]
    y = lax.conv_general_dilated(z, w[:, None, :].astype(z.dtype), window_strides=(1,),
                                 padding=[(CONV_K // 2, CONV_K // 2)],
                                 dimension_numbers=('NWC', 'WIO', 'NWC'),
                                 feature_group_count=ch)
    return y + b

def _mlstm_chunk_scan(q, k, v, log_f, log_i):
    G, S, H, dk = q.shape
    dv = v.shape[-1]
    L = MLSTM_CHUNK
    nc = S // L

    def chunks(t):
        t = t.reshape((G, nc, L, H) + t.shape[3:])
        return jnp.moveaxis(t, (1, 3), (0, 2))

    tril = jnp.tril(jnp.ones((L, L), dtype=bool))

    def body(carry, xs):
        C, n, m = carry
        qc, kc, vc, lf, ig = xs
        b = jnp.cumsum(lf, axis=-1)
        d = b[..., :, None] - b[..., None, :] + ig[..., None, :]
        d = jnp.where(tril, d, -jnp.inf)
        inter = b + m[..., None]
        m_t = jnp.maximum(inter, jnp.max(d, axis=-1))
        w_intra = jnp.exp(d - m_t[..., None])
        w_inter = jnp.exp(inter - m_t)
        s = jnp.einsum('ghtd,ghsd->ghts', qc, kc) * w_intra
        num = (jnp.einsum('ghts,ghsv->ghtv', s, vc)
               + w_inter[..., None] * jnp.einsum('ghtd,ghdv->ghtv', qc, C))
        den = jnp.sum(s, -1) + w_inter * jnp.einsum('ghtd,ghd->ght', qc, n)
        h = num / jnp.maximum(jnp.abs(den), jnp.exp(-m_t))[..., None]
        b_last = b[..., -1]
        a = b_last[..., None] - b + ig
        m_new = jnp.maximum(b_last + m, jnp.max(a, axis=-1))
        w_a = jnp.exp(a - m_new[..., None])
        decay = jnp.exp(b_last + m - m_new)
        C_new = decay[..., None, None] * C + jnp.einsum('ghs,ghsd,ghsv->ghdv', w_a, kc, vc)
        n_new = decay[..., None] * n + jnp.einsum('ghs,ghsd->ghd', w_a, kc)
        return (C_new, n_new, m_new), h

    init = (jnp.zeros((G, H, dk, dv), jnp.float32), jnp.zeros((G, H, dk), jnp.float32),
            jnp.zeros((G, H), jnp.float32))
    xs = (chunks(q), chunks(k), chunks(v), chunks(log_f), chunks(log_i))
    _, ys = lax.scan(body, init, xs)
    return jnp.moveaxis(ys, (0, 2), (1, 3)).reshape(G, S, H, dv)

def _mlstm_bidir(q, k, v, gates):
    B = q.shape[0]
    flip = lambda t: jnp.flip(t, axis=1)
    both = lambda t: jnp.concatenate([t, flip(t)], axis=0)
    log_i = jnp.concatenate([gates[:, :, 0, 0], flip(gates[:, :, 1, 0])], axis=0)
    log_f = jax.nn.log_sigmoid(
        jnp.concatenate([gates[:, :, 0, 1], flip(gates[:, :, 1, 1])], axis=0))
    h = _mlstm_chunk_scan(both(q), both(k), both(v), log_f, log_i)
    return h[:B] + flip(h[B:])

def _hybrid_mixer(u, w_in, b_in, conv_w, conv_b, norm_w, w_out):
    B, S, _ = u.shape
    proj = u @ w_in + b_in
    offsets = [int(o) for o in np.cumsum(IN_SIZES)[:-1]]
    gb, gc, hin, q, k, v, o, gates = jnp.split(proj, offsets, axis=-1)
    y_conv = gb * _short_conv(gc * hin, conv_w, conv_b)
    f32 = jnp.float32
    q = q.reshape(B, S, MLSTM_HEADS, MLSTM_QK).astype(f32) * (MLSTM_QK ** -0.5)
    k = k.reshape(B, S, MLSTM_HEADS, MLSTM_QK).astype(f32)
    v = v.reshape(B, S, MLSTM_HEADS, MLSTM_V).astype(f32)
    gates = gates.reshape(B, S, 2, 2, MLSTM_HEADS).astype(f32)
    h = _mlstm_bidir(q, k, v, gates)
    mu = jnp.mean(h, -1, keepdims=True)
    var = jnp.mean(jnp.square(h - mu), -1, keepdims=True)
    hn = (h - mu) * lax.rsqrt(var + LN_EPS) * norm_w.reshape(MLSTM_HEADS, MLSTM_V).astype(f32)
    og = jax.nn.sigmoid(o.astype(f32)).reshape(B, S, MLSTM_HEADS, MLSTM_V)
    y_m = (og * hn).reshape(B, S, MLSTM_WIDTH).astype(u.dtype)
    return jnp.concatenate([y_conv, y_m], axis=-1) @ w_out

def _peer(u, wq, subkeys, pu, pv):
    B, S, D = u.shape
    T = B * S
    ut = u.reshape(T, D)
    qh = (ut @ wq).reshape(T, PEER_HEADS, 2, PEER_KEY_DIM // 2)
    scores = jnp.einsum('thpd,hpnd->thpn', qh, subkeys)
    top_s, top_i = lax.top_k(scores, PEER_TOPK)
    cand = top_s[:, :, 0, :, None] + top_s[:, :, 1, None, :]
    best_s, best_c = lax.top_k(cand.reshape(T, PEER_HEADS, PEER_TOPK * PEER_TOPK), PEER_TOPK)
    i1 = jnp.take_along_axis(top_i[:, :, 0], best_c // PEER_TOPK, axis=-1)
    i2 = jnp.take_along_axis(top_i[:, :, 1], best_c % PEER_TOPK, axis=-1)
    expert = i1 * N_KEYS + i2
    gate = jax.nn.softmax(best_s.astype(jnp.float32), axis=-1).astype(u.dtype)
    nb = T // PEER_BLOCK

    def block(args):
        xb, eb, gbk = args
        act = jax.nn.gelu(jnp.einsum('pd,phkd->phk', xb, pu[eb]), approximate=False)
        return jnp.einsum('phk,phkd->pd', gbk * act, pv[eb])

    out = lax.map(block, (ut.reshape(nb, PEER_BLOCK, D),
                          expert.reshape(nb, PEER_BLOCK, PEER_HEADS, PEER_TOPK),
                          gate.reshape(nb, PEER_BLOCK, PEER_HEADS, PEER_TOPK)))
    return out.reshape(B, S, D)

def setup_inputs(seed: int = 0) -> dict:
    key = jax.random.key(seed)
    ks = jax.random.split(key, 20)
    D = D_MODEL
    nrm = lambda k, shape, std: jax.random.normal(k, shape, jnp.float32) * std
    f_bias = jnp.linspace(3.0, 6.0, MLSTM_HEADS)
    gate_offset = jnp.tile(jnp.stack([jnp.zeros(MLSTM_HEADS), f_bias])[None], (2, 1, 1)).reshape(N_GATE_COLS)
    b_in = nrm(ks[5], (DEPTH, IN_COLS), 0.02).at[:, -N_GATE_COLS:].add(gate_offset)
    return {
        'x': nrm(ks[0], (BATCH, SEQ, D), 1.0),
        'c': nrm(ks[1], (BATCH, D), 1.0),
        'w_ada': nrm(ks[2], (DEPTH, D, 6 * D), D ** -0.5),
        'b_ada': nrm(ks[3], (DEPTH, 6 * D), 0.02),
        'w_in': nrm(ks[4], (DEPTH, D, IN_COLS), D ** -0.5),
        'b_in': b_in,
        'conv_w': nrm(ks[6], (DEPTH, CONV_K, CONV_WIDTH), CONV_K ** -0.5),
        'conv_b': nrm(ks[7], (DEPTH, CONV_WIDTH), 0.02),
        'mlstm_norm_w': 1.0 + nrm(ks[8], (DEPTH, MLSTM_WIDTH), 0.02),
        'w_out': nrm(ks[9], (DEPTH, D, D), BETA * D ** -0.5),
        'ln1_w': 1.0 + nrm(ks[10], (DEPTH, D), 0.02),
        'ln1_b': nrm(ks[11], (DEPTH, D), 0.02),
        'peer_wq': nrm(ks[12], (DEPTH, D, PEER_HEADS * PEER_KEY_DIM), D ** -0.5),
        'peer_subkeys': nrm(ks[13], (DEPTH, PEER_HEADS, 2, N_KEYS, PEER_KEY_DIM // 2), (PEER_KEY_DIM // 2) ** -0.5),
        'peer_u': nrm(ks[14], (DEPTH, N_EXPERTS, D), D ** -0.5),
        'peer_v': nrm(ks[15], (DEPTH, N_EXPERTS, D), BETA),
        'ln2_w': 1.0 + nrm(ks[16], (DEPTH, D), 0.02),
        'ln2_b': nrm(ks[17], (DEPTH, D), 0.02),
    }

def reference(x, c, w_ada, b_ada, w_in, b_in, conv_w, conv_b, mlstm_norm_w, w_out,
              ln1_w, ln1_b, peer_wq, peer_subkeys, peer_u, peer_v, ln2_w, ln2_b):
    cond = jax.nn.silu(c)
    for l in range(DEPTH):
        mod = cond @ w_ada[l] + b_ada[l]
        sh1, sc1, g1, sh2, sc2, g2 = jnp.split(mod, 6, axis=-1)
        u = _modulate(x, sh1, sc1)
        y = _hybrid_mixer(u, w_in[l], b_in[l], conv_w[l], conv_b[l], mlstm_norm_w[l], w_out[l])
        x = _post_norm(ALPHA * x + g1[:, None, :] * y, ln1_w[l], ln1_b[l])
        u = _modulate(x, sh2, sc2)
        y = _peer(u, peer_wq[l], peer_subkeys[l], peer_u[l], peer_v[l])
        x = _post_norm(ALPHA * x + g2[:, None, :] * y, ln2_w[l], ln2_b[l])
    return x


_drawn_inputs = setup_inputs


def setup_inputs(seed=0):
    import zlib

    import numpy as np

    out = dict(_drawn_inputs(seed))
    spreads = {}
    factors = {'conv_b': 3.76, 'mlstm_norm_w': 6.079, 'ln2_w': 2.894, 'ln2_b': 2.826}
    for name, (base, spread) in spreads.items():
        noise = np.random.default_rng([zlib.crc32(name.encode()), seed]).standard_normal(out[name].shape)
        drawn = base * np.exp(spread * noise) if base else spread * noise
        out[name] = __import__('jax').numpy.asarray(drawn.astype(out[name].dtype))
    for name, factor in factors.items():
        out[name] = (out[name] * factor).astype(out[name].dtype)
    return out
```

```python
from contextlib import ExitStack

import numpy as np

import concourse.bass as bass
from concourse import mybir

ALU = mybir.AluOpType
ACT = mybir.ActivationFunctionType
F32 = mybir.dt.float32
F32R = mybir.dt.float32r
U32 = mybir.dt.uint32
AX_X = mybir.AxisListType.X

P = 128
T = 512
NT = T // P
D = 2048
KD = D // P
CH = 512
MT = CH // P
SLABS = 4
HEADS, DK, DV = 4, 128, 256
CONV = 1024
GATE_COL = 6144
PH, TOPK, NK = 8, 16, 128
NE = NK * NK
ET = NE // P
LN_EPS = 1e-5
LOWEST = float(np.finfo(np.float32).min)

SH1, SC1, G1, SH2, SC2, G2 = (KD * i for i in range(6))
GB_CH, GC_CH, HIN_CH, Q_CH, V_CH, O_CH = 0, 2, 4, 6, 8, 10
J_V, J_CONV, J_O, J_OUT, J_WQ = 2, 4, 10, 12, 16
ADA_FIRST = 8
ADA_ALL = 24


class Tally:

    def __init__(self, eng, sem):
        self.eng, self.sem, self.base, self.k = eng, sem, 0, 0

    def loop(self, i, per):
        self.start, self.per = self.base + self.k, per
        self.base, self.k = i * per + self.start, 0

    def end(self, rounds):
        assert self.k == self.per, (self.k, self.per)
        self.base, self.k = self.start + rounds * self.per, 0

    def mark(self, ins):
        ins.then_inc(self.sem, 1)
        self.k += 1

    def settle(self):
        self.eng.wait_ge(self.sem, self.base + self.k)

    def link(self, ins):
        self.mark(ins)
        self.settle()


def build_layer(nc, x, c, w_ada, b_ada, w_in, b_in, conv_w, conv_b, mlstm_norm_w, w_out, ln1_w, ln1_b,
                peer_wq, peer_subkeys, peer_u, peer_v, ln2_w, ln2_b, out, alpha):
    with ExitStack() as ctx:
        def at(name, shape, offset, dt=F32):
            return nc.alloc_sbuf_tensor_at(name, shape, dt, offset=offset)

        def sem(name):
            return ctx.enter_context(nc.semaphore(name))

        KB = 1024
        base = (nc.sbuf_base + 31) // 32 * 32
        raw = [at(f"raw{s}", [P, 4, CH], base + 8 * KB * s) for s in range(SLABS)]
        o_split = base + 32 * KB
        w_hi = [at(f"w_hi{i}", [P, 4, CH], o_split + 8 * KB * i, F32R) for i in range(2)]
        w_lo = [at(f"w_lo{i}", [P, 4, CH], o_split + 16 * KB + 8 * KB * i, F32R) for i in range(2)]
        o_u = o_split + 32 * KB
        u_hi = at("u_hi", [P, KD, T], o_u, F32R)
        u_lo = at("u_lo", [P, KD, T], o_u + 32 * KB, F32R)

        o_const = [o_u + 64 * KB]

        def const(name, shape, dt=F32):
            t = at(name, shape, o_const[0], dt)
            n = 4
            for m in shape[1:]:
                n *= m
            o_const[0] += (n + 31) // 32 * 32
            return t

        ident = const("ident", [P, P])
        ones = const("ones", [P, P])
        iota = const("iota", [P, P])
        mask_fwd = const("mask_fwd", [P, P])
        mask_bwd = const("mask_bwd", [P, P])
        cond = const("cond", [P, KD])
        b_ada_c = const("b_ada_c", [P, 6 * KD])
        mod = const("mod", [P, 6 * KD])
        vec_c = const("vec_c", [P, 64])
        CONV_W, CONV_B = 32, 56
        gate_b = const("gate_b", [P, 1])
        stat = const("stat", [P, NT, 4, 6])
        mv = const("mv", [P, 4 * NT, 2])
        rstd = const("rstd", [P, 4 * NT])
        a_col = const("a_col", [P, 2, NT, HEADS])
        em_col = const("em_col", [P, 2, NT, HEADS])
        den = const("den", [P, 2, 2])
        W1 = o_const[0]
        H0 = W1 + 33024

        xz = at("xz", [P, NT, D], H0)
        u_f = [at(f"u_f{i}", [P, T], W1 + 16 * KB + 2 * KB * i) for i in range(2)]
        c_rows = at("c_rows", [KD, P], W1 + 24 * KB)
        c_sig = at("c_sig", [KD, P], W1 + 25 * KB)
        ada_rows = at("ada_rows", [6 * KD, P], W1 + 26 * KB)
        vec_rows = at("vec_rows", [64, P], W1 + 27 * KB)
        qk = at("qk", [P, 2, HEADS, T], W1)
        v_aug = at("v_aug", [P, NT, HEADS, DV + 2], W1 + 16 * KB)
        h_sum = at("h_sum", [P, NT, HEADS, DV], H0)
        g_hi = at("g_hi", [P, KD, P], H0, F32R)
        g_lo = at("g_lo", [P, KD, P], H0 + 8 * KB, F32R)
        gate_t = at("gate_t", [HEADS, 4, T], H0 + 16 * KB)
        g_raw = at("g_raw", [P, KD, 16], H0 + 24 * KB)
        prob = at("prob", [P, NT, T], H0 + 16 * KB)
        v_bias = at("v_bias", [P, 2 * CH], H0 + 16 * KB)
        g_M = at("g_M", [HEADS, 2, T], H0 + 24 * KB)
        g_b = at("g_b", [HEADS, 2, T], H0 + 28 * KB)
        norm_row = at("norm_row", [P, HEADS * DV], H0 + 28 * KB)
        sel = at("sel", [HEADS, HEADS, P], H0 + 32 * KB)
        yc_hi = at("yc_hi", [P, 8, T], W1, F32R)
        yc_lo = at("yc_lo", [P, 8, T], W1 + 16 * KB, F32R)
        conv_h = at("conv_h", [P, MT, T], H0 + 16 * KB)
        conv_c = at("conv_c", [P, MT, T + 2], H0 + 24 * KB)
        o_sig = at("o_sig", [P, 4, CH], H0 + 16 * KB)
        o_bias = at("o_bias", [P, 2 * CH], H0 + 28 * KB)
        ada_acc = at("ada_acc", [P, 4, CH], H0 + 34 * KB)
        assert H0 + 42 * KB <= nc.sbuf_usable_end, (H0 + 42 * KB, nc.sbuf_usable_end)
        g1_row = at("g1_row", [P, D], o_u + 16 * KB)
        ln1w_row = at("ln1w_row", [P, D], o_u + 24 * KB)
        ln1b_row = at("ln1b_row", [P, D], o_u + 48 * KB)
        diag = at("diag", [P, 4, P], o_u + 56 * KB)
        sk_raw = at("sk_raw", [P, 2 * PH, P], W1)
        sk_t = at("sk_t", [P, 2 * PH, P], H0 + 34 * KB)
        q_t = at("q_t", [P, 2 * PH, T], W1)
        scores = at("scores", [P, NT, 2 * PH, NK], H0)
        pick = [W1]

        def scratch(name, shape, dt=F32):
            t = at(name, shape, pick[0], dt)
            n = 4
            for m in shape[1:]:
                n *= m
            pick[0] += (n + 31) // 32 * 32
            return t

        ws = scratch("ws", [P, 2, NK])
        ws2 = scratch("ws2", [P, 2, NK])
        top_s = scratch("top_s", [P, 2, TOPK])
        top_i = scratch("top_i", [P, 2, TOPK], U32)
        top_f = scratch("top_f", [P, 2, TOPK])
        cand = scratch("cand", [P, TOPK, TOPK])
        cand2 = scratch("cand2", [P, TOPK, TOPK])
        best_s = scratch("best_s", [P, TOPK])
        best_c = scratch("best_c", [P, TOPK], U32)
        best_j = scratch("best_j", [P, 2, TOPK], U32)
        best_f = scratch("best_f", [P, 2, TOPK])
        hot = scratch("hot", [P, 2, TOPK, TOPK])
        neg_max = scratch("neg_max", [P, 1])
        g_exp = scratch("g_exp", [P, TOPK])
        g_sum = scratch("g_sum", [P, 1])
        g_inv = scratch("g_inv", [P, 1])
        picks = scratch("picks", [P, 3, PH, TOPK])
        G_TOK = 8
        G_BATCH = 64
        gates_sb = at("gates_sb", [P, NK, G_BATCH], W1)
        hot1 = at("hot1", [P, G_TOK, NK], H0, F32R)
        hot2 = at("hot2", [P, G_TOK, NK], H0 + 4 * KB)
        hot2_hi = at("hot2_hi", [P, G_TOK, NK], H0 + 8 * KB, F32R)
        hot2_lo = at("hot2_lo", [P, G_TOK, NK], H0 + 12 * KB, F32R)
        gt_hr = at("gt_hr", [P, G_TOK], H0 + 16 * KB + 32, F32R)
        gt_lo = at("gt_lo", [P, G_TOK], H0 + 16 * KB + 64)
        h_stage = [at(f"h_stage{i}", [P, T], H0 + 32 * KB + 2 * KB * i) for i in range(2)]
        by_pick = at("by_pick", [P, 3, T], H0 + 36 * KB)
        a_hi = [at(f"a_hi{i}", [P, 4, T], o_u + 8 * KB * i, F32R) for i in range(2)]
        a_lo = [at(f"a_lo{i}", [P, 4, T], o_u + 16 * KB + 8 * KB * i, F32R) for i in range(2)]
        h_in = [at(f"h_in{i}", [P, 4, T], o_u + 32 * KB + 8 * KB * i) for i in range(2)]
        g_in = [at(f"g_in{i}", [P, 4, T], o_u + 48 * KB + 8 * KB * i) for i in range(2)]
        y_acc = at("y_acc", [P, NT, D], W1)
        g2_row = at("g2_row", [P, D], o_u)
        ln2w_row = at("ln2w_row", [P, D], o_u + 8 * KB)
        ln2b_row = at("ln2b_row", [P, D], o_u + 16 * KB)
        diag2 = at("diag2", [P, 4, P], o_u + 24 * KB)

        ps = ctx.enter_context(nc.psum_tensor("ps", [P, 8, CH], F32))

        x1_dram = nc.dram_tensor("x1_scratch", [T, D], F32, kind="Internal").ap()
        h_dram = nc.dram_tensor("h_scratch", [NE, T], F32, kind="Internal").ap()
        g_dram = nc.dram_tensor("g_scratch", [NE, T], F32, kind="Internal").ap()

        x_v = x.rearrange("b (n p) d -> p (b n) d", p=P)
        out_v = out.rearrange("b (n p) d -> p (b n) d", p=P)
        x1_v = x1_dram.rearrange("(n p) d -> p n d", p=P)
        ada_v = w_ada[0].rearrange("(k p) n -> p k n", p=P)
        win_v = w_in[0].rearrange("(k p) n -> p k n", p=P)
        wout_v = w_out[0].rearrange("(k p) n -> p k n", p=P)
        wq_v = peer_wq[0].rearrange("(k p) n -> p k n", p=P)
        pu_v = peer_u[0].rearrange("(e p) (k n) -> p e k n", p=P, n=CH)
        pv_v = peer_v[0].rearrange("(e p) n -> p e n", p=P)
        h_v = h_dram.rearrange("(e p) t -> p e t", p=P)
        g_v = g_dram.rearrange("(e p) t -> p e t", p=P)

        def row(v, lo, n):
            return v[0, lo:lo + n].partition_broadcast(P)

        small_in = sem("small_in")
        x_in = sem("x_in")
        rows_in = sem("rows_in")
        slab_in = [sem(f"slab_in{s}") for s in range(SLABS)]
        const_made = sem("const_made")
        silu_made = sem("silu_made")
        first_turned = sem("first_turned")
        cond_ready = sem("cond_ready")
        x_normal = sem("x_normal")
        sqrt_asked = sem("sqrt_asked")
        sqrt_made = sem("sqrt_made")
        x_turned = sem("x_turned")
        uf_made = sem("uf_made")
        uhi_made = sem("uhi_made")
        ulo_made = sem("ulo_made")
        ada_read = sem("ada_read")
        ada_reduced = sem("ada_reduced")
        ada_kept = sem("ada_kept")
        hi_made = sem("hi_made")
        lo_made = sem("lo_made")
        slab_used = sem("slab_used")
        tile_done = sem("tile_done")
        bank_free = sem("bank_free")
        gates_zero = sem("gates_zero")
        gates_hi = sem("gates_hi")
        gates_lo = sem("gates_lo")
        gate_b_in = sem("gate_b_in")
        norm_in = sem("norm_in")
        y_zero = sem("y_zero")
        gates_proj = sem("gates_proj")
        gate_step = sem("gate_step")
        gate_act = sem("gate_act")
        gates_ready = sem("gates_ready")
        gates_turned = sem("gates_turned")
        cols_kept = sem("cols_kept")
        s_made = sem("s_made")
        m_made = sem("m_made")
        e_asked = sem("e_asked")
        e_made = sem("e_made")
        p_made = sem("p_made")
        hd_out = sem("hd_out")
        hd_kept = sem("hd_kept")
        conv_done = sem("conv_done")
        yhi_made = sem("yhi_made")
        ylo_made = sem("ylo_made")
        o_added = sem("o_added")
        o_sigd = sem("o_sigd")
        y_gated = sem("y_gated")
        y_turned = sem("y_turned")
        ym_hi = sem("ym_hi")
        ym_lo = sem("ym_lo")
        diag_made = sem("diag_made")
        row_made = sem("row_made")
        row_kept = sem("row_kept")
        x1_made = sem("x1_made")
        x1_out = sem("x1_out")
        sk_turned = sem("sk_turned")
        sk_kept = sem("sk_kept")
        sc_made = sem("sc_made")
        sc_kept = sem("sc_kept")
        u_turned = sem("u_turned")
        eu_hi = sem("eu_hi")
        eu_lo = sem("eu_lo")
        u_done = sem("u_done")
        h_made = sem("h_made")
        h_out = [sem(f"h_out{i}") for i in range(2)]
        gexp_asked = sem("gexp_asked")
        gexp_made = sem("gexp_made")
        picked = sem("picked")
        pick_turned = sem("pick_turned")
        pick_kept = sem("pick_kept")
        hot_made = sem("hot_made")
        g_done = sem("g_done")
        g_kept = sem("g_kept")
        g_out = sem("g_out")
        hg_in = [sem(f"hg_in{i}") for i in range(2)]
        a_mul = sem("a_mul")
        ahi_made = sem("ahi_made")
        alo_made = sem("alo_made")
        v_done = sem("v_done")
        v_free = sem("v_free")
        x1_back = sem("x1_back")
        out_made = sem("out_made")
        out_sent = sem("out_sent")
        dve_order = sem("dve_order")
        paced = sem("paced")
        act_order = sem("act_order")
        pool_order = sem("pool_order")

        NC = 20
        NB = ET // 4

        block = ctx.enter_context(nc.Block())

        @block.sync
        def _(sp):
            for n in range(NT):
                sp.dma_start(xz[:, n, :], x_v[:, n, :]).then_inc(x_in, 16)

            def load(s, src):
                sp.dma_start(raw[s][:, :, :], src).then_inc(slab_in[s], 16)

            for s in range(SLABS):
                load(s, ada_v[:, 4 * s:4 * s + 4, 0:CH])
            with sp.Fori(1, ADA_FIRST, 1) as g:
                for s in range(SLABS):
                    sp.wait_ge(ada_read, g * 4 + (s - 3))
                    load(s, ada_v[:, 4 * s:4 * s + 4, bass.ds(g * CH, CH)])

            def projection(j, src, col, ada):
                for s in range(SLABS):
                    sp.wait_ge(ada_read, j * 4 + (4 * ADA_FIRST - 4 + s + 1))
                    load(s, src[:, 4 * s:4 * s + 4, bass.ds(col, CH)])
                for s in range(SLABS):
                    sp.wait_ge(lo_made, j * 4 + (s + 1))
                    load(s, ada_v[:, 4 * s:4 * s + 4, bass.ds(ada * CH, CH)])

            with sp.Fori(0, 4, 1) as i:
                projection(i, win_v, (i + Q_CH) * CH, i + ADA_FIRST)
            with sp.Fori(0, 2, 1) as i:
                for r, first in enumerate((HIN_CH, GC_CH, GB_CH)):
                    projection(i * 3 + (J_CONV + r), win_v, (i + first) * CH, i * 3 + (J_CONV + r + ADA_FIRST))
            with sp.Fori(0, 2, 1) as i:
                projection(i + J_O, win_v, (i + O_CH) * CH, i + (J_O + ADA_FIRST))
            with sp.Fori(0, 4, 1) as i:
                projection(i + J_OUT, wout_v, i * CH, i + (J_OUT + ADA_FIRST))
            for s in range(SLABS):
                sp.wait_ge(ada_read, 4 * ADA_ALL - 4 + s + 1)
                load(s, wq_v[:, 4 * s:4 * s + 4, 0:CH])
            with sp.Fori(1, 4, 1) as i:
                for s in range(SLABS):
                    sp.wait_ge(lo_made, i * 4 + (4 * (J_WQ - 1) + s + 1))
                    load(s, wq_v[:, 4 * s:4 * s + 4, bass.ds(i * CH, CH)])
            for s in range(SLABS):
                sp.wait_ge(lo_made, 4 * (NC - 1) + s + 1)
                load(s, pu_v[:, s, :, :])
            with sp.Fori(1, NB, 1) as b:
                for s in range(SLABS):
                    sp.wait_ge(u_turned, b * 8 + (2 * s - 6))
                    load(s, pu_v[:, b * 4 + s, :, :])

            def load_hg(b, i, stored):
                if stored is not None:
                    sp.wait_ge(alo_made, stored)
                sp.dma_start(h_in[i][:, :, :], h_v[:, bass.ds(b * 4, 4), :]).then_inc(hg_in[i], 16)
                sp.dma_start(g_in[i][:, :, :], g_v[:, bass.ds(b * 4, 4), :]).then_inc(hg_in[i], 16)

            sp.wait_ge(h_made, ET)
            sp.wait_ge(h_out[0], 16 * ET // 2)
            sp.wait_ge(h_out[1], 16 * ET // 2)
            sp.wait_ge(g_out, 32 * T // G_BATCH)
            load_hg(0, 0, None)
            load_hg(1, 1, None)
            for s in range(SLABS):
                sp.wait_ge(u_turned, 2 * (ET - 4 + s + 1))
                load(s, pv_v[:, 0:4, s * CH:s * CH + CH])
            for s in range(SLABS):
                sp.wait_ge(lo_made, 4 * NC + s + 1)
                load(s, pv_v[:, 4:8, s * CH:s * CH + CH])
            with sp.Fori(1, NB // 2, 1) as r:
                for i in range(2):
                    load_hg(r * 2 + i, i, r * 2 + (i - 1))
                    for s in range(SLABS):
                        sp.wait_ge(lo_made, r * 8 + (4 * i + 4 * NC - 4 + s + 1))
                        load(s, pv_v[:, bass.ds((r * 2 + i) * 4, 4), s * CH:s * CH + CH])
            for n in range(NT):
                sp.wait_ge(out_made, n + 1)
                sp.dma_start(out_v[:, n, :], xz[:, n, :]).then_inc(out_sent, 16)
            sp.wait_ge(out_sent, 16 * NT)
            sp.wait_ge(x1_out, 16 * NT)

        @block.gpsimd
        def _(pool):
            order = Tally(pool, pool_order)
            order.mark(pool.memset(ident[:, :], 0.0))
            order.mark(pool.memset(ones[:, :], 1.0))
            order.mark(pool.memset(sel[:, :, :], 0.0))
            order.mark(pool.memset(gate_b[:, :], 0.0))
            order.settle()
            order.mark(pool.affine_select(out=ident[:, :], in_=ident[:, :], compare_op=ALU.not_equal, fill=1.0,
                                          base=0, pattern=[[-1, P]], channel_multiplier=1))
            order.mark(pool.affine_select(out=mask_fwd[:, :], in_=ones[:, :], compare_op=ALU.is_ge, fill=0.0,
                                          base=0, pattern=[[1, P]], channel_multiplier=-1))
            order.mark(pool.affine_select(out=mask_bwd[:, :], in_=ones[:, :], compare_op=ALU.is_ge, fill=0.0,
                                          base=0, pattern=[[-1, P]], channel_multiplier=1))
            order.mark(pool.affine_select(out=sel[:, :, :], in_=sel[:, :, :], compare_op=ALU.not_equal, fill=1.0,
                                          base=0, pattern=[[-1, HEADS], [0, P]], channel_multiplier=1))
            order.mark(pool.iota(iota[:, :], [[1, P]], base=0, channel_multiplier=0,
                                 allow_small_or_imprecise_dtypes=True))
            order.settle()
            pool.sem_inc(const_made, 1)
            for g in range(4):
                pool.dma_start(gate_b[32 * g:32 * g + HEADS, :],
                               b_in[0, GATE_COL + HEADS * g:GATE_COL + HEADS * (g + 1)].unsqueeze(1)
                               ).then_inc(gate_b_in, 16)

            def store_h(i, slot):
                pool.wait_ge(h_made, i + 1)
                pool.dma_start(h_v[:, i, :], h_stage[slot][:, :]).then_inc(h_out[slot], 16)

            with pool.Fori(0, 16, 1) as r:
                for i in range(2):
                    store_h(r * 2 + i, i)
            with pool.Fori(0, T // G_BATCH, 1) as b:
                for i in range(8):
                    store_h(b * 8 + (32 + i), i % 2)
                pool.wait_ge(g_kept, b * 16 + 16)
                for h in range(2):
                    keys = slice(h * NK // 2, (h + 1) * NK // 2)
                    pool.dma_start(g_dram.rearrange("(a b) t -> b a t", b=P)[:, keys, bass.ds(b * G_BATCH, G_BATCH)],
                                   gates_sb[:, keys, :]).then_inc(g_out, 16)
            pool.wait_ge(g_out, 32 * T // G_BATCH)
            pool.memset(y_acc[:, :, :], 0.0).then_inc(y_zero, 1)
            with pool.Fori(0, 16, 1) as r:
                for i in range(2):
                    store_h(r * 2 + (96 + i), i)

        @block.scalar
        def _(act):
            order = Tally(act, act_order)
            act.dma_start(c_rows[:, :], c.rearrange("b (k p) -> (b k) p", p=P)).then_inc(small_in, 16)
            act.dma_start(ada_rows[:, :], b_ada[0].rearrange("(k p) -> k p", p=P)).then_inc(small_in, 16)
            act.dma_start(vec_rows[0:32, :], b_in[0, 0:32 * P].rearrange("(k p) -> k p", p=P)).then_inc(small_in, 16)
            act.dma_start(vec_rows[32:56, :], conv_w[0].rearrange("w (k p) -> (w k) p", p=P)).then_inc(small_in, 16)
            act.dma_start(vec_rows[56:64, :], conv_b[0].rearrange("(k p) -> k p", p=P)).then_inc(small_in, 16)
            act.wait_ge(small_in, 80)
            act.activation(c_sig[:, :], c_rows[:, :], ACT.Sigmoid).then_inc(silu_made, 1)

            def root(n, width):
                act.wait_ge(sqrt_asked, n)
                act.activation(rstd[:, 0:width], rstd[:, 0:width], ACT.Sqrt).then_inc(sqrt_made, 1)

            def split_u(r):
                with act.Fori(0, KD // 2, 1) as i:
                    for k in range(2):
                        act.wait_ge(uf_made, i * 2 + (KD * r + k + 1))
                        act.activation(u_hi[:, i * 2 + k, :], u_f[k][:, :], ACT.Copy).then_inc(uhi_made, 1)

            def hi(s, loaded, used, count):
                act.wait_ge(slab_in[s], loaded)
                act.wait_ge(used, count)
                act.activation(w_hi[s % 2][:, :, :], raw[s][:, :, :], ACT.Copy).then_inc(hi_made, 1)

            def chunk(j, loaded, loaded_next):
                hi(1, loaded, tile_done, j * 4)
                hi(2, loaded, slab_used, j * 3 + 1)
                hi(3, loaded, slab_used, j * 3 + 2)
                if loaded_next is not None:
                    hi(0, loaded_next, slab_used, j * 3 + 3)

            def paired(j):
                chunk(j, j * 32 + 16 * (ADA_FIRST + 1), j * 32 + 16 * (ADA_FIRST + 3))

            root(1, NT)
            split_u(0)
            act.wait_ge(x_turned, KD)
            act.dma_start(g_raw[:, :, :], win_v[:, :, GATE_COL:GATE_COL + 16]).then_inc(small_in, 16)
            act.wait_ge(small_in, 96)
            act.wait_ge(gates_zero, 1)
            for g in range(4):
                act.activation(g_hi[:, :, 32 * g:32 * g + HEADS], g_raw[:, :, HEADS * g:HEADS * (g + 1)], ACT.Copy
                               ).then_inc(gates_hi, 1)
            act.wait_ge(slab_in[0], 16 * (ADA_FIRST + 1))
            act.activation(w_hi[0][:, :, :], raw[0][:, :, :], ACT.Copy).then_inc(hi_made, 1)
            act.wait_ge(gate_step, 1)
            order.link(act.activation(g_M[:, :, :], gate_t[:, 1::2, :], ACT.Abs))
            order.link(act.activation(g_M[:, :, :], g_M[:, :, :], ACT.Exp, scale=-1.0))
            act.activation(g_M[:, :, :], g_M[:, :, :], ACT.Ln, bias=1.0).then_inc(gate_act, 1)
            act.wait_ge(gate_step, 2)
            act.activation(g_b[:, :, :], g_b[:, :, :], ACT.Exp, scale=-1.0).then_inc(gate_act, 1)
            act.wait_ge(cols_kept, 1)
            act.dma_start(v_bias[:, :], row(b_in, V_CH * CH, 2 * CH)).then_inc(rows_in, 16)
            act.dma_start(norm_row[:, :], row(mlstm_norm_w, 0, HEADS * DV)).then_inc(norm_in, 16)

            with act.Fori(0, J_CONV, 1) as i:
                paired(i)
            for n in range(2 * HEADS):
                for st in range(NT):
                    act.wait_ge(e_asked, NT * n + st + 1)
                    lo_c, hi_c = (st * P, T) if n % 2 == 0 else (0, (st + 1) * P)
                    act.activation(prob[:, st, lo_c:hi_c], prob[:, st, lo_c:hi_c], ACT.Exp, scale=-1.0
                                   ).then_inc(e_made, 1)
            root(2, 4 * NT)
            with act.Fori(0, 2, 1) as i:
                for r in range(3):
                    paired(i * 3 + (J_CONV + r))
                for m in range(MT):
                    act.wait_ge(conv_done, i * MT + (m + 1))
                    act.activation(yc_hi[:, i * MT + m, :], conv_h[:, m, :], ACT.Copy).then_inc(yhi_made, 1)
            act.wait_ge(ylo_made, 8)
            act.dma_start(o_bias[:, :], row(b_in, O_CH * CH, 2 * CH)).then_inc(rows_in, 16)
            with act.Fori(0, 2, 1) as i:
                paired(i + J_O)
                for t in range(NT):
                    act.wait_ge(o_added, i * NT + (t + 1))
                    act.activation(o_sig[:, t, :], o_sig[:, t, :], ACT.Sigmoid).then_inc(o_sigd, 1)
            for k in range(8):
                act.wait_ge(y_turned, k + 1)
                act.activation(u_hi[:, k, :], ps[:, 4 + k % 2, :], ACT.Copy).then_inc(ym_hi, 1)
            act.dma_start(ln1w_row[:, :], row(ln1_w, 0, D)).then_inc(rows_in, 16)
            act.dma_start(ln1b_row[:, :], row(ln1_b, 0, D)).then_inc(rows_in, 16)
            for n in range(NT):
                act.dma_start(xz[:, n, :], x_v[:, n, :]).then_inc(x_in, 16)
            with act.Fori(0, 3, 1) as i:
                paired(i + J_OUT)
            first_wq = 16 * (ADA_FIRST + 2 * J_WQ + 1)
            chunk(J_WQ - 1, first_wq - 32, first_wq)
            act.wait_ge(tile_done, 4 * J_WQ)
            act.dma_start(sk_raw[:, :, :], peer_subkeys[0].rearrange("h s n k -> n (h s) k")).then_inc(small_in, 16)
            root(3, NT)
            for n in range(NT):
                act.wait_ge(x1_made, n + 1)
                act.dma_start(x1_v[:, n, :], xz[:, n, :]).then_inc(x1_out, 16)
            root(4, NT)
            split_u(1)
            with act.Fori(0, 3, 1) as i:
                chunk(i + J_WQ, i * 16 + first_wq, i * 16 + (first_wq + 16))
            chunk(NC - 1, first_wq + 48, None)

            def turn_hi(i, par):
                for h in range(2):
                    act.wait_ge(u_turned, i * 2 + (h + 1))
                    act.activation(w_hi[par][:, 2 * h:2 * h + 2, :], ps[:, 2 * h:2 * h + 2, :], ACT.Copy
                                   ).then_inc(eu_hi, 1)

            def gelu(i, slot, stored):
                act.wait_ge(u_done, i + 1)
                act.wait_ge(h_out[slot], stored)
                act.activation(h_stage[slot][:, :], ps[:, 4 + slot, :], ACT.Gelu).then_inc(h_made, 1)

            act.wait_ge(tile_done, 4 * NC)
            turn_hi(0, 0)
            with act.Fori(0, NT, 1) as r:
                for h in range(PH):
                    turn_hi(r * 8 + (h + 1), (h + 1) % 2)
                    gelu(r * 8 + h, h % 2, r * 64 + 16 * (h // 2))
                    act.wait_ge(gexp_asked, r * 8 + (h + 1))
                    act.activation(g_exp[:, :], best_s[:, :], ACT.Exp, bias=neg_max[:, :], accum_out=g_sum[:, :]
                                   ).then_inc(gexp_made, 1)
            with act.Fori(0, T // G_BATCH, 1) as b:
                for n in range(8):
                    turn_hi(b * 8 + (33 + n), (n + 1) % 2)
                    gelu(b * 8 + (32 + n), n % 2, b * 64 + (256 + 16 * (n // 2)))
                    if n == 0:
                        act.wait_ge(g_out, b * 32)
                    act.wait_ge(g_done, b * 8 + (n + 1))
                    for h in range(2):
                        t0 = G_TOK * n + 4 * h
                        act.activation(gates_sb[:, :, t0:t0 + 4].rearrange("p a t -> p t a"),
                                       ps[:, 6 + h, :].rearrange("p (t a) -> p t a", t=4), ACT.Copy
                                       ).then_inc(g_kept, 1)
            with act.Fori(0, 15, 1) as r:
                for n in range(2):
                    turn_hi(r * 2 + (97 + n), (n + 1) % 2)
                    gelu(r * 2 + (96 + n), n, r * 16 + 768)
            turn_hi(ET - 1, 1)
            gelu(ET - 2, 0, 1008)
            gelu(ET - 1, 1, 1008)

            def v_hi(s, loaded, done):
                act.wait_ge(slab_in[s], loaded)
                if done is not None:
                    act.wait_ge(v_done, done)
                act.activation(w_hi[s % 2][:, :, :], raw[s][:, :, :], ACT.Copy).then_inc(hi_made, 1)

            def a_split(b, par, done):
                act.wait_ge(a_mul, b + 1)
                if done is not None:
                    act.wait_ge(v_done, done)
                act.activation(a_hi[par][:, :, :], h_in[par][:, :, :], ACT.Copy).then_inc(ahi_made, 1)

            def v_block(b, par, last):
                for dc in range(SLABS):
                    if dc < 3:
                        v_hi(dc + 1, b * 16 + 16 * 77, b * 16 + 4 * dc)
                    elif not last:
                        v_hi(0, b * 16 + 16 * 78, b * 16 + 12)
                    if dc == 1 and not last:
                        a_split(b + 1, 1 - par, b * 16)

            a_split(0, 0, None)
            v_hi(0, 16 * 77, None)
            with act.Fori(0, NB // 2 - 1, 1) as r:
                v_block(r * 2, 0, False)
                v_block(r * 2 + 1, 1, False)
            v_block(NB - 2, 0, False)
            act.dma_start(xz[:, :, :], x1_v).then_inc(x1_back, 16)
            v_block(NB - 1, 1, True)
            act.wait_ge(v_done, 16 * NB)
            act.dma_start(ln2w_row[:, :], row(ln2_w, 0, D)).then_inc(rows_in, 16)
            act.dma_start(ln2b_row[:, :], row(ln2_b, 0, D)).then_inc(rows_in, 16)
            root(5, NT)

        @block.vector
        def _(dve):
            order = Tally(dve, dve_order)
            dve.sem_inc(bank_free, 4)
            dve.sem_inc(v_free, 8)



            def root(n, width):
                order.settle()
                dve.tensor_scalar(rstd[:, 0:width], mv[:, 0:width, 1], LN_EPS, None, ALU.add).then_inc(sqrt_asked, 1)
                dve.wait_ge(sqrt_made, n)
                order.link(dve.reciprocal(rstd[:, 0:width], rstd[:, 0:width]))

            def row_stats(n):
                for q in range(4):
                    order.mark(dve.bn_stats(stat[:, n, q, :], xz[:, n, q * CH:(q + 1) * CH]))
                order.settle()
                order.mark(dve.bn_aggr(mv[:, n, :], stat[:, n, :, :]))

            def normal(n):
                return dve.tensor_scalar(xz[:, n, :], xz[:, n, :], mv[:, n, 0:1], rstd[:, n:n + 1],
                                         ALU.subtract, ALU.mult)

            def split_u(r, scale, shift):
                with dve.Fori(0, KD // 2, 1) as i:
                    for k in range(2):
                        dve.wait_ge(x_turned, i * 2 + (KD * r + k + 1))
                        if k == 0:
                            dve.wait_ge(ulo_made, i * 2 + KD * r)
                        dve.tensor_scalar(u_f[k][:, :], ps[:, 4 + k, :], mod[:, bass.ds(i * 2 + (scale + k), 1)],
                                          mod[:, bass.ds(i * 2 + (shift + k), 1)], ALU.mult, ALU.add
                                          ).then_inc(uf_made, 1)
                    for k in range(2):
                        dve.wait_ge(uhi_made, i * 2 + (KD * r + k + 1))
                        dve.tensor_tensor(u_lo[:, i * 2 + k, :], u_f[k][:, :], u_hi[:, i * 2 + k, :].bitcast(F32),
                                          ALU.subtract).then_inc(ulo_made, 1)

            def lo(s, n):
                dve.wait_ge(hi_made, n)
                dve.tensor_tensor(w_lo[s % 2][:, :, :], raw[s][:, :, :], w_hi[s % 2][:, :, :].bitcast(F32),
                                  ALU.subtract).then_inc(lo_made, 1)

            def ada_chunk(a, loaded):
                dve.wait_ge(ada_reduced, a)
                for s in range(SLABS):
                    dve.wait_ge(slab_in[s], loaded)
                    if s:
                        dve.wait_ge(ada_read, a * 4 + s)
                    for k in range(4):
                        w, m = raw[s][:, k, :], cond[:, 4 * s + k:4 * s + k + 1]
                        if s == 0:
                            ins = dve.tensor_scalar(ada_acc[:, k, :], w, m, None, ALU.mult)
                        else:
                            ins = dve.scalar_tensor_tensor(ada_acc[:, k, :], w, m, ada_acc[:, k, :],
                                                           ALU.mult, ALU.add)
                    ins.then_inc(ada_read, 1)

            def ada_keep(a):
                dve.wait_ge(ada_reduced, a + 1)
                dve.tensor_tensor(mod[:, bass.ds(a * 4, 4)], ps[:, 6, 0:4], b_ada_c[:, bass.ds(a * 4, 4)],
                                  ALU.add).then_inc(ada_kept, 1)

            def chunk(j, read_bank, prepare=None):
                for s in range(1, SLABS):
                    lo(s, j * 4 + (s + 1))
                ada_chunk(j + ADA_FIRST, j * 32 + 16 * (ADA_FIRST + 2))
                if prepare:
                    prepare()
                lo(0, j * 4 + 5)
                for m in range(MT):
                    dve.wait_ge(tile_done, j * 4 + (m + 1))
                    read_bank(m)
                ada_keep(j + ADA_FIRST)

            dve.wait_ge(silu_made, 1)
            dve.tensor_tensor(c_sig[:, :], c_rows[:, :], c_sig[:, :], ALU.mult).then_inc(cond_ready, 1)
            dve.wait_ge(first_turned, 1)
            order.mark(dve.tensor_copy(cond[:, :], ps[:, 7, 0:KD]))
            order.mark(dve.tensor_copy(b_ada_c[:, :], ps[:, 7, 128:128 + 6 * KD]))
            order.mark(dve.tensor_copy(vec_c[:, :], ps[:, 7, 256:256 + 64]))
            order.settle()
            ada_chunk(0, 16)
            dve.wait_ge(x_in, 16 * NT)
            for n in range(NT):
                row_stats(n)
            root(1, NT)
            for n in range(NT):
                normal(n).then_inc(x_normal, 1)
            ada_keep(0)
            with dve.Fori(1, ADA_FIRST, 1) as a:
                ada_chunk(a, a * 16 + 16)
                ada_keep(a)
            dve.wait_ge(ada_kept, ADA_FIRST)
            order.link(dve.tensor_scalar(mod[:, SC1:SC1 + KD], mod[:, SC1:SC1 + KD], 1.0, None, ALU.add))
            split_u(0, SC1, SH1)
            dve.wait_ge(ulo_made, KD)
            order.mark(dve.memset(g_hi[:, :, :].bitcast(F32), 0.0))
            order.mark(dve.memset(g_lo[:, :, :].bitcast(F32), 0.0))
            order.mark(dve.memset(v_aug[:, :, :, DV:DV + 2], 1.0))
            order.settle()
            dve.sem_inc(gates_zero, 1)
            for g in range(4):
                dve.wait_ge(gates_hi, g + 1)
                dve.tensor_tensor(g_lo[:, :, 32 * g:32 * g + HEADS], g_raw[:, :, HEADS * g:HEADS * (g + 1)],
                                  g_hi[:, :, 32 * g:32 * g + HEADS].bitcast(F32), ALU.subtract).then_inc(gates_lo, 1)
            lo(0, 1)
            dve.wait_ge(gates_proj, 1)
            dve.wait_ge(gate_b_in, 64)
            for g in range(4):
                order.mark(dve.tensor_scalar(gate_t[:, g, :], ps[32 * g:32 * g + HEADS, 7, :],
                                             gate_b[32 * g:32 * g + HEADS, :], None, ALU.add))
            order.settle()
            dve.sem_inc(gate_step, 1)
            dve.wait_ge(gate_act, 1)
            f, i_g = gate_t[:, 1::2, :], gate_t[:, 0::2, :]
            order.link(dve.scalar_tensor_tensor(f, f, 0.0, g_M[:, :, :], ALU.min, ALU.subtract))
            f0, f1 = gate_t[:, 1, :], gate_t[:, 3, :]
            order.mark(dve.tensor_tensor_scan(g_b[:, 0, :], f0, f0, 0.0, ALU.add, ALU.min))
            order.mark(dve.tensor_tensor_scan(g_b[:, 1, ::-1], f1[:, ::-1], f1[:, ::-1], 0.0, ALU.add, ALU.min))
            order.settle()
            order.link(dve.tensor_tensor(i_g, i_g, g_b[:, :, :], ALU.subtract))
            a0, a1 = gate_t[:, 0, :], gate_t[:, 2, :]
            order.mark(dve.tensor_tensor_scan(g_M[:, 0, :], a0, a0, 0.0, ALU.max, ALU.max))
            order.mark(dve.tensor_tensor_scan(g_M[:, 1, ::-1], a1[:, ::-1], a1[:, ::-1], 0.0, ALU.max, ALU.max))
            order.settle()
            dve.tensor_tensor(g_b[:, :, :], g_b[:, :, :], g_M[:, :, :], ALU.add).then_inc(gate_step, 1)
            dve.wait_ge(gates_turned, 1)
            order.mark(dve.tensor_copy(a_col[:, :, :, :].rearrange("p d t h -> p (d t h)"), ps[:, 7, 0:32]))
            order.mark(dve.tensor_copy(em_col[:, :, :, :].rearrange("p d t h -> p (d t h)"), ps[:, 7, 32:64]))
            order.settle()
            dve.sem_inc(cols_kept, 1)

            with dve.Fori(0, 2, 1) as i:
                def keep_qk(m):
                    dve.tensor_scalar(qk[:, i, m, :], ps[:, m, :], vec_c[:, bass.ds(i * MT + (Q_CH * MT + m), 1)],
                                      None, ALU.add).then_inc(bank_free, 1)
                chunk(i, keep_qk)
            dve.wait_ge(rows_in, 16)
            with dve.Fori(0, 2, 1) as i:
                def keep_v(t):
                    dve.tensor_tensor(v_aug[:, t, bass.ds(i * 2, 2), 0:DV],
                                      ps[:, t, :].rearrange("p (h v) -> p h v", h=2),
                                      v_bias[:, bass.ds(i * CH, CH)].rearrange("p (h v) -> p h v", h=2),
                                      ALU.add).then_inc(bank_free, 1)
                chunk(i + J_V, keep_v)
            dve.wait_ge(bank_free, 4 * J_CONV + 4)

            for h in range(HEADS):
                for d in range(2):
                    n = 2 * h + d
                    mask = mask_fwd if d == 0 else mask_bwd
                    dve.wait_ge(m_made, h + 1)
                    if n:
                        dve.wait_ge(hd_out, NT * n)
                    for st in range(NT):
                        lo_c, hi_c = (st * P, T) if d == 0 else (0, (st + 1) * P)
                        dve.tensor_scalar(prob[:, st, lo_c:hi_c], ps[:, 4 + d, lo_c:hi_c], a_col[:, d, st, h:h + 1],
                                          0.0, ALU.subtract, ALU.max).then_inc(e_asked, 1)
                    for st in range(NT):
                        dve.wait_ge(e_made, NT * n + st + 1)
                        own = prob[:, st, st * P:(st + 1) * P]
                        order.mark(dve.tensor_tensor(own, own, mask[:, :], ALU.mult))
                    order.settle()
                    for st in range(NT):
                        lo_c, hi_c = (st * P, T) if d == 0 else (0, (st + 1) * P)
                        dve.wait_ge(s_made, NT * h + st + 1)
                        dve.scalar_tensor_tensor(prob[:, st, lo_c:hi_c], ps[:, st, lo_c:hi_c], DK ** -0.5,
                                                 prob[:, st, lo_c:hi_c], ALU.mult, ALU.mult).then_inc(p_made, 1)
                    for t in range(NT):
                        b = 6 + t % 2
                        dve.wait_ge(hd_out, NT * n + t + 1)
                        order.link(dve.tensor_scalar(den[:, t % 2, 0:1], ps[:, b, DV:DV + 1], -1.0,
                                                     em_col[:, d, t, h:h + 1], ALU.mult, ALU.max))
                        order.link(dve.tensor_tensor(den[:, t % 2, 0:1], ps[:, b, DV:DV + 1], den[:, t % 2, 0:1],
                                                     ALU.max))
                        order.link(dve.reciprocal(den[:, t % 2, 1:2], den[:, t % 2, 0:1]))
                        if d == 0:
                            dve.tensor_scalar(h_sum[:, t, h, :], ps[:, b, 0:DV], den[:, t % 2, 1:2], None, ALU.mult
                                              ).then_inc(hd_kept, 1)
                        else:
                            dve.scalar_tensor_tensor(h_sum[:, t, h, :], ps[:, b, 0:DV], den[:, t % 2, 1:2],
                                                     h_sum[:, t, h, :], ALU.mult, ALU.add).then_inc(hd_kept, 1)
            dve.wait_ge(hd_kept, 8 * NT)
            for t in range(NT):
                for h in range(HEADS):
                    order.mark(dve.bn_stats(stat[:, t, h, :], h_sum[:, t, h, :]))
            order.settle()
            for t in range(NT):
                for h in range(HEADS):
                    order.mark(dve.bn_aggr(mv[:, 4 * t + h, :], stat[:, t, h, :]))
            root(2, 4 * NT)
            for t in range(NT):
                for h in range(HEADS):
                    q = 4 * t + h
                    order.mark(dve.tensor_scalar(h_sum[:, t, h, :], h_sum[:, t, h, :], mv[:, q, 0:1],
                                                 rstd[:, q:q + 1], ALU.subtract, ALU.mult))
            order.settle()
            dve.wait_ge(norm_in, 16)
            for t in range(NT):
                hs = h_sum[:, t, :, :].rearrange("p h v -> p (h v)")
                order.mark(dve.tensor_tensor(hs, hs, norm_row[:, :], ALU.mult))
            order.settle()
            order.mark(dve.memset(conv_c[:, :, 0:1], 0.0))
            order.mark(dve.memset(conv_c[:, :, T + 1:T + 2], 0.0))
            order.settle()

            with dve.Fori(0, 2, 1) as i:
                order.loop(i, 4 * MT)

                def col(first, m):
                    return vec_c[:, bass.ds(i * MT + (first + m), 1)]

                def keep_h(m):
                    dve.tensor_scalar(conv_h[:, m, :], ps[:, m, :], col(HIN_CH * MT, m), None, ALU.add
                                      ).then_inc(bank_free, 1)

                def keep_c(m):
                    dve.scalar_tensor_tensor(conv_c[:, m, 1:T + 1], ps[:, m, :], col(GC_CH * MT, m),
                                             conv_h[:, m, :], ALU.add, ALU.mult).then_inc(bank_free, 1)

                def taps():
                    for k in range(3):
                        for m in range(MT):
                            src = conv_c[:, m, k:k + T]
                            if k == 0:
                                order.mark(dve.tensor_scalar(conv_h[:, m, :], src, col(CONV_W, m), col(CONV_B, m),
                                                             ALU.mult, ALU.add))
                            else:
                                order.mark(dve.scalar_tensor_tensor(conv_h[:, m, :], src, col(CONV_W + 8 * k, m),
                                                                    conv_h[:, m, :], ALU.mult, ALU.add))
                        order.settle()

                def keep_y(m):
                    dve.scalar_tensor_tensor(conv_h[:, m, :], ps[:, m, :], col(GB_CH * MT, m), conv_h[:, m, :],
                                             ALU.add, ALU.mult).then_inc(conv_done, 1)

                chunk(i * 3 + J_CONV, keep_h)
                dve.wait_ge(bank_free, i * 12 + (4 * J_CONV + 4 + 4))
                chunk(i * 3 + (J_CONV + 1), keep_c)
                dve.wait_ge(bank_free, i * 12 + (4 * J_CONV + 8 + 4))
                chunk(i * 3 + (J_CONV + 2), keep_y, taps)
                dve.wait_ge(conv_done, i * MT + MT)
                dve.sem_inc(bank_free, 4)
                for m in range(MT):
                    dve.wait_ge(yhi_made, i * MT + (m + 1))
                    order.mark(dve.tensor_tensor(yc_lo[:, i * MT + m, :], conv_h[:, m, :],
                                                 yc_hi[:, i * MT + m, :].bitcast(F32), ALU.subtract))
                order.settle()
                dve.sem_inc(ylo_made, 4)
                order.end(2)

            dve.wait_ge(rows_in, 32)
            with dve.Fori(0, 2, 1) as i:
                def keep_o(t):
                    dve.tensor_tensor(o_sig[:, t, :], ps[:, t, :], o_bias[:, bass.ds(i * CH, CH)], ALU.add
                                      ).then_inc(o_added, 1)
                chunk(i + J_O, keep_o)
                dve.wait_ge(o_added, i * NT + NT)
                dve.sem_inc(bank_free, 4)
                for t in range(NT):
                    dve.wait_ge(o_sigd, i * NT + (t + 1))
                    hs = h_sum[:, t, bass.ds(i * 2, 2), :]
                    dve.tensor_tensor(hs, hs, o_sig[:, t, :].rearrange("p (h v) -> p h v", h=2), ALU.mult
                                      ).then_inc(y_gated, 1)
            for k in range(8):
                dve.wait_ge(ym_hi, k + 1)
                dve.tensor_tensor(u_lo[:, k, :], ps[:, 4 + k % 2, :], u_hi[:, k, :].bitcast(F32), ALU.subtract
                                  ).then_inc(ym_lo, 1)

            def spread(col, dst, tile, r):
                for q in range(4):
                    for m in range(4):
                        c0 = col + 4 * q + m
                        order.mark(dve.tensor_scalar(tile[:, m, :], ident[:, :], mod[:, c0:c0 + 1], None, ALU.mult))
                    order.settle()
                    dve.sem_inc(diag_made, 1)
                    dve.wait_ge(row_made, 4 * r + q + 1)
                    dve.tensor_copy(dst[:, q * CH:(q + 1) * CH], ps[:, 7, :]).then_inc(row_kept, 1)

            spread(G1, g1_row, diag, 0)
            dve.wait_ge(row_kept, 4)
            dve.wait_ge(x_in, 32 * NT)
            with dve.Fori(0, 4, 1) as i:
                order.loop(i, NT)

                def keep_z(t):
                    order.link(dve.tensor_tensor(ps[:, t, :], ps[:, t, :], g1_row[:, bass.ds(i * CH, CH)], ALU.mult))
                    z = xz[:, t, bass.ds(i * CH, CH)]
                    dve.scalar_tensor_tensor(z, z, alpha, ps[:, t, :], ALU.mult, ALU.add).then_inc(bank_free, 1)

                chunk(i + J_OUT, keep_z)
                order.end(4)
            dve.wait_ge(bank_free, 4 * J_WQ + 4)
            dve.wait_ge(ada_reduced, ADA_ALL)
            for q in range(4):
                dve.wait_ge(sk_turned, q + 1)
                dve.tensor_copy(sk_t[:, 4 * q:4 * q + 4, :], ps[:, q, :].rearrange("p (a b) -> p a b", a=4)
                                ).then_inc(sk_kept, 1)
            for n in range(NT):
                row_stats(n)
            root(3, NT)
            for n in range(NT):
                order.mark(normal(n))
            order.settle()
            dve.wait_ge(rows_in, 64)
            for n in range(NT):
                order.mark(dve.tensor_tensor(xz[:, n, :], xz[:, n, :], ln1w_row[:, :], ALU.mult))
            order.settle()
            for n in range(NT):
                dve.tensor_tensor(xz[:, n, :], xz[:, n, :], ln1b_row[:, :], ALU.add).then_inc(x1_made, 1)
            dve.wait_ge(x1_made, NT)
            for n in range(NT):
                row_stats(n)
            root(4, NT)
            dve.wait_ge(x1_out, 16 * NT)
            for n in range(NT):
                normal(n).then_inc(x_normal, 1)
            dve.wait_ge(ada_kept, ADA_ALL)
            order.link(dve.tensor_scalar(mod[:, SC2:SC2 + KD], mod[:, SC2:SC2 + KD], 1.0, None, ALU.add))
            split_u(1, SC2, SH2)
            dve.wait_ge(ulo_made, 2 * KD)

            def q_chunk(i, last):
                for s in range(1, SLABS):
                    lo(s, i * 4 + (4 * J_WQ + s + 1))
                if not last:
                    lo(0, i * 4 + (4 * J_WQ + 5))
                for m in range(MT):
                    dve.wait_ge(tile_done, i * 4 + (4 * J_WQ + m + 1))
                    dve.tensor_copy(q_t[:, i * MT + m, :], ps[:, m, :]).then_inc(bank_free, 1)

            with dve.Fori(0, 3, 1) as i:
                q_chunk(i, False)
            q_chunk(3, True)
            with dve.Fori(0, NT, 1) as t:
                for g in range(4):
                    dve.wait_ge(sc_made, t * 4 + (g + 1))
                    dve.tensor_copy(scores[:, t, 4 * g:4 * g + 4, :], ps[:, 4 + g, :].rearrange("p (a b) -> p a b", a=4)
                                    ).then_inc(sc_kept, 1)

            def turn_lo(i, par):
                for h in range(2):
                    dve.wait_ge(eu_hi, i * 2 + (h + 1))
                    dve.tensor_tensor(w_lo[par][:, 2 * h:2 * h + 2, :], ps[:, 2 * h:2 * h + 2, :],
                                      w_hi[par][:, 2 * h:2 * h + 2, :].bitcast(F32), ALU.subtract).then_inc(eu_lo, 1)

            def pick(t, h, n):
                order.link(dve.tensor_copy(ws[:, :, :], scores[:, t, 2 * h:2 * h + 2, :]))
                dve.sem_inc(paced, 1)
                for half, src in ((0, ws), (8, ws2)):
                    for s in range(2):
                        order.mark(dve.max(top_s[:, s, half:half + 8], src[:, s, :]))
                    order.settle()
                    dve.sem_inc(paced, 1)
                    for s in range(2):
                        order.mark(dve.max_index(top_i[:, s, half:half + 8], top_s[:, s, half:half + 8], src[:, s, :]))
                    if half == 0:
                        for s in range(2):
                            order.mark(dve.match_replace(ws2[:, s, :], top_s[:, s, 0:8], ws[:, s, :], LOWEST))
                    order.settle()
                    dve.sem_inc(paced, 1)
                order.mark(dve.tensor_copy(top_f[:, :, :], top_i[:, :, :]))
                order.link(dve.tensor_tensor(cand[:, :, :], top_s[:, 0, :].unsqueeze(2).to_broadcast([P, TOPK, TOPK]),
                                             top_s[:, 1, :].unsqueeze(1).to_broadcast([P, TOPK, TOPK]), ALU.add))
                flat, flat2 = (v[:, :, :].rearrange("p a b -> p (a b)") for v in (cand, cand2))
                dve.sem_inc(paced, 1)
                order.link(dve.max(best_s[:, 0:8], flat))
                dve.sem_inc(paced, 1)
                order.mark(dve.max_index(best_c[:, 0:8], best_s[:, 0:8], flat))
                order.link(dve.match_replace(flat2, best_s[:, 0:8], flat, LOWEST))
                dve.sem_inc(paced, 1)
                order.link(dve.max(best_s[:, 8:16], flat2))
                dve.sem_inc(paced, 1)
                order.mark(dve.max_index(best_c[:, 8:16], best_s[:, 8:16], flat2))
                dve.tensor_scalar(neg_max[:, :], best_s[:, 0:1], -1.0, None, ALU.mult).then_inc(gexp_asked, 1)
                order.settle()
                order.mark(dve.tensor_scalar(best_j[:, 0, :], best_c[:, :], 4, None, ALU.logical_shift_right))
                order.link(dve.tensor_scalar(best_j[:, 1, :], best_c[:, :], 15, None, ALU.bitwise_and))
                order.link(dve.tensor_copy(best_f[:, :, :], best_j[:, :, :]))
                for s in range(2):
                    order.mark(dve.tensor_tensor(hot[:, s, :, :], best_f[:, s, :].unsqueeze(2).to_broadcast([P, TOPK, TOPK]),
                                                 iota[:, 0:TOPK].unsqueeze(1).to_broadcast([P, TOPK, TOPK]),
                                                 ALU.is_equal))
                order.settle()
                for s in range(2):
                    order.mark(dve.tensor_tensor(hot[:, s, :, :], hot[:, s, :, :],
                                                 top_f[:, s, :].unsqueeze(1).to_broadcast([P, TOPK, TOPK]), ALU.mult))
                order.settle()
                for s in range(2):
                    order.mark(dve.tensor_reduce(picks[:, s, h, :], hot[:, s, :, :], AX_X, ALU.add))
                dve.wait_ge(gexp_made, n)
                order.link(dve.reciprocal(g_inv[:, :], g_sum[:, :]))
                order.mark(dve.tensor_scalar(picks[:, 2, h, :], g_exp[:, :], g_inv[:, :], None, ALU.mult))

            def spread_gates(q):
                tok = bass.ds(q * G_TOK, G_TOK)
                shape = [P, G_TOK, NK]
                keys = iota[:, :].unsqueeze(1).to_broadcast(shape)
                dve.wait_ge(g_done, q)
                order.mark(dve.tensor_copy(gt_hr[:, :], by_pick[:, 2, tok]))
                order.mark(dve.tensor_tensor(hot1[:, :, :], by_pick[:, 0, tok].unsqueeze(2).to_broadcast(shape), keys,
                                             ALU.is_equal))
                order.link(dve.tensor_tensor(hot2[:, :, :], by_pick[:, 1, tok].unsqueeze(2).to_broadcast(shape), keys,
                                             ALU.is_equal))
                order.link(dve.tensor_tensor(gt_lo[:, :], by_pick[:, 2, tok], gt_hr[:, :].bitcast(F32), ALU.subtract))
                dve.tensor_tensor(hot2_hi[:, :, :], hot2[:, :, :],
                                  gt_hr[:, :].bitcast(F32).unsqueeze(2).to_broadcast(shape), ALU.mult
                                  ).then_inc(hot_made, 1)
                dve.tensor_tensor(hot2_lo[:, :, :], hot2[:, :, :], gt_lo[:, :].unsqueeze(2).to_broadcast(shape),
                                  ALU.mult).then_inc(hot_made, 1)

            turn_lo(0, 0)
            with dve.Fori(0, NT, 1) as r:
                order.loop(r, PH * 29 + 1)
                for h in range(PH):
                    turn_lo(r * 8 + (h + 1), (h + 1) % 2)
                    pick(r, h, r * 8 + (h + 1))
                order.settle()
                dve.sem_inc(picked, 1)
                dve.wait_ge(pick_turned, r + 1)
                order.link(dve.tensor_copy(by_pick[:, :, bass.ds(r * P, P)],
                                           ps[:, 6, 0:3 * P].rearrange("p (c t) -> p c t", c=3)))
                dve.sem_inc(pick_kept, 1)
                order.end(NT)
            with dve.Fori(0, T // G_BATCH, 1) as b:
                order.loop(b, 8 * 4)
                for n in range(8):
                    turn_lo(b * 8 + (33 + n), (n + 1) % 2)
                    spread_gates(b * 8 + n)
                order.end(T // G_BATCH)
            with dve.Fori(0, 15, 1) as r:
                for n in range(2):
                    turn_lo(r * 2 + (97 + n), (n + 1) % 2)
            turn_lo(ET - 1, 1)

            def gated(b, par):
                dve.wait_ge(hg_in[par], (b >> 1) * 32 + 32 if isinstance(b, int) else b * 16 + 32 - 16 * par)
                dve.tensor_tensor(h_in[par][:, :, :], h_in[par][:, :, :], g_in[par][:, :, :], ALU.mult
                                  ).then_inc(a_mul, 1)

            def gated_lo(b, par):
                dve.wait_ge(ahi_made, b + 1)
                dve.tensor_tensor(a_lo[par][:, :, :], h_in[par][:, :, :], a_hi[par][:, :, :].bitcast(F32),
                                  ALU.subtract).then_inc(alo_made, 1)

            def v_block(b, par, last):
                for dc in range(SLABS):
                    if dc < 3 or not last:
                        lo((dc + 1) % 4, b * 4 + (4 * NC + dc + 2))
                    if dc == 0 and not last:
                        gated(b + 1, 1 - par)
                    if dc == 1 and not last:
                        gated_lo(b + 1, 1 - par)
                    for t in range(NT):
                        dve.wait_ge(v_done, b * 16 + (4 * dc + t + 1))
                        y = y_acc[:, t, dc * CH:(dc + 1) * CH]
                        dve.tensor_tensor(y, y, ps[:, (4 * dc + t) % 8, :], ALU.add).then_inc(v_free, 1)

            gated(0, 0)
            gated_lo(0, 0)
            lo(0, 4 * NC + 1)
            dve.wait_ge(y_zero, 1)
            with dve.Fori(0, NB // 2 - 1, 1) as r:
                v_block(r * 2, 0, False)
                v_block(r * 2 + 1, 1, False)
            v_block(NB - 2, 0, False)
            v_block(NB - 1, 1, True)

            spread(G2, g2_row, diag2, 1)
            dve.wait_ge(row_kept, 8)
            dve.wait_ge(v_free, 16 * NB + 8)
            for n in range(NT):
                order.mark(dve.tensor_tensor(y_acc[:, n, :], y_acc[:, n, :], g2_row[:, :], ALU.mult))
            order.settle()
            dve.wait_ge(x1_back, 16)
            for n in range(NT):
                order.mark(dve.scalar_tensor_tensor(xz[:, n, :], xz[:, n, :], alpha, y_acc[:, n, :], ALU.mult, ALU.add))
            order.settle()
            for n in range(NT):
                row_stats(n)
            root(5, NT)
            for n in range(NT):
                order.mark(normal(n))
            order.settle()
            dve.wait_ge(rows_in, 96)
            for n in range(NT):
                order.mark(dve.tensor_tensor(xz[:, n, :], xz[:, n, :], ln2w_row[:, :], ALU.mult))
            order.settle()
            for n in range(NT):
                dve.tensor_tensor(xz[:, n, :], xz[:, n, :], ln2b_row[:, :], ALU.add).then_inc(out_made, 1)

        @block.tensor
        def _(pe):
            def ada_reduce(a):
                pe.wait_ge(ada_read, a * 4 + 4)
                pe.wait_ge(ada_kept, a)
                for m in range(4):
                    for k in range(4):
                        mm = pe.matmul(ps[:, 6, m:m + 1], ada_acc[:, k, m * P:(m + 1) * P], ones[:, 0:1],
                                       start=k == 0, stop=k == 3)
                mm.then_inc(ada_reduced, 1)

            def turn_x(r):
                pe.wait_ge(x_normal, NT * (r + 1))
                for k in range(KD):
                    if k >= 2:
                        pe.wait_ge(uf_made, KD * r + k - 1)
                    for n in range(NT):
                        mm = pe.transpose(ps[:, 4 + k % 2, n * P:(n + 1) * P], xz[:, n, k * P:(k + 1) * P],
                                          ident[:, :])
                    mm.then_inc(x_turned, 1)

            def three(bank, stat_hi, stat_lo, mov_hi, mov_lo, first, last):
                pe.matmul(bank, stat_hi, mov_hi, start=first, stop=False)
                pe.matmul(bank, stat_hi, mov_lo, start=False, stop=False)
                return pe.matmul(bank, stat_lo, mov_hi, start=False, stop=last)

            def u_tile(k):
                return u_hi[:, k, :], u_lo[:, k, :]

            def y_tile(k):
                if k < 8:
                    return yc_hi[:, k, :], yc_lo[:, k, :]
                return u_hi[:, k - 8, :], u_lo[:, k - 8, :]

            def chunk(j, feature_major, tile=u_tile):
                for s in range(SLABS):
                    pe.wait_ge(lo_made, j * 4 + (s + 1))
                    wh, wl = w_hi[s % 2], w_lo[s % 2]
                    for m in range(MT):
                        if s == 0:
                            pe.wait_ge(bank_free, j * 4 + (m + 1))
                        own = slice(m * P, (m + 1) * P)
                        for k in range(4):
                            uh, ul = tile(4 * s + k)
                            first, last = s == 0 and k == 0, s == 3 and k == 3
                            if feature_major:
                                mm = three(ps[:, m, :], wh[:, k, own], wl[:, k, own], uh, ul, first, last)
                            else:
                                mm = three(ps[:, m, :], uh[:, own], ul[:, own], wh[:, k, :], wl[:, k, :], first, last)
                        if s == 3:
                            mm.then_inc(tile_done, 1)
                    if s < 3:
                        mm.then_inc(slab_used, 1)

            pe.wait_ge(const_made, 1)
            pe.wait_ge(cond_ready, 1)
            pe.transpose(ps[:, 7, 0:KD], c_sig[:, :], ident[0:KD, 0:KD])
            pe.wait_ge(small_in, 80)
            pe.transpose(ps[:, 7, 128:128 + 6 * KD], ada_rows[:, :], ident[0:6 * KD, 0:6 * KD])
            pe.transpose(ps[:, 7, 256:256 + 64], vec_rows[:, :], ident[0:64, 0:64]).then_inc(first_turned, 1)
            with pe.Fori(0, ADA_FIRST, 1) as a:
                ada_reduce(a)
            turn_x(0)
            pe.wait_ge(ulo_made, KD)
            pe.wait_ge(gates_lo, 4)
            for k in range(KD):
                mm = three(ps[:, 7, :], g_hi[:, k, :], g_lo[:, k, :], *u_tile(k), k == 0, k == KD - 1)
            mm.then_inc(gates_proj, 1)
            pe.wait_ge(gate_step, 2)
            pe.wait_ge(gate_act, 2)
            for d in range(2):
                for t in range(NT):
                    c0 = (d * NT + t) * HEADS
                    pe.transpose(ps[:, 7, c0:c0 + HEADS], gate_t[:, 2 * d, t * P:(t + 1) * P],
                                 ident[0:HEADS, 0:HEADS])
                    mm = pe.transpose(ps[:, 7, 32 + c0:32 + c0 + HEADS], g_b[:, d, t * P:(t + 1) * P],
                                      ident[0:HEADS, 0:HEADS])
            mm.then_inc(gates_turned, 1)
            with pe.Fori(0, 2, 1) as i:
                chunk(i, True)
                ada_reduce(i + ADA_FIRST)
            with pe.Fori(0, 2, 1) as i:
                chunk(i + J_V, False)
                ada_reduce(i + (ADA_FIRST + J_V))
            pe.wait_ge(ada_kept, ADA_FIRST + J_CONV)
            pe.wait_ge(bank_free, 4 * J_CONV + 4)
            for h in range(HEADS):
                if h:
                    pe.wait_ge(p_made, 2 * NT * h)
                for st in range(NT):
                    pe.matmul(ps[:, st, :], qk[:, 1, h, st * P:(st + 1) * P], qk[:, 0, h, :], start=True, stop=True
                              ).then_inc(s_made, 1)
                for d in range(2):
                    mm = pe.matmul(ps[:, 4 + d, :], sel[:, h, :], g_M[:, d, :], start=True, stop=True)
                mm.then_inc(m_made, 1)
                for d in range(2):
                    n = 2 * h + d
                    pe.wait_ge(p_made, NT * (n + 1))
                    for t in range(NT):
                        if NT * n + t >= 2:
                            pe.wait_ge(hd_kept, NT * n + t - 1)
                        sts = list(range(t + 1)) if d == 0 else list(range(t, NT))
                        for st in sts:
                            mm = pe.matmul(ps[:, 6 + t % 2, 0:DV + 1], prob[:, st, t * P:(t + 1) * P],
                                           v_aug[:, st, h, 0:DV + 1], start=st == sts[0], stop=st == sts[-1])
                        mm.then_inc(hd_out, 1)
            pe.wait_ge(hd_kept, 8 * NT)
            with pe.Fori(0, 2, 1) as i:
                for r in range(3):
                    chunk(i * 3 + (J_CONV + r), True)
                    ada_reduce(i * 3 + (ADA_FIRST + J_CONV + r))
            with pe.Fori(0, 2, 1) as i:
                chunk(i + J_O, False)
                ada_reduce(i + (ADA_FIRST + J_O))
            pe.wait_ge(y_gated, 2 * NT)
            for k in range(8):
                if k >= 2:
                    pe.wait_ge(ym_lo, k - 1)
                for t in range(NT):
                    mm = pe.transpose(ps[:, 4 + k % 2, t * P:(t + 1) * P],
                                      h_sum[:, t, k // 2, (k % 2) * P:(k % 2 + 1) * P], ident[:, :])
                mm.then_inc(y_turned, 1)

            def spread(tile, r):
                for q in range(4):
                    pe.wait_ge(diag_made, 4 * r + q + 1)
                    pe.wait_ge(row_kept, 4 * r + q)
                    for m in range(4):
                        mm = pe.matmul(ps[:, 7, m * P:(m + 1) * P], ones[:, :], tile[:, m, :], start=True, stop=True)
                    mm.then_inc(row_made, 1)

            spread(diag, 0)
            pe.wait_ge(ylo_made, 8)
            pe.wait_ge(ym_lo, 8)
            with pe.Fori(0, 4, 1) as i:
                chunk(i + J_OUT, False, y_tile)
                ada_reduce(i + (ADA_FIRST + J_OUT))
            pe.wait_ge(bank_free, 4 * J_WQ + 4)
            pe.wait_ge(small_in, 112)
            for q in range(4):
                for m in range(4):
                    mm = pe.transpose(ps[:, q, m * P:(m + 1) * P], sk_raw[:, 4 * q + m, :], ident[:, :])
                mm.then_inc(sk_turned, 1)
            turn_x(1)
            pe.wait_ge(ulo_made, 2 * KD)
            pe.wait_ge(sk_kept, 4)
            with pe.Fori(0, 4, 1) as i:
                chunk(i + J_WQ, True)
            pe.wait_ge(bank_free, 4 * NC + 4)
            for t in range(NT):
                for g in range(4):
                    if t:
                        pe.wait_ge(sc_kept, 4 * (t - 1) + g + 1)
                    for m in range(4):
                        mm = pe.matmul(ps[:, 4 + g, m * P:(m + 1) * P], q_t[:, 4 * g + m, t * P:(t + 1) * P],
                                       sk_t[:, 4 * g + m, :], start=True, stop=True)
                    mm.then_inc(sc_made, 1)
            pe.wait_ge(sc_kept, 16)

            def turn_u(i, slot, loaded, read):
                pe.wait_ge(slab_in[slot], loaded)
                for h in range(2):
                    if read is not None:
                        pe.wait_ge(eu_lo, read + h)
                    for k in range(8 * h, 8 * h + 8):
                        own = slice((k % 4) * P, (k % 4 + 1) * P)
                        mm = pe.transpose(ps[:, k // 4, own], raw[slot][:, k // 4, own], ident[:, :])
                    mm.then_inc(u_turned, 1)

            def u_products(i, par):
                pe.wait_ge(eu_lo, i * 2 + 2)
                for k in range(KD):
                    own = slice((k % 4) * P, (k % 4 + 1) * P)
                    mm = three(ps[:, 4 + par, :], w_hi[par][:, k // 4, own], w_lo[par][:, k // 4, own], *u_tile(k),
                               k == 0, k == KD - 1)
                mm.then_inc(u_done, 1)

            def u_step(i, n, loaded):
                turn_u(i + 1, (n + 1) % 4, loaded, i * 2 + 1)
                u_products(i, n % 2)

            turn_u(0, 0, 16 * 45, None)
            with pe.Fori(0, NT, 1) as r:
                for n in range(8):
                    u_step(r * 8 + n, n, r * 32 + 16 * (45 + (n + 1) // 4))
                pe.wait_ge(picked, r + 1)
                pe.wait_ge(pick_kept, r)
                for s in range(3):
                    mm = pe.transpose(ps[:, 6, s * P:(s + 1) * P], picks[:, s, :, :].rearrange("p h k -> p (h k)"),
                                      ident[:, :])
                mm.then_inc(pick_turned, 1)
            pe.wait_ge(pick_kept, NT)
            with pe.Fori(0, T // G_BATCH, 1) as b:
                for n in range(8):
                    u_step(b * 8 + (32 + n), n, b * 32 + 16 * (53 + (n + 1) // 4))
                    pe.wait_ge(hot_made, b * 16 + (2 * n + 2))
                    pe.wait_ge(g_kept, b * 16 + 2 * n)
                    for t in range(G_TOK):
                        bank = ps[:, 6 + t // 4, (t % 4) * P:(t % 4 + 1) * P]
                        pe.matmul(bank, hot2_hi[:, t, :], hot1[:, t, :], start=True, stop=False)
                        mm = pe.matmul(bank, hot2_lo[:, t, :], hot1[:, t, :], start=False, stop=True)
                    mm.then_inc(g_done, 1)
            with pe.Fori(0, 7, 1) as r:
                for n in range(4):
                    u_step(r * 4 + (96 + n), n, r * 16 + 16 * (69 + (n + 1) // 4))
            for n in range(3):
                u_step(124 + n, n, 16 * 76)
            u_products(ET - 1, 1)

            def v_block(b, par):
                pe.wait_ge(alo_made, b + 1)
                for dc in range(SLABS):
                    pe.wait_ge(lo_made, b * 4 + (4 * NC + dc + 1))
                    for t in range(NT):
                        pe.wait_ge(v_free, b * 16 + (4 * dc + t + 1))
                        own = slice(t * P, (t + 1) * P)
                        for e in range(4):
                            mm = three(ps[:, (4 * dc + t) % 8, :], a_hi[par][:, e, own], a_lo[par][:, e, own],
                                       w_hi[dc % 2][:, e, :], w_lo[dc % 2][:, e, :], e == 0, e == 3)
                        mm.then_inc(v_done, 1)

            pe.wait_ge(h_made, ET)
            with pe.Fori(0, NB // 2, 1) as r:
                for i in range(2):
                    v_block(r * 2 + i, i)
            pe.wait_ge(v_free, 16 * NB + 8)
            spread(diag2, 1)


_INS = ['x', 'c', 'w_ada', 'b_ada', 'w_in', 'b_in', 'conv_w', 'conv_b', 'mlstm_norm_w', 'w_out', 'ln1_w', 'ln1_b',
        'peer_wq', 'peer_subkeys', 'peer_u', 'peer_v', 'ln2_w', 'ln2_b']
_OUT = (1, T, D)


def kernel(**inputs):
    import concourse.bacc as _bacc
    from concourse.bass_utils import run_bass_kernel_spmd as _run

    nc = _bacc.Bacc("TRN2", target_bir_lowering=False, num_devices=1)
    arrays, args = {}, []
    for name in _INS:
        a = np.ascontiguousarray(inputs[name])
        arrays[f"in_{name}_dram"] = a
        args.append(nc.dram_tensor(f"in_{name}_dram", a.shape, mybir.dt.from_np(a.dtype), kind="ExternalInput").ap())
    args.append(nc.dram_tensor("out_dram", _OUT, F32, kind="ExternalOutput").ap())
    build_layer(nc, *args, alpha=2.0 ** 0.25)
    r = _run(nc, [arrays], core_ids=[0])
    return r.results[0]["out_dram"]
```

```python
from contextlib import ExitStack

import numpy as np

import concourse.bass as bass
from concourse import mybir

ALU = mybir.AluOpType
ACT = mybir.ActivationFunctionType
F32 = mybir.dt.float32
F32R = mybir.dt.float32r
U32 = mybir.dt.uint32
AX_X = mybir.AxisListType.X

P = 128
T = 512
NT = T // P
D = 2048
KD = D // P
CH = 512
MT = CH // P
SLABS = 4
HEADS, DK, DV = 4, 128, 256
CONV = 1024
GATE_COL = 6144
PH, TOPK, NK = 8, 16, 128
G_TOK = 8
NE = NK * NK
ET = NE // P
LN_EPS = 1e-5
LOWEST = float(np.finfo(np.float32).min)

SH1, SC1, G1, SH2, SC2, G2 = (KD * i for i in range(6))
GB_CH, GC_CH, HIN_CH, Q_CH, V_CH, O_CH = 0, 2, 4, 6, 8, 10
J_V, J_CONV, J_O, J_OUT, J_WQ = 2, 4, 10, 12, 16
ADA_FIRST = 8
ADA_ALL = 24


class Tally:

    def __init__(self, eng, sem):
        self.eng, self.sem, self.base, self.k = eng, sem, 0, 0

    def loop(self, i, per):
        self.start, self.per = self.base + self.k, per
        self.base, self.k = i * per + self.start, 0

    def end(self, rounds):
        assert self.k == self.per, (self.k, self.per)
        self.base, self.k = self.start + rounds * self.per, 0

    def mark(self, ins):
        ins.then_inc(self.sem, 1)
        self.k += 1

    def settle(self):
        self.eng.wait_ge(self.sem, self.base + self.k)

    def link(self, ins):
        self.mark(ins)
        self.settle()


def build_layer(nc, x, c, w_ada, b_ada, w_in, b_in, conv_w, conv_b, mlstm_norm_w, w_out, ln1_w, ln1_b,
                peer_wq, peer_subkeys, peer_u, peer_v, ln2_w, ln2_b, out, alpha):
    with ExitStack() as ctx:
        def at(name, shape, offset, dt=F32):
            return nc.alloc_sbuf_tensor_at(name, shape, dt, offset=offset)

        def sem(name):
            return ctx.enter_context(nc.semaphore(name))

        KB = 1024
        base = (nc.sbuf_base + 31) // 32 * 32
        raw = [at(f"raw{s}", [P, 4, CH], base + 8 * KB * s) for s in range(SLABS)]
        o_split = base + 32 * KB
        w_hi = [at(f"w_hi{i}", [P, 4, CH], o_split + 8 * KB * i, F32R) for i in range(2)]
        w_lo = [at(f"w_lo{i}", [P, 4, CH], o_split + 16 * KB + 8 * KB * i, F32R) for i in range(2)]
        o_u = o_split + 32 * KB
        u_hi = at("u_hi", [P, KD, T], o_u, F32R)
        u_lo = at("u_lo", [P, KD, T], o_u + 32 * KB, F32R)

        o_const = [o_u + 64 * KB]

        def const(name, shape, dt=F32):
            t = at(name, shape, o_const[0], dt)
            n = 4
            for m in shape[1:]:
                n *= m
            o_const[0] += (n + 31) // 32 * 32
            return t

        ident = const("ident", [P, P])
        ones = const("ones", [P, P])
        iota = const("iota", [P, P])
        mask_fwd = const("mask_fwd", [P, P])
        mask_bwd = const("mask_bwd", [P, P])
        cond = const("cond", [P, KD])
        b_ada_c = const("b_ada_c", [P, 6 * KD])
        mod = const("mod", [P, 6 * KD])
        vec_c = const("vec_c", [P, 64])
        CONV_W, CONV_B = 32, 56
        gate_b = const("gate_b", [P, 1])
        stat = const("stat", [P, NT, 4, 6])
        mv = const("mv", [P, 4 * NT, 2])
        rstd = const("rstd", [P, 4 * NT])
        a_col = const("a_col", [P, 2, NT, HEADS])
        em_col = const("em_col", [P, 2, NT, HEADS])
        den = const("den", [P, 2, 2])
        gt_hr = const("gt_hr", [P, 2, G_TOK], F32R)
        gt_lo = const("gt_lo", [P, 2, G_TOK])
        W1 = o_const[0]
        H0 = W1 + 33024

        xz = at("xz", [P, NT, D], H0)
        u_f = [at(f"u_f{i}", [P, T], W1 + 16 * KB + 2 * KB * i) for i in range(4)]
        c_rows = at("c_rows", [KD, P], W1 + 24 * KB)
        c_sig = at("c_sig", [KD, P], W1 + 25 * KB)
        ada_rows = at("ada_rows", [6 * KD, P], W1 + 26 * KB)
        vec_rows = at("vec_rows", [64, P], W1 + 27 * KB)
        qk = at("qk", [P, 2, HEADS, T], W1)
        v_aug = at("v_aug", [P, NT, HEADS, DV + 2], W1 + 16 * KB)
        h_sum = at("h_sum", [P, NT, HEADS, DV], H0)
        g_hi = at("g_hi", [P, KD, P], H0, F32R)
        g_lo = at("g_lo", [P, KD, P], H0 + 8 * KB, F32R)
        gate_t = at("gate_t", [HEADS, 4, T], H0 + 16 * KB)
        g_raw = at("g_raw", [P, KD, 16], H0 + 24 * KB)
        prob = [at(f"prob{d}", [P, NT, T], H0 + (16 + 18 * d) * KB) for d in range(2)]
        v_bias = at("v_bias", [P, 2 * CH], H0 + 16 * KB)
        g_M = at("g_M", [HEADS, 2, T], H0 + 24 * KB)
        g_b = at("g_b", [HEADS, 2, T], H0 + 28 * KB)
        norm_row = at("norm_row", [P, HEADS * DV], H0 + 24 * KB)
        sel = at("sel", [HEADS, HEADS, P], H0 + 32 * KB)
        yc_hi = at("yc_hi", [P, 8, T], W1, F32R)
        yc_lo = at("yc_lo", [P, 8, T], W1 + 16 * KB, F32R)
        conv_h = at("conv_h", [P, MT, T], H0 + 16 * KB)
        conv_c = at("conv_c", [P, MT, T + 2], H0 + 24 * KB)
        o_sig = at("o_sig", [P, 4, CH], H0 + 16 * KB)
        o_bias = at("o_bias", [P, 2 * CH], H0 + 28 * KB)
        ada_acc = [at("ada_acc", [P, 4, CH], H0 + 34 * KB), at("ada_acc1", [P, 4, CH], W1)]
        assert H0 + 42 * KB <= nc.sbuf_usable_end, (H0 + 42 * KB, nc.sbuf_usable_end)
        g1_row = at("g1_row", [P, D], o_u + 16 * KB)
        ln1w_row = at("ln1w_row", [P, D], o_u + 24 * KB)
        ln1b_row = at("ln1b_row", [P, D], o_u + 48 * KB)
        diag = at("diag", [P, 4, P], o_u + 56 * KB)
        sk_raw = at("sk_raw", [P, 2 * PH, P], W1)
        sk_t = at("sk_t", [P, 2 * PH, P], H0 + 34 * KB)
        q_t = at("q_t", [P, 2 * PH, T], W1)
        scores = at("scores", [P, NT, 2 * PH, NK], H0)
        pick = [W1]

        def scratch(name, shape, dt=F32):
            t = at(name, shape, pick[0], dt)
            n = 4
            for m in shape[1:]:
                n *= m
            pick[0] += (n + 31) // 32 * 32
            return t

        ws = scratch("ws", [P, 2, NK])
        ws2 = scratch("ws2", [P, 2, NK])
        top_s = scratch("top_s", [P, 2, TOPK])
        top_i = scratch("top_i", [P, 2, TOPK], U32)
        top_f = scratch("top_f", [P, 2, TOPK])
        cand = scratch("cand", [P, TOPK, TOPK])
        cand2 = scratch("cand2", [P, TOPK, TOPK])
        best_s = scratch("best_s", [P, TOPK])
        best_c = scratch("best_c", [P, TOPK], U32)
        best_j = scratch("best_j", [P, 2, TOPK], U32)
        best_f = scratch("best_f", [P, 2, TOPK])
        hot = scratch("hot", [P, 2, TOPK, TOPK])
        neg_max = scratch("neg_max", [P, PH])
        g_exp = scratch("g_exp", [P, PH, TOPK])
        g_sum = scratch("g_sum", [P, PH])
        g_inv = scratch("g_inv", [P, PH])
        picks = scratch("picks", [P, 3, PH, TOPK])
        G_BATCH = 64
        STEPS_HOT = [2, 1, 1, 2, 1, 1, 0, 0]
        STEPS_MUL = [1, 2, 1, 1, 2, 1, 0, 0]
        LAST_STEP = 5
        gates_sb = at("gates_sb", [P, NK, G_BATCH], W1)
        hot1 = [at(f"hot1_{i}", [P, G_TOK, NK], H0 + 16 * KB * i, F32R) for i in range(2)]
        hot2 = [at(f"hot2_{i}", [P, G_TOK, NK], H0 + 16 * KB * i + 4 * KB) for i in range(2)]
        hot2_hi = [at(f"hot2_hi{i}", [P, G_TOK, NK], H0 + 16 * KB * i + 8 * KB, F32R) for i in range(2)]
        hot2_lo = [at(f"hot2_lo{i}", [P, G_TOK, NK], H0 + 16 * KB * i + 12 * KB, F32R) for i in range(2)]
        h_stage = at("h_stage", [P, T], H0 + 32 * KB)
        by_pick = at("by_pick", [P, 3, T], H0 + 36 * KB)
        a_hi = [at(f"a_hi{i}", [P, 4, T], o_u + 8 * KB * i, F32R) for i in range(2)]
        a_lo = [at(f"a_lo{i}", [P, 4, T], o_u + 16 * KB + 8 * KB * i, F32R) for i in range(2)]
        h_in = [at(f"h_in{i}", [P, 4, T], H0 + 8 * KB * i) for i in range(2)]
        g_in = [at(f"g_in{i}", [P, 4, T], H0 + 16 * KB + 8 * KB * i) for i in range(2)]
        y_acc = at("y_acc", [P, NT, D], W1)
        x1 = at("x1", [P, NT, D], o_u + 32 * KB)
        g2_row = at("g2_row", [P, D], H0 + 34 * KB)
        ln2w_row = at("ln2w_row", [P, D], H0)
        ln2b_row = at("ln2b_row", [P, D], H0 + 16 * KB)

        ps = ctx.enter_context(nc.psum_tensor("ps", [P, 8, CH], F32))

        x1_dram = nc.dram_tensor("x1_scratch", [T, D], F32, kind="Internal").ap()
        h_dram = nc.dram_tensor("h_scratch", [NE, T], F32, kind="Internal").ap()
        g_dram = nc.dram_tensor("g_scratch", [NE, T], F32, kind="Internal").ap()

        x_v = x.rearrange("b (n p) d -> p (b n) d", p=P)
        out_v = out.rearrange("b (n p) d -> p (b n) d", p=P)
        x1_v = x1_dram.rearrange("(n p) d -> p n d", p=P)
        ada_v = w_ada[0].rearrange("(k p) n -> p k n", p=P)
        win_v = w_in[0].rearrange("(k p) n -> p k n", p=P)
        wout_v = w_out[0].rearrange("(k p) n -> p k n", p=P)
        wq_v = peer_wq[0].rearrange("(k p) n -> p k n", p=P)
        pu_v = peer_u[0].rearrange("(e p) (k n) -> p e k n", p=P, n=CH)
        pv_v = peer_v[0].rearrange("(e p) n -> p e n", p=P)
        h_v = h_dram.rearrange("(e p) t -> p e t", p=P)
        g_v = g_dram.rearrange("(e p) t -> p e t", p=P)

        def row(v, lo, n):
            return v[0, lo:lo + n].partition_broadcast(P)

        small_in = sem("small_in")
        x_in = sem("x_in")
        rows_in = sem("rows_in")
        slab_in = [sem(f"slab_in{s}") for s in range(SLABS)]
        const_made = sem("const_made")
        silu_made = sem("silu_made")
        first_turned = sem("first_turned")
        cond_ready = sem("cond_ready")
        x_normal = sem("x_normal")
        sqrt_asked = sem("sqrt_asked")
        sqrt_made = sem("sqrt_made")
        x_turned = sem("x_turned")
        mod_ready = sem("mod_ready")
        uf_made = sem("uf_made")
        uhi_made = sem("uhi_made")
        ulo_made = sem("ulo_made")
        ada_read = sem("ada_read")
        ada_half = sem("ada_half")
        ada_added = sem("ada_added")
        ada_reduced = sem("ada_reduced")
        ada_kept = sem("ada_kept")
        hi_made = sem("hi_made")
        lo_made = sem("lo_made")
        slab_used = sem("slab_used")
        tile_done = sem("tile_done")
        bank_free = sem("bank_free")
        gates_zero = sem("gates_zero")
        gates_hi = sem("gates_hi")
        gates_lo = sem("gates_lo")
        gate_b_in = sem("gate_b_in")
        norm_in = sem("norm_in")
        y_zero = sem("y_zero")
        gates_proj = sem("gates_proj")
        gate_step = sem("gate_step")
        gate_act = sem("gate_act")
        gates_ready = sem("gates_ready")
        gates_turned = sem("gates_turned")
        cols_kept = sem("cols_kept")
        s_made = sem("s_made")
        m_made = sem("m_made")
        e_asked = sem("e_asked")
        e_made = sem("e_made")
        p_made = sem("p_made")
        hd_out = sem("hd_out")
        hd_kept = sem("hd_kept")
        conv_done = sem("conv_done")
        yhi_made = sem("yhi_made")
        ylo_made = sem("ylo_made")
        o_added = sem("o_added")
        o_sigd = sem("o_sigd")
        y_gated = sem("y_gated")
        y_turned = sem("y_turned")
        ym_hi = sem("ym_hi")
        ym_lo = sem("ym_lo")
        diag_made = sem("diag_made")
        row_made = sem("row_made")
        row_kept = sem("row_kept")
        x1_made = sem("x1_made")
        x1_out = sem("x1_out")
        sk_turned = sem("sk_turned")
        sk_kept = sem("sk_kept")
        sc_made = sem("sc_made")
        sc_kept = sem("sc_kept")
        u_turned = sem("u_turned")
        eu_hi = sem("eu_hi")
        eu_lo = sem("eu_lo")
        u_done = sem("u_done")
        h_made = sem("h_made")
        h_out = sem("h_out")
        gexp_asked = sem("gexp_asked")
        gexp_made = sem("gexp_made")
        picked = sem("picked")
        pick_turned = sem("pick_turned")
        pick_kept = sem("pick_kept")
        hot_made = sem("hot_made")
        g_done = sem("g_done")
        g_kept = sem("g_kept")
        g_out = sem("g_out")
        batch_out = sem("batch_out")
        hg_in = [sem(f"hg_in{i}") for i in range(2)]
        a_mul = sem("a_mul")
        ahi_made = sem("ahi_made")
        alo_made = sem("alo_made")
        v_done = sem("v_done")
        v_free = sem("v_free")
        x1_back = sem("x1_back")
        out_made = sem("out_made")
        out_sent = sem("out_sent")
        dve_order = sem("dve_order")
        paced = sem("paced")
        act_order = sem("act_order")
        pool_order = sem("pool_order")

        NC = 20
        NB = ET // 4

        block = ctx.enter_context(nc.Block())

        @block.sync
        def _(sp):
            def load(s, src):
                sp.dma_start(raw[s][:, :, :], src).then_inc(slab_in[s], 16)

            for s in range(SLABS):
                load(s, ada_v[:, 4 * s:4 * s + 4, 0:CH])
            for n in range(NT):
                sp.dma_start(xz[:, n, :], x_v[:, n, :]).then_inc(x_in, 16)
            with sp.Fori(1, ADA_FIRST, 1) as g:
                for s in range(SLABS):
                    sp.wait_ge(ada_read, g * 4 + (s - 3))
                    load(s, ada_v[:, 4 * s:4 * s + 4, bass.ds(g * CH, CH)])

            def projection(j, src, col, ada):
                for s in range(SLABS):
                    sp.wait_ge(ada_read, j * 4 + (4 * ADA_FIRST - 4 + s + 1))
                    load(s, src[:, 4 * s:4 * s + 4, bass.ds(col, CH)])
                for s in range(SLABS):
                    sp.wait_ge(lo_made, j * 4 + (s + 1))
                    load(s, ada_v[:, 4 * s:4 * s + 4, bass.ds(ada * CH, CH)])

            with sp.Fori(0, 4, 1) as i:
                projection(i, win_v, (i + Q_CH) * CH, i + ADA_FIRST)
            with sp.Fori(0, 2, 1) as i:
                for r, first in enumerate((HIN_CH, GC_CH, GB_CH)):
                    projection(i * 3 + (J_CONV + r), win_v, (i + first) * CH, i * 3 + (J_CONV + r + ADA_FIRST))
            with sp.Fori(0, 2, 1) as i:
                projection(i + J_O, win_v, (i + O_CH) * CH, i + (J_O + ADA_FIRST))
            with sp.Fori(0, 4, 1) as i:
                projection(i + J_OUT, wout_v, i * CH, i + (J_OUT + ADA_FIRST))
            for s in range(SLABS):
                sp.wait_ge(ada_read, 4 * ADA_ALL - 4 + s + 1)
                load(s, wq_v[:, 4 * s:4 * s + 4, 0:CH])
            with sp.Fori(1, 4, 1) as i:
                for s in range(SLABS):
                    sp.wait_ge(lo_made, i * 4 + (4 * (J_WQ - 1) + s + 1))
                    load(s, wq_v[:, 4 * s:4 * s + 4, bass.ds(i * CH, CH)])
            for s in range(SLABS):
                sp.wait_ge(lo_made, 4 * (NC - 1) + s + 1)
                load(s, pu_v[:, s, :, :])
            with sp.Fori(1, NB, 1) as b:
                for s in range(SLABS):
                    sp.wait_ge(u_turned, b * 8 + (2 * s - 6))
                    load(s, pu_v[:, b * 4 + s, :, :])

            def load_hg(b, i, stored):
                if stored is not None:
                    sp.wait_ge(alo_made, stored)
                sp.dma_start(h_in[i][:, :, :], h_v[:, bass.ds(b * 4, 4), :]).then_inc(hg_in[i], 16)
                sp.dma_start(g_in[i][:, :, :], g_v[:, bass.ds(b * 4, 4), :]).then_inc(hg_in[i], 16)

            sp.wait_ge(h_out, 16 * 96)
            sp.wait_ge(g_out, 32 * T // G_BATCH)
            load_hg(0, 0, None)
            load_hg(1, 1, None)
            for s in range(SLABS):
                sp.wait_ge(u_turned, 2 * (ET - 4 + s + 1))
                load(s, pv_v[:, 0:4, s * CH:s * CH + CH])
            for s in range(SLABS):
                sp.wait_ge(lo_made, 4 * NC + s + 1)
                load(s, pv_v[:, 4:8, s * CH:s * CH + CH])
            with sp.Fori(1, NB // 2, 1) as r:
                for i in range(2):
                    sp.wait_ge(h_out, r * 128 + (64 * i + 64))
                    load_hg(r * 2 + i, i, r * 2 + (i - 1))
                    for s in range(SLABS):
                        sp.wait_ge(lo_made, r * 8 + (4 * i + 4 * NC - 4 + s + 1))
                        load(s, pv_v[:, bass.ds((r * 2 + i) * 4, 4), s * CH:s * CH + CH])
            for n in range(NT):
                sp.wait_ge(out_made, n + 1)
                sp.dma_start(out_v[:, n, :], x1[:, n, :]).then_inc(out_sent, 16)
            sp.wait_ge(out_sent, 16 * NT)
            sp.wait_ge(x1_out, 16 * NT)

        @block.gpsimd
        def _(pool):
            order = Tally(pool, pool_order)
            order.mark(pool.memset(ident[:, :], 0.0))
            order.mark(pool.memset(ones[:, :], 1.0))
            order.mark(pool.memset(sel[:, :, :], 0.0))
            order.mark(pool.memset(gate_b[:, :], 0.0))
            order.settle()
            order.mark(pool.affine_select(out=ident[:, :], in_=ident[:, :], compare_op=ALU.not_equal, fill=1.0,
                                          base=0, pattern=[[-1, P]], channel_multiplier=1))
            order.mark(pool.affine_select(out=mask_fwd[:, :], in_=ones[:, :], compare_op=ALU.is_ge, fill=0.0,
                                          base=0, pattern=[[1, P]], channel_multiplier=-1))
            order.mark(pool.affine_select(out=mask_bwd[:, :], in_=ones[:, :], compare_op=ALU.is_ge, fill=0.0,
                                          base=0, pattern=[[-1, P]], channel_multiplier=1))
            order.mark(pool.affine_select(out=sel[:, :, :], in_=sel[:, :, :], compare_op=ALU.not_equal, fill=1.0,
                                          base=0, pattern=[[-1, HEADS], [0, P]], channel_multiplier=1))
            order.mark(pool.iota(iota[:, :], [[1, P]], base=0, channel_multiplier=0,
                                 allow_small_or_imprecise_dtypes=True))
            order.settle()
            pool.sem_inc(const_made, 1)
            for g in range(4):
                pool.dma_start(gate_b[32 * g:32 * g + HEADS, :],
                               b_in[0, GATE_COL + HEADS * g:GATE_COL + HEADS * (g + 1)].unsqueeze(1)
                               ).then_inc(gate_b_in, 16)

            def ada_add(a, acc):
                pool.wait_ge(ada_read, a * 4 + 4)
                pool.tensor_tensor(acc[:, 0:2, :], acc[:, 0:2, :], acc[:, 2:4, :], ALU.add).then_inc(ada_half, 1)
                pool.wait_ge(ada_half, a + 1)
                pool.tensor_tensor(acc[:, 0, :], acc[:, 0, :], acc[:, 1, :], ALU.add).then_inc(ada_added, 1)

            with pool.Fori(0, ADA_FIRST // 2, 1) as i:
                for k in range(2):
                    ada_add(i * 2 + k, ada_acc[k])
            with pool.Fori(ADA_FIRST, ADA_FIRST + J_CONV, 1) as a:
                ada_add(a, ada_acc[0])
            with pool.Fori(0, 2, 1) as i:
                for r in range(3):
                    ada_add(i * 3 + (ADA_FIRST + J_CONV + r), ada_acc[0])
                for m in range(MT):
                    pool.wait_ge(yhi_made, i * MT + (m + 1))
                    pool.tensor_tensor(yc_lo[:, i * MT + m, :], conv_h[:, m, :],
                                       yc_hi[:, i * MT + m, :].bitcast(F32), ALU.subtract).then_inc(ylo_made, 1)
            with pool.Fori(ADA_FIRST + J_O, ADA_ALL, 1) as a:
                ada_add(a, ada_acc[0])

            def store_h(i):
                pool.wait_ge(h_made, i + 1)
                pool.dma_start(h_v[:, i, :], h_stage[:, :]).then_inc(h_out, 16)

            with pool.Fori(0, 32, 1) as i:
                store_h(i)

            def store_gates(b):
                pool.wait_ge(g_kept, 1 + b * 16 + 16)
                for h in range(2):
                    keys = slice(h * NK // 2, (h + 1) * NK // 2)
                    pool.dma_start(g_dram.rearrange("(a b) t -> b a t", b=P)[:, keys, bass.ds(b * G_BATCH, G_BATCH)],
                                   gates_sb[:, keys, :]).then_inc(g_out, 16)

            with pool.Fori(0, T // G_BATCH, 1) as b:
                for i in range(8):
                    store_h(b * 8 + (32 + i))
                    if i == LAST_STEP:
                        store_gates(b)
                pool.wait_ge(g_out, b * 32 + 32)
                pool.sem_inc(batch_out, 1)
            pool.wait_ge(g_out, 32 * T // G_BATCH)
            pool.memset(y_acc[:, :, :], 0.0).then_inc(y_zero, 1)
            with pool.Fori(96, ET, 1) as i:
                store_h(i)

        @block.scalar
        def _(act):
            order = Tally(act, act_order)
            act.sem_inc(g_kept, 1)
            act.dma_start(c_rows[:, :], c.rearrange("b (k p) -> (b k) p", p=P)).then_inc(small_in, 16)
            act.dma_start(ada_rows[:, :], b_ada[0].rearrange("(k p) -> k p", p=P)).then_inc(small_in, 16)
            act.dma_start(vec_rows[0:32, :], b_in[0, 0:32 * P].rearrange("(k p) -> k p", p=P)).then_inc(small_in, 16)
            act.dma_start(vec_rows[32:56, :], conv_w[0].rearrange("w (k p) -> (w k) p", p=P)).then_inc(small_in, 16)
            act.dma_start(vec_rows[56:64, :], conv_b[0].rearrange("(k p) -> k p", p=P)).then_inc(small_in, 16)
            act.wait_ge(small_in, 80)
            act.activation(c_sig[:, :], c_rows[:, :], ACT.Sigmoid).then_inc(silu_made, 1)

            def root(n, width):
                act.wait_ge(sqrt_asked, n)
                act.activation(rstd[:, 0:width], rstd[:, 0:width], ACT.Sqrt).then_inc(sqrt_made, 1)

            def split_u(r, scale, shift):
                act.wait_ge(mod_ready, r + 1)
                with act.Fori(0, KD // 4, 1) as i:
                    order.loop(i, 2)
                    for k in range(4):
                        if k % 2:
                            act.wait_ge(x_turned, i * 4 + (KD * r + k + 1))
                            act.wait_ge(ulo_made, i * 4 + (KD * r + k + 1))
                            order.link(act.activation(u_f[k][:, :], ps[:, 4 + k, :], ACT.Identity,
                                                      scale=mod[:, bass.ds(i * 4 + (scale + k), 1)],
                                                      bias=mod[:, bass.ds(i * 4 + (shift + k), 1)]))
                        else:
                            act.wait_ge(uf_made, i * 2 + (KD // 2 * r + k // 2 + 1))
                        act.activation(u_hi[:, i * 4 + k, :], u_f[k][:, :], ACT.Copy).then_inc(uhi_made, 1)
                    order.end(KD // 4)

            def hi(s, loaded, used, count):
                act.wait_ge(slab_in[s], loaded)
                act.wait_ge(used, count)
                act.activation(w_hi[s % 2][:, :, :], raw[s][:, :, :], ACT.Copy).then_inc(hi_made, 1)

            def chunk(j, loaded, loaded_next):
                hi(1, loaded, tile_done, 1 + j * 4)
                hi(2, loaded, slab_used, j * 3 + 1)
                hi(3, loaded, slab_used, j * 3 + 2)
                if loaded_next is not None:
                    hi(0, loaded_next, slab_used, j * 3 + 3)

            def paired(j):
                chunk(j, j * 32 + 16 * (ADA_FIRST + 1), j * 32 + 16 * (ADA_FIRST + 3))

            root(1, NT)
            split_u(0, SC1, SH1)
            act.wait_ge(x_turned, KD)
            act.dma_start(g_raw[:, :, :], win_v[:, :, GATE_COL:GATE_COL + 16]).then_inc(small_in, 16)
            act.wait_ge(small_in, 96)
            act.wait_ge(gates_zero, 1)
            for g in range(4):
                act.activation(g_hi[:, :, 32 * g:32 * g + HEADS], g_raw[:, :, HEADS * g:HEADS * (g + 1)], ACT.Copy
                               ).then_inc(gates_hi, 1)
            act.wait_ge(slab_in[0], 16 * (ADA_FIRST + 1))
            act.activation(w_hi[0][:, :, :], raw[0][:, :, :], ACT.Copy).then_inc(hi_made, 1)
            act.wait_ge(gate_step, 1)
            order.link(act.activation(g_M[:, :, :], gate_t[:, 1::2, :], ACT.Abs))
            order.link(act.activation(g_M[:, :, :], g_M[:, :, :], ACT.Exp, scale=-1.0))
            act.activation(g_M[:, :, :], g_M[:, :, :], ACT.Ln, bias=1.0).then_inc(gate_act, 1)
            act.wait_ge(gate_step, 2)
            act.activation(g_b[:, :, :], g_b[:, :, :], ACT.Exp, scale=-1.0).then_inc(gate_act, 1)
            with act.Fori(0, J_V, 1) as i:
                paired(i)
            act.wait_ge(cols_kept, 1)
            act.dma_start(v_bias[:, :], row(b_in, V_CH * CH, 2 * CH)).then_inc(rows_in, 16)
            with act.Fori(J_V, J_CONV, 1) as i:
                paired(i)
            for n in range(2 * HEADS):
                for st in range(NT):
                    act.wait_ge(e_asked, NT * n + st + 1)
                    lo_c, hi_c = (st * P, T) if n % 2 == 0 else (0, (st + 1) * P)
                    act.activation(prob[n % 2][:, st, lo_c:hi_c], prob[n % 2][:, st, lo_c:hi_c], ACT.Exp, scale=-1.0
                                   ).then_inc(e_made, 1)
            root(2, 4 * NT)
            with act.Fori(0, 2, 1) as i:
                for r in range(3):
                    paired(i * 3 + (J_CONV + r))
                for m in range(MT):
                    act.wait_ge(conv_done, i * MT + (m + 1))
                    act.activation(yc_hi[:, i * MT + m, :], conv_h[:, m, :], ACT.Copy).then_inc(yhi_made, 1)
            act.wait_ge(ylo_made, 12)
            act.dma_start(o_bias[:, :], row(b_in, O_CH * CH, 2 * CH)).then_inc(rows_in, 16)
            act.dma_start(norm_row[:, :], row(mlstm_norm_w, 0, HEADS * DV)).then_inc(norm_in, 16)
            with act.Fori(0, 2, 1) as i:
                paired(i + J_O)
                for t in range(NT):
                    act.wait_ge(o_added, i * NT + (t + 1))
                    act.activation(o_sig[:, t, :], o_sig[:, t, :], ACT.Sigmoid).then_inc(o_sigd, 1)
            for k in range(8):
                act.wait_ge(y_turned, k + 1)
                act.activation(u_hi[:, k, :], ps[:, 4 + k % 4, :], ACT.Copy).then_inc(ym_hi, 1)
            act.dma_start(ln1w_row[:, :], row(ln1_w, 0, D)).then_inc(rows_in, 16)
            act.dma_start(ln1b_row[:, :], row(ln1_b, 0, D)).then_inc(rows_in, 16)
            for n in range(NT):
                act.dma_start(xz[:, n, :], x_v[:, n, :]).then_inc(x_in, 16)
            with act.Fori(0, 3, 1) as i:
                paired(i + J_OUT)
            first_wq = 16 * (ADA_FIRST + 2 * J_WQ + 1)
            chunk(J_WQ - 1, first_wq - 32, first_wq)
            act.wait_ge(tile_done, 1 + 4 * J_WQ)
            act.dma_start(sk_raw[:, :, :], peer_subkeys[0].rearrange("h s n k -> n (h s) k")).then_inc(small_in, 16)
            root(3, NT)
            for n in range(NT):
                act.wait_ge(x1_made, n + 1)
                act.dma_start(x1_v[:, n, :], xz[:, n, :]).then_inc(x1_out, 16)
            root(4, NT)
            split_u(1, SC2, SH2)
            with act.Fori(0, 3, 1) as i:
                chunk(i + J_WQ, i * 16 + first_wq, i * 16 + (first_wq + 16))
            chunk(NC - 1, first_wq + 48, None)

            def turn_hi(i, par):
                for h in range(2):
                    act.wait_ge(u_turned, i * 2 + (h + 1))
                    act.activation(w_hi[par][:, 2 * h:2 * h + 2, :], ps[:, 2 * h:2 * h + 2, :], ACT.Copy
                                   ).then_inc(eu_hi, 1)

            def gelu(i, par):
                act.wait_ge(u_done, i + 1)
                act.activation(h_stage[:, :], ps[:, 4 + par, :], ACT.Gelu).then_inc(h_made, 1)

            def stored(i):
                act.wait_ge(h_out, i * 16 + 16)

            act.wait_ge(tile_done, 1 + 4 * NC)
            turn_hi(0, 0)
            turn_hi(1, 1)
            act.sem_inc(gexp_made, 1)
            with act.Fori(0, NT, 1) as r:
                for h in range(PH):
                    gelu(r * 8 + h, h % 2)
                    act.wait_ge(gexp_asked, r * 8 + (h + 1))
                    act.activation(g_exp[:, h, :], best_s[:, :], ACT.Exp, bias=neg_max[:, h:h + 1],
                                   accum_out=g_sum[:, h:h + 1]).then_inc(gexp_made, 1)
                    turn_hi(r * 8 + (h + 2), h % 2)
                    stored(r * 8 + h)

            act.sem_inc(batch_out, 1)

            def keep_gates(b, step):
                act.wait_ge(g_done, b * 8 + (step + 3))
                if step == 0:
                    act.wait_ge(batch_out, b + 1)
                for h in range(2):
                    t0 = G_TOK * step + 4 * h
                    act.activation(gates_sb[:, :, t0:t0 + 4].rearrange("p a t -> p t a"),
                                   ps[:, 6 + h, :].rearrange("p (t a) -> p t a", t=4), ACT.Copy).then_inc(g_kept, 1)

            with act.Fori(0, T // G_BATCH, 1) as b:
                for n in range(8):
                    step = sum(STEPS_MUL[:n])
                    if STEPS_MUL[n] == 2:
                        keep_gates(b, step)
                    gelu(b * 8 + (32 + n), n % 2)
                    if STEPS_MUL[n]:
                        keep_gates(b, step + STEPS_MUL[n] - 1)
                    turn_hi(b * 8 + (34 + n), n % 2)
                    stored(b * 8 + (32 + n))
            with act.Fori(0, 15, 1) as r:
                for n in range(2):
                    gelu(r * 2 + (96 + n), n)
                    turn_hi(r * 2 + (98 + n), n)
                    stored(r * 2 + (96 + n))
            gelu(ET - 2, 0)
            stored(ET - 2)

            def v_hi(s, loaded, done):
                act.wait_ge(slab_in[s], loaded)
                if done is not None:
                    act.wait_ge(v_done, 1 + done)
                act.activation(w_hi[s % 2][:, :, :], raw[s][:, :, :], ACT.Copy).then_inc(hi_made, 1)

            def a_split(b, par, done):
                act.wait_ge(a_mul, b + 1)
                if done is not None:
                    act.wait_ge(v_done, 1 + done)
                act.activation(a_hi[par][:, :, :], h_in[par][:, :, :], ACT.Copy).then_inc(ahi_made, 1)

            def v_block(b, par, last):
                for dc in range(SLABS):
                    if dc < 3:
                        v_hi(dc + 1, b * 16 + 16 * 77, b * 16 + 4 * dc)
                    elif not last:
                        v_hi(0, b * 16 + 16 * 78, b * 16 + 12)
                    if dc == 1 and not last:
                        a_split(b + 1, 1 - par, b * 16)

            v_hi(0, 16 * 77, None)
            act.wait_ge(u_done, ET)
            a_split(0, 0, None)
            gelu(ET - 1, 1)
            act.dma_start(x1[:, :, :], x1_v).then_inc(x1_back, 16)
            with act.Fori(0, NB // 2 - 1, 1) as r:
                v_block(r * 2, 0, False)
                v_block(r * 2 + 1, 1, False)
            v_block(NB - 2, 0, False)
            act.wait_ge(alo_made, NB - 1)
            act.dma_start(ln2w_row[:, :], row(ln2_w, 0, D)).then_inc(rows_in, 16)
            act.dma_start(ln2b_row[:, :], row(ln2_b, 0, D)).then_inc(rows_in, 16)
            v_block(NB - 1, 1, True)
            root(5, NT)

        @block.vector
        def _(dve):
            order = Tally(dve, dve_order)
            dve.sem_inc(bank_free, 4)
            dve.sem_inc(v_free, 8)
            for counted_from_one in (ada_kept, pick_kept):
                dve.sem_inc(counted_from_one, 1)
            dve.sem_inc(ulo_made, 4)
            dve.sem_inc(ylo_made, 4)

            def root(n, width):
                order.settle()
                dve.tensor_scalar(rstd[:, 0:width], mv[:, 0:width, 1], LN_EPS, None, ALU.add).then_inc(sqrt_asked, 1)
                dve.wait_ge(sqrt_made, n)
                order.link(dve.reciprocal(rstd[:, 0:width], rstd[:, 0:width]))

            def row_stats(n):
                for q in range(4):
                    order.mark(dve.bn_stats(stat[:, n, q, :], xz[:, n, q * CH:(q + 1) * CH]))
                order.settle()
                order.mark(dve.bn_aggr(mv[:, n, :], stat[:, n, :, :]))

            def normal(n):
                return dve.tensor_scalar(xz[:, n, :], xz[:, n, :], mv[:, n, 0:1], rstd[:, n:n + 1],
                                         ALU.subtract, ALU.mult)

            def affine(z, w_row, b_row, made):
                for n in range(NT):
                    order.mark(dve.scalar_tensor_tensor(z[:, n, :], z[:, n, :], mv[:, n, 0:1], w_row[:, :],
                                                        ALU.subtract, ALU.mult))
                    order.settle()
                    dve.scalar_tensor_tensor(z[:, n, :], z[:, n, :], rstd[:, n:n + 1], b_row[:, :],
                                             ALU.mult, ALU.add).then_inc(made, 1)

            def split_u(r, scale, shift):
                with dve.Fori(0, KD // 4, 1) as i:
                    for k in (0, 2):
                        dve.wait_ge(x_turned, i * 4 + (KD * r + k + 1))
                        if k == 0:
                            dve.wait_ge(ulo_made, i * 4 + (KD * r + 4))
                        dve.tensor_scalar(u_f[k][:, :], ps[:, 4 + k, :], mod[:, bass.ds(i * 4 + (scale + k), 1)],
                                          mod[:, bass.ds(i * 4 + (shift + k), 1)], ALU.mult, ALU.add
                                          ).then_inc(uf_made, 1)
                    for k in range(4):
                        dve.wait_ge(uhi_made, i * 4 + (KD * r + k + 1))
                        dve.tensor_tensor(u_lo[:, i * 4 + k, :], u_f[k][:, :], u_hi[:, i * 4 + k, :].bitcast(F32),
                                          ALU.subtract).then_inc(ulo_made, 1)

            def lo(s, n):
                dve.wait_ge(hi_made, n)
                dve.tensor_tensor(w_lo[s % 2][:, :, :], raw[s][:, :, :], w_hi[s % 2][:, :, :].bitcast(F32),
                                  ALU.subtract).then_inc(lo_made, 1)

            def ada_chunk(a, loaded, acc, reduced):
                if reduced is not None:
                    dve.wait_ge(ada_reduced, reduced)
                for s in range(SLABS):
                    dve.wait_ge(slab_in[s], loaded)
                    if s:
                        dve.wait_ge(ada_read, a * 4 + s)
                    for k in range(4):
                        w, m = raw[s][:, k, :], cond[:, 4 * s + k:4 * s + k + 1]
                        if s == 0:
                            ins = dve.tensor_scalar(acc[:, k, :], w, m, None, ALU.mult)
                        else:
                            ins = dve.scalar_tensor_tensor(acc[:, k, :], w, m, acc[:, k, :],
                                                           ALU.mult, ALU.add)
                    ins.then_inc(ada_read, 1)

            def ada_keep(a):
                dve.wait_ge(ada_reduced, a + 1)
                dve.tensor_tensor(mod[:, bass.ds(a * 4, 4)], ps[:, 6, 0:4], b_ada_c[:, bass.ds(a * 4, 4)],
                                  ALU.add).then_inc(ada_kept, 1)

            def chunk(j, read_bank, prepare=None):
                for s in range(1, SLABS):
                    lo(s, j * 4 + (s + 1))
                ada_chunk(j + ADA_FIRST, j * 32 + 16 * (ADA_FIRST + 2), ada_acc[0], j + ADA_FIRST)
                if prepare:
                    prepare()
                lo(0, j * 4 + 5)
                for m in range(MT):
                    dve.wait_ge(tile_done, 1 + j * 4 + (m + 1))
                    read_bank(m)
                ada_keep(j + ADA_FIRST)

            dve.wait_ge(silu_made, 1)
            dve.tensor_tensor(c_sig[:, :], c_rows[:, :], c_sig[:, :], ALU.mult).then_inc(cond_ready, 1)
            dve.wait_ge(first_turned, 1)
            order.mark(dve.tensor_copy(cond[:, :], ps[:, 7, 0:KD]))
            order.mark(dve.tensor_copy(b_ada_c[:, :], ps[:, 7, 128:128 + 6 * KD]))
            order.mark(dve.tensor_copy(vec_c[:, :], ps[:, 7, 256:256 + 64]))
            order.settle()
            ada_chunk(0, 16, ada_acc[0], None)
            dve.wait_ge(x_in, 16 * NT)
            for n in range(NT):
                row_stats(n)
            root(1, NT)
            for n in range(NT):
                normal(n).then_inc(x_normal, 1)
            ada_chunk(1, 32, ada_acc[1], None)
            ada_keep(0)
            with dve.Fori(1, ADA_FIRST // 2, 1) as i:
                for k in range(2):
                    ada_chunk(i * 2 + k, i * 32 + 16 * (k + 1), ada_acc[k], i * 2 + (k - 1))
                    ada_keep(i * 2 + (k - 1))
            ada_keep(ADA_FIRST - 1)
            dve.wait_ge(ada_kept, 1 + ADA_FIRST)
            order.link(dve.tensor_scalar(mod[:, SC1:SC1 + KD], mod[:, SC1:SC1 + KD], 1.0, None, ALU.add))
            dve.sem_inc(mod_ready, 1)
            split_u(0, SC1, SH1)
            dve.wait_ge(ulo_made, 4 + KD)
            order.mark(dve.memset(g_hi[:, :, :].bitcast(F32), 0.0))
            order.mark(dve.memset(g_lo[:, :, :].bitcast(F32), 0.0))
            order.mark(dve.memset(v_aug[:, :, :, DV:DV + 2], 1.0))
            order.settle()
            dve.sem_inc(gates_zero, 1)
            for g in range(4):
                dve.wait_ge(gates_hi, g + 1)
                dve.tensor_tensor(g_lo[:, :, 32 * g:32 * g + HEADS], g_raw[:, :, HEADS * g:HEADS * (g + 1)],
                                  g_hi[:, :, 32 * g:32 * g + HEADS].bitcast(F32), ALU.subtract).then_inc(gates_lo, 1)
            lo(0, 1)
            dve.wait_ge(gates_proj, 1)
            dve.wait_ge(gate_b_in, 64)
            for g in range(4):
                order.mark(dve.tensor_scalar(gate_t[:, g, :], ps[32 * g:32 * g + HEADS, 7, :],
                                             gate_b[32 * g:32 * g + HEADS, :], None, ALU.add))
            order.settle()
            dve.sem_inc(gate_step, 1)
            dve.wait_ge(gate_act, 1)
            f, i_g = gate_t[:, 1::2, :], gate_t[:, 0::2, :]
            order.link(dve.scalar_tensor_tensor(f, f, 0.0, g_M[:, :, :], ALU.min, ALU.subtract))
            f0, f1 = gate_t[:, 1, :], gate_t[:, 3, :]
            order.mark(dve.tensor_tensor_scan(g_b[:, 0, :], f0, f0, 0.0, ALU.add, ALU.min))
            order.mark(dve.tensor_tensor_scan(g_b[:, 1, ::-1], f1[:, ::-1], f1[:, ::-1], 0.0, ALU.add, ALU.min))
            order.settle()
            order.link(dve.tensor_tensor(i_g, i_g, g_b[:, :, :], ALU.subtract))
            a0, a1 = gate_t[:, 0, :], gate_t[:, 2, :]
            order.mark(dve.tensor_tensor_scan(g_M[:, 0, :], a0, a0, 0.0, ALU.max, ALU.max))
            order.mark(dve.tensor_tensor_scan(g_M[:, 1, ::-1], a1[:, ::-1], a1[:, ::-1], 0.0, ALU.max, ALU.max))
            order.settle()
            dve.tensor_tensor(g_b[:, :, :], g_b[:, :, :], g_M[:, :, :], ALU.add).then_inc(gate_step, 1)

            with dve.Fori(0, 2, 1) as i:
                def keep_qk(m):
                    dve.tensor_scalar(qk[:, i, m, :], ps[:, m, :], vec_c[:, bass.ds(i * MT + (Q_CH * MT + m), 1)],
                                      None, ALU.add).then_inc(bank_free, 1)
                chunk(i, keep_qk)
            dve.wait_ge(gates_turned, 1)
            order.mark(dve.tensor_copy(a_col[:, :, :, :].rearrange("p d t h -> p (d t h)"), ps[:, 7, 0:32]))
            order.mark(dve.tensor_copy(em_col[:, :, :, :].rearrange("p d t h -> p (d t h)"), ps[:, 7, 32:64]))
            order.settle()
            dve.sem_inc(cols_kept, 1)
            dve.wait_ge(rows_in, 16)
            with dve.Fori(0, 2, 1) as i:
                def keep_v(t):
                    dve.tensor_tensor(v_aug[:, t, bass.ds(i * 2, 2), 0:DV],
                                      ps[:, t, :].rearrange("p (h v) -> p h v", h=2),
                                      v_bias[:, bass.ds(i * CH, CH)].rearrange("p (h v) -> p h v", h=2),
                                      ALU.add).then_inc(bank_free, 1)
                chunk(i + J_V, keep_v)
            dve.wait_ge(bank_free, 4 * J_CONV + 4)

            def live(d, st):
                return slice(st * P, T) if d == 0 else slice(0, (st + 1) * P)

            def exponents(n):
                h, d = n // 2, n % 2
                dve.wait_ge(m_made, h + 1)
                if n >= 2:
                    dve.wait_ge(hd_out, NT * (n - 1))
                for st in range(NT):
                    dve.tensor_scalar(prob[d][:, st, live(d, st)], ps[:, 4 + d, live(d, st)],
                                      a_col[:, d, st, h:h + 1], 0.0, ALU.subtract, ALU.max).then_inc(e_asked, 1)

            def weights(n):
                h, d = n // 2, n % 2
                for st in range(NT):
                    dve.wait_ge(e_made, NT * n + st + 1)
                    own = prob[d][:, st, st * P:(st + 1) * P]
                    order.mark(dve.tensor_tensor(own, own, (mask_fwd, mask_bwd)[d][:, :], ALU.mult))
                order.settle()
                for st in range(NT):
                    dve.wait_ge(s_made, NT * h + st + 1)
                    w = prob[d][:, st, live(d, st)]
                    dve.scalar_tensor_tensor(w, ps[:, st, live(d, st)], DK ** -0.5, w, ALU.mult, ALU.mult
                                             ).then_inc(p_made, 1)

            def outputs(n):
                h, d = n // 2, n % 2
                for k, t in enumerate(reversed(range(NT)) if d == 0 else range(NT)):
                    b = 6 + k % 2
                    dve.wait_ge(hd_out, NT * n + k + 1)
                    order.link(dve.tensor_scalar(den[:, k % 2, 0:1], ps[:, b, DV:DV + 1], -1.0,
                                                 em_col[:, d, t, h:h + 1], ALU.mult, ALU.max))
                    order.link(dve.tensor_tensor(den[:, k % 2, 0:1], ps[:, b, DV:DV + 1], den[:, k % 2, 0:1],
                                                 ALU.max))
                    order.link(dve.reciprocal(den[:, k % 2, 1:2], den[:, k % 2, 0:1]))
                    if d == 0:
                        dve.tensor_scalar(h_sum[:, t, h, :], ps[:, b, 0:DV], den[:, k % 2, 1:2], None, ALU.mult
                                          ).then_inc(hd_kept, 1)
                    else:
                        dve.scalar_tensor_tensor(h_sum[:, t, h, :], ps[:, b, 0:DV], den[:, k % 2, 1:2],
                                                 h_sum[:, t, h, :], ALU.mult, ALU.add).then_inc(hd_kept, 1)

            exponents(0)
            exponents(1)
            weights(0)
            for h in range(HEADS):
                weights(2 * h + 1)
                outputs(2 * h)
                if h < HEADS - 1:
                    exponents(2 * h + 2)
                outputs(2 * h + 1)
                if h < HEADS - 1:
                    weights(2 * h + 2)
                    exponents(2 * h + 3)
            dve.wait_ge(hd_kept, 8 * NT)
            for t in range(NT):
                for h in range(HEADS):
                    order.mark(dve.bn_stats(stat[:, t, h, :], h_sum[:, t, h, :]))
            order.settle()
            for t in range(NT):
                for h in range(HEADS):
                    order.mark(dve.bn_aggr(mv[:, 4 * t + h, :], stat[:, t, h, :]))
            root(2, 4 * NT)
            order.mark(dve.memset(conv_c[:, :, 0:1], 0.0))
            order.mark(dve.memset(conv_c[:, :, T + 1:T + 2], 0.0))
            order.settle()

            with dve.Fori(0, 2, 1) as i:
                order.loop(i, 3 * MT)

                def col(first, m):
                    return vec_c[:, bass.ds(i * MT + (first + m), 1)]

                def keep_h(m):
                    dve.wait_ge(ylo_made, i * MT + MT)
                    dve.tensor_scalar(conv_h[:, m, :], ps[:, m, :], col(HIN_CH * MT, m), None, ALU.add
                                      ).then_inc(bank_free, 1)

                def keep_c(m):
                    dve.scalar_tensor_tensor(conv_c[:, m, 1:T + 1], ps[:, m, :], col(GC_CH * MT, m),
                                             conv_h[:, m, :], ALU.add, ALU.mult).then_inc(bank_free, 1)

                def taps():
                    for k in range(3):
                        for m in range(MT):
                            src = conv_c[:, m, k:k + T]
                            if k == 0:
                                order.mark(dve.tensor_scalar(conv_h[:, m, :], src, col(CONV_W, m), col(CONV_B, m),
                                                             ALU.mult, ALU.add))
                            else:
                                order.mark(dve.scalar_tensor_tensor(conv_h[:, m, :], src, col(CONV_W + 8 * k, m),
                                                                    conv_h[:, m, :], ALU.mult, ALU.add))
                        order.settle()

                def keep_y(m):
                    dve.scalar_tensor_tensor(conv_h[:, m, :], ps[:, m, :], col(GB_CH * MT, m), conv_h[:, m, :],
                                             ALU.add, ALU.mult).then_inc(conv_done, 1)

                chunk(i * 3 + J_CONV, keep_h)
                dve.wait_ge(bank_free, i * 12 + (4 * J_CONV + 4 + 4))
                chunk(i * 3 + (J_CONV + 1), keep_c)
                dve.wait_ge(bank_free, i * 12 + (4 * J_CONV + 8 + 4))
                chunk(i * 3 + (J_CONV + 2), keep_y, taps)
                dve.wait_ge(conv_done, i * MT + MT)
                dve.sem_inc(bank_free, 4)
                order.end(2)

            dve.wait_ge(rows_in, 32)
            dve.wait_ge(ylo_made, 12)
            dve.wait_ge(norm_in, 16)
            with dve.Fori(0, 2, 1) as i:
                order.loop(i, 2 * NT)

                def head(t, h):
                    return (h_sum[:, t, bass.ds(i * 2 + h, 1), :].rearrange("p h v -> p (h v)"),
                            bass.ds(i * 2 + (4 * t + h), 1))

                def centre():
                    for t in range(NT):
                        for h in range(2):
                            hs, q = head(t, h)
                            order.mark(dve.scalar_tensor_tensor(hs, hs, mv[:, q, 0:1].rearrange("p a b -> p (a b)"),
                                                                norm_row[:, bass.ds(i * 2 * DV + h * DV, DV)],
                                                                ALU.subtract, ALU.mult))

                def keep_o(t):
                    dve.tensor_tensor(o_sig[:, t, :], ps[:, t, :], o_bias[:, bass.ds(i * CH, CH)], ALU.add
                                      ).then_inc(o_added, 1)
                chunk(i + J_O, keep_o, centre)
                order.settle()
                dve.wait_ge(o_added, i * NT + NT)
                dve.sem_inc(bank_free, 4)
                for t in range(NT):
                    dve.wait_ge(o_sigd, i * NT + (t + 1))
                    for h in range(2):
                        hs, q = head(t, h)
                        dve.scalar_tensor_tensor(hs, hs, rstd[:, q], o_sig[:, t, h * DV:(h + 1) * DV],
                                                 ALU.mult, ALU.mult).then_inc(y_gated, 1)
                order.end(2)
            for k in range(8):
                dve.wait_ge(ym_hi, k + 1)
                dve.tensor_tensor(u_lo[:, k, :], ps[:, 4 + k % 4, :], u_hi[:, k, :].bitcast(F32), ALU.subtract
                                  ).then_inc(ym_lo, 1)

            def spread_diag(col, tiles, q):
                w = len(tiles)
                for m in range(w):
                    order.mark(dve.tensor_scalar(tiles[m], ident[:, :], mod[:, bass.ds(q * w + (col + m), 1)], None,
                                                 ALU.mult))
                order.settle()
                dve.sem_inc(diag_made, 1)

            def spread_keep(dst, w, q, made):
                dve.wait_ge(row_made, made)
                dve.tensor_copy(dst[:, bass.ds(q * (w * P), w * P)], ps[:, 7, 0:w * P]).then_inc(row_kept, 1)

            for q in range(4):
                spread_diag(G1, [diag[:, m, :] for m in range(4)], q)
                spread_keep(g1_row, 4, q, q + 1)
            dve.wait_ge(row_kept, 5)
            dve.wait_ge(x_in, 32 * NT)
            with dve.Fori(0, 4, 1) as i:
                order.loop(i, 2 * NT)

                def keep_z(t):
                    order.link(dve.tensor_tensor(ps[:, t, :], ps[:, t, :], g1_row[:, bass.ds(i * CH, CH)], ALU.mult))
                    z = xz[:, t, bass.ds(i * CH, CH)]
                    dve.scalar_tensor_tensor(z, z, alpha, ps[:, t, :], ALU.mult, ALU.add).then_inc(bank_free, 1)

                chunk(i + J_OUT, keep_z)
                dve.wait_ge(bank_free, i * 4 + (4 * J_OUT + 8))
                for t in range(NT):
                    order.mark(dve.bn_stats(stat[:, t, bass.ds(i, 1), :].rearrange("p a b -> p (a b)"),
                                            xz[:, t, bass.ds(i * CH, CH)]))
                order.settle()
                order.end(4)
            dve.wait_ge(bank_free, 4 * J_WQ + 4)
            dve.wait_ge(ada_reduced, ADA_ALL)
            for q in range(4):
                dve.wait_ge(sk_turned, q + 1)
                dve.tensor_copy(sk_t[:, 4 * q:4 * q + 4, :], ps[:, q, :].rearrange("p (a b) -> p a b", a=4)
                                ).then_inc(sk_kept, 1)
            for n in range(NT):
                order.mark(dve.bn_aggr(mv[:, n, :], stat[:, n, :, :]))
            root(3, NT)
            dve.wait_ge(rows_in, 64)
            affine(xz, ln1w_row, ln1b_row, x1_made)
            dve.wait_ge(x1_made, NT)
            for n in range(NT):
                row_stats(n)
            root(4, NT)
            dve.wait_ge(x1_out, 16 * NT)
            for n in range(NT):
                normal(n).then_inc(x_normal, 1)
            dve.wait_ge(ada_kept, 1 + ADA_ALL)
            order.link(dve.tensor_scalar(mod[:, SC2:SC2 + KD], mod[:, SC2:SC2 + KD], 1.0, None, ALU.add))
            dve.sem_inc(mod_ready, 1)
            split_u(1, SC2, SH2)
            dve.wait_ge(ulo_made, 4 + 2 * KD)

            def q_chunk(i, last):
                for s in range(1, SLABS):
                    lo(s, i * 4 + (4 * J_WQ + s + 1))
                if not last:
                    lo(0, i * 4 + (4 * J_WQ + 5))
                for m in range(MT):
                    dve.wait_ge(tile_done, 1 + i * 4 + (4 * J_WQ + m + 1))
                    dve.tensor_copy(q_t[:, i * MT + m, :], ps[:, m, :]).then_inc(bank_free, 1)

            with dve.Fori(0, 3, 1) as i:
                q_chunk(i, False)
            q_chunk(3, True)
            with dve.Fori(0, NT, 1) as t:
                for g in range(4):
                    dve.wait_ge(sc_made, t * 4 + (g + 1))
                    dve.tensor_copy(scores[:, t, 4 * g:4 * g + 4, :], ps[:, 4 + g, :].rearrange("p (a b) -> p a b", a=4)
                                    ).then_inc(sc_kept, 1)

            def turn_lo(i, par):
                for h in range(2):
                    dve.wait_ge(eu_hi, i * 2 + (h + 1))
                    dve.tensor_tensor(w_lo[par][:, 2 * h:2 * h + 2, :], ps[:, 2 * h:2 * h + 2, :],
                                      w_hi[par][:, 2 * h:2 * h + 2, :].bitcast(F32), ALU.subtract).then_inc(eu_lo, 1)

            def pick(t, h, meanwhile=None):
                dve.wait_ge(gexp_made, t * 8 + (h + 1))
                order.link(dve.tensor_copy(ws[:, :, :], scores[:, t, 2 * h:2 * h + 2, :]))
                dve.sem_inc(paced, 1)
                for half, src in ((0, ws), (8, ws2)):
                    for s in range(2):
                        order.mark(dve.max(top_s[:, s, half:half + 8], src[:, s, :]))
                    order.settle()
                    dve.sem_inc(paced, 1)
                    for s in range(2):
                        order.mark(dve.max_index(top_i[:, s, half:half + 8], top_s[:, s, half:half + 8], src[:, s, :]))
                    if half == 0:
                        for s in range(2):
                            order.mark(dve.match_replace(ws2[:, s, :], top_s[:, s, 0:8], ws[:, s, :], LOWEST))
                    order.settle()
                    dve.sem_inc(paced, 1)
                order.mark(dve.tensor_copy(top_f[:, :, :], top_i[:, :, :]))
                order.link(dve.tensor_tensor(cand[:, :, :], top_s[:, 0, :].unsqueeze(2).to_broadcast([P, TOPK, TOPK]),
                                             top_s[:, 1, :].unsqueeze(1).to_broadcast([P, TOPK, TOPK]), ALU.add))
                flat, flat2 = (v[:, :, :].rearrange("p a b -> p (a b)") for v in (cand, cand2))
                dve.sem_inc(paced, 1)
                order.link(dve.max(best_s[:, 0:8], flat))
                dve.sem_inc(paced, 1)
                order.mark(dve.max_index(best_c[:, 0:8], best_s[:, 0:8], flat))
                order.link(dve.match_replace(flat2, best_s[:, 0:8], flat, LOWEST))
                dve.sem_inc(paced, 1)
                order.link(dve.max(best_s[:, 8:16], flat2))
                dve.sem_inc(paced, 1)
                order.mark(dve.max_index(best_c[:, 8:16], best_s[:, 8:16], flat2))
                dve.tensor_scalar(neg_max[:, h:h + 1], best_s[:, 0:1], -1.0, None, ALU.mult).then_inc(gexp_asked, 1)
                order.settle()
                order.mark(dve.tensor_scalar(best_j[:, 0, :], best_c[:, :], 4, None, ALU.logical_shift_right))
                order.link(dve.tensor_scalar(best_j[:, 1, :], best_c[:, :], 15, None, ALU.bitwise_and))
                order.link(dve.tensor_copy(best_f[:, :, :], best_j[:, :, :]))
                for s in range(2):
                    order.mark(dve.tensor_tensor(hot[:, s, :, :], best_f[:, s, :].unsqueeze(2).to_broadcast([P, TOPK, TOPK]),
                                                 iota[:, 0:TOPK].unsqueeze(1).to_broadcast([P, TOPK, TOPK]),
                                                 ALU.is_equal))
                order.settle()
                for s in range(2):
                    order.mark(dve.tensor_tensor(hot[:, s, :, :], hot[:, s, :, :],
                                                 top_f[:, s, :].unsqueeze(1).to_broadcast([P, TOPK, TOPK]), ALU.mult))
                order.settle()
                if meanwhile:
                    meanwhile()
                for s in range(2):
                    order.mark(dve.tensor_reduce(picks[:, s, h, :], hot[:, s, :, :], AX_X, ALU.add))

            def spread_gates(b, step):
                tok = bass.ds(b * G_BATCH + step * G_TOK, G_TOK)
                i = step % 2
                shape = [P, G_TOK, NK]
                keys = iota[:, :].unsqueeze(1).to_broadcast(shape)
                dve.wait_ge(g_done, b * 8 + (step + 1))
                order.mark(dve.tensor_copy(gt_hr[:, i, :], by_pick[:, 2, tok]))
                order.mark(dve.tensor_tensor(hot1[i][:, :, :], by_pick[:, 0, tok].unsqueeze(2).to_broadcast(shape),
                                             keys, ALU.is_equal))
                order.link(dve.tensor_tensor(hot2[i][:, :, :], by_pick[:, 1, tok].unsqueeze(2).to_broadcast(shape),
                                             keys, ALU.is_equal))
                order.link(dve.tensor_tensor(gt_lo[:, i, :], by_pick[:, 2, tok], gt_hr[:, i, :].bitcast(F32), ALU.subtract))
                dve.tensor_tensor(hot2_hi[i][:, :, :], hot2[i][:, :, :],
                                  gt_hr[:, i, :].bitcast(F32).unsqueeze(2).to_broadcast(shape), ALU.mult
                                  ).then_inc(hot_made, 1)
                dve.tensor_tensor(hot2_lo[i][:, :, :], hot2[i][:, :, :], gt_lo[:, i, :].unsqueeze(2).to_broadcast(shape),
                                  ALU.mult).then_inc(hot_made, 1)

            turn_lo(0, 0)
            def keep_picks(r):
                dve.wait_ge(pick_turned, r + 1)
                order.link(dve.tensor_copy(by_pick[:, :, bass.ds(r * P, P)],
                                           ps[:, 6, 0:3 * P].rearrange("p (c t) -> p c t", c=3)))
                dve.sem_inc(pick_kept, 1)

            def pick_tile(r, meanwhile=None):
                for h in range(PH):
                    turn_lo(r * 8 + (h + 1), (h + 1) % 2)
                    pick(r, h, meanwhile if h == 0 else None)
                dve.wait_ge(gexp_made, r * 8 + (PH + 1))
                order.link(dve.reciprocal(g_inv[:, :], g_sum[:, :]))
                order.mark(dve.tensor_tensor(picks[:, 2, :, :], g_exp[:, :, :],
                                             g_inv[:, :].unsqueeze(2).to_broadcast([P, PH, TOPK]), ALU.mult))
                order.settle()
                dve.sem_inc(picked, 1)

            pick_tile(0)
            with dve.Fori(0, NT - 1, 1) as r:
                order.loop(r, PH * 27 + 3)
                pick_tile(r + 1, lambda: keep_picks(r))
                order.end(NT - 1)
            keep_picks(NT - 1)
            with dve.Fori(0, T // G_BATCH, 1) as b:
                order.loop(b, 8 * 4)
                for n in range(8):
                    turn_lo(b * 8 + (33 + n), (n + 1) % 2)
                    for step in range(sum(STEPS_HOT[:n]), sum(STEPS_HOT[:n + 1])):
                        spread_gates(b, step)
                order.end(T // G_BATCH)
            dve.wait_ge(g_done, 2 + T // G_TOK)
            def spread_g2(q):
                spread_diag(G2, [mask_fwd[:, :], mask_bwd[:, :]], q)

            with dve.Fori(0, 7, 1) as r:
                order.loop(r, 2)
                for n in range(4):
                    turn_lo(r * 4 + (97 + n), (n + 1) % 2)
                    if n == 0:
                        spread_g2(r)
                    if n == 1:
                        spread_keep(g2_row, 2, r, r + 5)
                order.end(7)
            turn_lo(ET - 3, 1)
            spread_g2(7)
            turn_lo(ET - 2, 0)
            spread_keep(g2_row, 2, 7, 12)
            turn_lo(ET - 1, 1)

            def gated(b, par):
                dve.wait_ge(hg_in[par], (b >> 1) * 32 + 32 if isinstance(b, int) else b * 16 + 32 - 16 * par)
                dve.tensor_tensor(h_in[par][:, :, :], h_in[par][:, :, :], g_in[par][:, :, :], ALU.mult
                                  ).then_inc(a_mul, 1)

            def gated_lo(b, par):
                dve.wait_ge(ahi_made, b + 1)
                dve.tensor_tensor(a_lo[par][:, :, :], h_in[par][:, :, :], a_hi[par][:, :, :].bitcast(F32),
                                  ALU.subtract).then_inc(alo_made, 1)

            def v_block(b, par, last):
                for dc in range(SLABS):
                    if dc < 3 or not last:
                        lo((dc + 1) % 4, b * 4 + (4 * NC + dc + 2))
                    if dc == 0 and not last:
                        gated(b + 1, 1 - par)
                    if dc == 1 and not last:
                        gated_lo(b + 1, 1 - par)
                    for t in range(NT):
                        dve.wait_ge(v_done, 1 + b * 16 + (4 * dc + t + 1))
                        y = y_acc[:, t, dc * CH:(dc + 1) * CH]
                        dve.tensor_tensor(y, y, ps[:, (4 * dc + t) % 8, :], ALU.add).then_inc(v_free, 1)

            gated(0, 0)
            lo(0, 4 * NC + 1)
            gated_lo(0, 0)
            dve.wait_ge(y_zero, 1)
            with dve.Fori(0, NB // 2 - 1, 1) as r:
                v_block(r * 2, 0, False)
                v_block(r * 2 + 1, 1, False)
            v_block(NB - 2, 0, False)
            dve.wait_ge(x1_back, 16)
            dve.wait_ge(row_kept, 13)
            for dc in range(SLABS):
                if dc < 3:
                    lo(dc + 1, 4 * NC + 4 * (NB - 1) + dc + 2)
                cols = slice(dc * CH, (dc + 1) * CH)
                for t in range(NT):
                    dve.wait_ge(v_done, 16 * (NB - 1) + 4 * dc + t + 2)
                    dve.tensor_tensor(y_acc[:, t, cols], y_acc[:, t, cols], ps[:, (4 * dc + t) % 8, :], ALU.add
                                      ).then_inc(v_free, 1)
                dve.wait_ge(v_free, 8 + 16 * (NB - 1) + 4 * dc + NT)
                for t in range(NT):
                    order.mark(dve.tensor_tensor(y_acc[:, t, cols], y_acc[:, t, cols], g2_row[:, cols], ALU.mult))
                order.settle()
                for t in range(NT):
                    order.mark(dve.scalar_tensor_tensor(x1[:, t, cols], x1[:, t, cols], alpha, y_acc[:, t, cols],
                                                        ALU.mult, ALU.add))
                order.settle()
                for t in range(NT):
                    order.mark(dve.bn_stats(stat[:, t, dc, :], x1[:, t, cols]))
            order.settle()
            for n in range(NT):
                order.mark(dve.bn_aggr(mv[:, n, :], stat[:, n, :, :]))
            root(5, NT)
            dve.wait_ge(rows_in, 96)
            affine(x1, ln2w_row, ln2b_row, out_made)

        @block.tensor
        def _(pe):
            for counted_from_one in (tile_done, v_done, row_kept):
                pe.sem_inc(counted_from_one, 1)
            pe.sem_inc(g_done, 2)
            def ada_reduce(a, acc=ada_acc[0]):
                pe.wait_ge(ada_added, a + 1)
                pe.wait_ge(ada_kept, 1 + a)
                for m in range(4):
                    mm = pe.matmul(ps[:, 6, m:m + 1], acc[:, 0, m * P:(m + 1) * P], ones[:, 0:1],
                                   start=True, stop=True)
                mm.then_inc(ada_reduced, 1)

            def turn_x(r):
                pe.wait_ge(x_normal, NT * (r + 1))
                pe.wait_ge(ada_kept, 1 + (ADA_FIRST if r == 0 else ADA_ALL))
                for k in range(KD):
                    if k >= 4:
                        pe.wait_ge(uhi_made, KD * r + k - 3)
                        if k % 2 == 0:
                            pe.wait_ge(uf_made, KD // 2 * r + k // 2 - 1)
                    for n in range(NT):
                        mm = pe.transpose(ps[:, 4 + k % 4, n * P:(n + 1) * P], xz[:, n, k * P:(k + 1) * P],
                                          ident[:, :])
                    mm.then_inc(x_turned, 1)

            def three(bank, stat_hi, stat_lo, mov_hi, mov_lo, first, last):
                pe.matmul(bank, stat_hi, mov_hi, start=first, stop=False)
                pe.matmul(bank, stat_hi, mov_lo, start=False, stop=False)
                return pe.matmul(bank, stat_lo, mov_hi, start=False, stop=last)

            def u_tile(k):
                return u_hi[:, k, :], u_lo[:, k, :]

            def y_tile(k):
                if k < 8:
                    return yc_hi[:, k, :], yc_lo[:, k, :]
                return u_hi[:, k - 8, :], u_lo[:, k - 8, :]

            def chunk(j, feature_major, tile=u_tile):
                for s in range(SLABS):
                    pe.wait_ge(lo_made, j * 4 + (s + 1))
                    wh, wl = w_hi[s % 2], w_lo[s % 2]
                    for m in range(MT):
                        if s == 0:
                            pe.wait_ge(bank_free, j * 4 + (m + 1))
                        own = slice(m * P, (m + 1) * P)
                        for k in range(4):
                            uh, ul = tile(4 * s + k)
                            first, last = s == 0 and k == 0, s == 3 and k == 3
                            if feature_major:
                                mm = three(ps[:, m, :], wh[:, k, own], wl[:, k, own], uh, ul, first, last)
                            else:
                                mm = three(ps[:, m, :], uh[:, own], ul[:, own], wh[:, k, :], wl[:, k, :], first, last)
                        if s == 3:
                            mm.then_inc(tile_done, 1)
                    if s < 3:
                        mm.then_inc(slab_used, 1)

            pe.wait_ge(const_made, 1)
            pe.wait_ge(cond_ready, 1)
            pe.transpose(ps[:, 7, 0:KD], c_sig[:, :], ident[0:KD, 0:KD])
            pe.wait_ge(small_in, 80)
            pe.transpose(ps[:, 7, 128:128 + 6 * KD], ada_rows[:, :], ident[0:6 * KD, 0:6 * KD])
            pe.transpose(ps[:, 7, 256:256 + 64], vec_rows[:, :], ident[0:64, 0:64]).then_inc(first_turned, 1)
            with pe.Fori(0, ADA_FIRST // 2, 1) as i:
                for k in range(2):
                    ada_reduce(i * 2 + k, ada_acc[k])
            turn_x(0)
            pe.wait_ge(ulo_made, 4 + KD)
            pe.wait_ge(gates_lo, 4)
            for k in range(KD):
                mm = three(ps[:, 7, :], g_hi[:, k, :], g_lo[:, k, :], *u_tile(k), k == 0, k == KD - 1)
            mm.then_inc(gates_proj, 1)
            with pe.Fori(0, 2, 1) as i:
                chunk(i, True)
                ada_reduce(i + ADA_FIRST)
            pe.wait_ge(gate_step, 2)
            pe.wait_ge(gate_act, 2)
            for d in range(2):
                for t in range(NT):
                    c0 = (d * NT + t) * HEADS
                    pe.transpose(ps[:, 7, c0:c0 + HEADS], gate_t[:, 2 * d, t * P:(t + 1) * P],
                                 ident[0:HEADS, 0:HEADS])
                    mm = pe.transpose(ps[:, 7, 32 + c0:32 + c0 + HEADS], g_b[:, d, t * P:(t + 1) * P],
                                      ident[0:HEADS, 0:HEADS])
            mm.then_inc(gates_turned, 1)
            with pe.Fori(0, 2, 1) as i:
                chunk(i + J_V, False)
                ada_reduce(i + (ADA_FIRST + J_V))
            pe.wait_ge(ada_kept, 1 + ADA_FIRST + J_CONV)
            pe.wait_ge(bank_free, 4 * J_CONV + 4)
            def head_inputs(h):
                if h:
                    pe.wait_ge(e_asked, 2 * NT * h)
                for d in range(2):
                    mm = pe.matmul(ps[:, 4 + d, :], sel[:, h, :], g_M[:, d, :], start=True, stop=True)
                mm.then_inc(m_made, 1)
                if h:
                    pe.wait_ge(p_made, 2 * NT * h)
                for st in range(NT):
                    pe.matmul(ps[:, st, :], qk[:, 1, h, st * P:(st + 1) * P], qk[:, 0, h, :], start=True, stop=True
                              ).then_inc(s_made, 1)

            def head_outputs(n):
                h, d = n // 2, n % 2
                pe.wait_ge(p_made, NT * (n + 1))
                for k, t in enumerate(reversed(range(NT)) if d == 0 else range(NT)):
                    if NT * n + k >= 2:
                        pe.wait_ge(hd_kept, NT * n + k - 1)
                    sts = list(range(t + 1)) if d == 0 else list(range(t, NT))
                    for st in sts:
                        mm = pe.matmul(ps[:, 6 + k % 2, 0:DV + 1], prob[d][:, st, t * P:(t + 1) * P],
                                       v_aug[:, st, h, 0:DV + 1], start=st == sts[0], stop=st == sts[-1])
                    mm.then_inc(hd_out, 1)

            head_inputs(0)
            for h in range(HEADS):
                head_outputs(2 * h)
                if h < HEADS - 1:
                    head_inputs(h + 1)
                head_outputs(2 * h + 1)
            pe.wait_ge(hd_kept, 8 * NT)
            with pe.Fori(0, 2, 1) as i:
                for r in range(3):
                    chunk(i * 3 + (J_CONV + r), True)
                    ada_reduce(i * 3 + (ADA_FIRST + J_CONV + r))
            with pe.Fori(0, 2, 1) as i:
                chunk(i + J_O, False)
                ada_reduce(i + (ADA_FIRST + J_O))
            pe.wait_ge(y_gated, 4 * NT)
            pe.wait_ge(ada_kept, 1 + ADA_FIRST + J_OUT)
            for k in range(8):
                if k >= 4:
                    pe.wait_ge(ym_lo, k - 3)
                for t in range(NT):
                    mm = pe.transpose(ps[:, 4 + k % 4, t * P:(t + 1) * P],
                                      h_sum[:, t, k // 2, (k % 2) * P:(k % 2 + 1) * P], ident[:, :])
                mm.then_inc(y_turned, 1)

            def spread(tiles, made):
                pe.wait_ge(diag_made, made)
                pe.wait_ge(row_kept, made)
                for m in range(len(tiles)):
                    mm = pe.matmul(ps[:, 7, m * P:(m + 1) * P], ones[:, :], tiles[m], start=True, stop=True)
                mm.then_inc(row_made, 1)

            pe.wait_ge(ym_lo, 8)
            for q in range(4):
                spread([diag[:, m, :] for m in range(4)], q + 1)
            pe.wait_ge(ylo_made, 12)
            with pe.Fori(0, 4, 1) as i:
                chunk(i + J_OUT, False, y_tile)
                ada_reduce(i + (ADA_FIRST + J_OUT))
            pe.wait_ge(bank_free, 4 * J_WQ + 4)
            pe.wait_ge(small_in, 112)
            for q in range(4):
                for m in range(4):
                    mm = pe.transpose(ps[:, q, m * P:(m + 1) * P], sk_raw[:, 4 * q + m, :], ident[:, :])
                mm.then_inc(sk_turned, 1)
            turn_x(1)
            pe.wait_ge(ulo_made, 4 + 2 * KD)
            pe.wait_ge(sk_kept, 4)
            with pe.Fori(0, 4, 1) as i:
                chunk(i + J_WQ, True)
            pe.wait_ge(bank_free, 4 * NC + 4)
            for t in range(NT):
                for g in range(4):
                    if t:
                        pe.wait_ge(sc_kept, 4 * (t - 1) + g + 1)
                    for m in range(4):
                        mm = pe.matmul(ps[:, 4 + g, m * P:(m + 1) * P], q_t[:, 4 * g + m, t * P:(t + 1) * P],
                                       sk_t[:, 4 * g + m, :], start=True, stop=True)
                    mm.then_inc(sc_made, 1)
            pe.wait_ge(sc_kept, 16)

            def turn_u(i, slot, loaded, read):
                pe.wait_ge(slab_in[slot], loaded)
                for h in range(2):
                    if read is not None:
                        pe.wait_ge(eu_lo, read + h)
                    for k in range(8 * h, 8 * h + 8):
                        own = slice((k % 4) * P, (k % 4 + 1) * P)
                        mm = pe.transpose(ps[:, k // 4, own], raw[slot][:, k // 4, own], ident[:, :])
                    mm.then_inc(u_turned, 1)

            def u_products(i, par, midway=None):
                pe.wait_ge(eu_lo, i * 2 + 2)
                for k in range(KD):
                    if k == KD // 2 and midway:
                        midway()
                    own = slice((k % 4) * P, (k % 4 + 1) * P)
                    mm = three(ps[:, 4 + par, :], w_hi[par][:, k // 4, own], w_lo[par][:, k // 4, own], *u_tile(k),
                               k == 0, k == KD - 1)
                mm.then_inc(u_done, 1)

            def u_step(i, n, loaded, midway=None):
                turn_u(i + 1, (n + 1) % 4, loaded, i * 2 + 1)
                u_products(i, n % 2, midway)

            def gate_step_products(b, step):
                pe.wait_ge(hot_made, b * 16 + (2 * step + 2))
                pe.wait_ge(g_kept, b * 16 + (2 * step + 1))
                for t in range(G_TOK):
                    bank = ps[:, 6 + t // 4, (t % 4) * P:(t % 4 + 1) * P]
                    pe.matmul(bank, hot2_hi[step % 2][:, t, :], hot1[step % 2][:, t, :], start=True, stop=False)
                    mm = pe.matmul(bank, hot2_lo[step % 2][:, t, :], hot1[step % 2][:, t, :], start=False, stop=True)
                mm.then_inc(g_done, 1)

            turn_u(0, 0, 16 * 45, None)
            def turn_picks(r):
                pe.wait_ge(picked, r + 1)
                pe.wait_ge(pick_kept, 1 + r)
                for c in range(3):
                    mm = pe.transpose(ps[:, 6, c * P:(c + 1) * P], picks[:, c, :, :].rearrange("p h k -> p (h k)"),
                                      ident[:, :])
                mm.then_inc(pick_turned, 1)

            for n in range(8):
                u_step(n, n, 16 * (45 + (n + 1) // 4))
            with pe.Fori(0, NT - 1, 1) as r:
                for n in range(8):
                    u_step(r * 8 + (8 + n), n, r * 32 + 16 * (47 + (n + 1) // 4),
                           (lambda: turn_picks(r)) if n == 0 else None)
            turn_picks(NT - 1)
            pe.wait_ge(pick_kept, 1 + NT)
            with pe.Fori(0, T // G_BATCH, 1) as b:
                for n in range(8):
                    step, steps = sum(STEPS_MUL[:n]), STEPS_MUL[n]
                    u_step(b * 8 + (32 + n), n, b * 32 + 16 * (53 + (n + 1) // 4),
                           (lambda: gate_step_products(b, step)) if steps == 2 else None)
                    if steps:
                        gate_step_products(b, step + steps - 1)
            pe.wait_ge(g_kept, 1 + 2 * T // G_TOK)

            def spread_g2(made):
                spread([mask_fwd[:, :], mask_bwd[:, :]], made)

            with pe.Fori(0, 7, 1) as r:
                for n in range(4):
                    u_step(r * 4 + (96 + n), n, r * 16 + 16 * (69 + (n + 1) // 4),
                           (lambda: spread_g2(r + 5)) if n == 1 else None)
            for n in range(3):
                u_step(124 + n, n, 16 * 76, (lambda: spread_g2(12)) if n == 1 else None)
            u_products(ET - 1, 1)

            def v_block(b, par):
                pe.wait_ge(alo_made, b + 1)
                for dc in range(SLABS):
                    pe.wait_ge(lo_made, b * 4 + (4 * NC + dc + 1))
                    for t in range(NT):
                        pe.wait_ge(v_free, b * 16 + (4 * dc + t + 1))
                        own = slice(t * P, (t + 1) * P)
                        for e in range(4):
                            mm = three(ps[:, (4 * dc + t) % 8, :], a_hi[par][:, e, own], a_lo[par][:, e, own],
                                       w_hi[dc % 2][:, e, :], w_lo[dc % 2][:, e, :], e == 0, e == 3)
                        mm.then_inc(v_done, 1)

            pe.wait_ge(h_made, ET)
            with pe.Fori(0, NB // 2, 1) as r:
                for i in range(2):
                    v_block(r * 2 + i, i)


_INS = ['x', 'c', 'w_ada', 'b_ada', 'w_in', 'b_in', 'conv_w', 'conv_b', 'mlstm_norm_w', 'w_out', 'ln1_w', 'ln1_b',
        'peer_wq', 'peer_subkeys', 'peer_u', 'peer_v', 'ln2_w', 'ln2_b']
_OUT = (1, T, D)


def kernel(**inputs):
    import concourse.bacc as _bacc
    from concourse.bass_utils import run_bass_kernel_spmd as _run

    nc = _bacc.Bacc("TRN2", target_bir_lowering=False, num_devices=1)
    arrays, args = {}, []
    for name in _INS:
        a = np.ascontiguousarray(inputs[name])
        arrays[f"in_{name}_dram"] = a
        args.append(nc.dram_tensor(f"in_{name}_dram", a.shape, mybir.dt.from_np(a.dtype), kind="ExternalInput").ap())
    args.append(nc.dram_tensor("out_dram", _OUT, F32, kind="ExternalOutput").ap())
    build_layer(nc, *args, alpha=2.0 ** 0.25)
    r = _run(nc, [arrays], core_ids=[0])
    return r.results[0]["out_dram"]
```

```python
from contextlib import ExitStack

import numpy as np

import concourse.bass as bass
from concourse import mybir

ALU = mybir.AluOpType
ACT = mybir.ActivationFunctionType
F32 = mybir.dt.float32
F32R = mybir.dt.float32r
U32 = mybir.dt.uint32
AX_X = mybir.AxisListType.X

P = 128
T = 512
NT = T // P
D = 2048
KD = D // P
CH = 512
MT = CH // P
SLABS = 4
HEADS, DK, DV = 4, 128, 256
GATE_COL = 6144
PH, TOPK, NK = 8, 16, 128
G_TOK = 4
G_SLOTS = 4
NE = NK * NK
ET = NE // P
LN_EPS = 1e-5
LOWEST = float(np.finfo(np.float32).min)

SH1, SC1, G1, SH2, SC2, G2 = (KD * i for i in range(6))
GB_CH, GC_CH, HIN_CH, Q_CH, V_CH, O_CH = 0, 2, 4, 6, 8, 10
J_V, J_CONV, J_O, J_OUT, J_WQ = 2, 4, 10, 12, 16
ADA_FIRST = 8
ADA_ALL = 24


class Tally:

    def __init__(self, eng, sem):
        self.eng, self.sem, self.base, self.k = eng, sem, 0, 0

    def loop(self, i, per):
        self.start, self.per = self.base + self.k, per
        self.base, self.k = i * per + self.start, 0

    def end(self, rounds):
        assert self.k == self.per, (self.k, self.per)
        self.base, self.k = self.start + rounds * self.per, 0

    def mark(self, ins):
        ins.then_inc(self.sem, 1)
        self.k += 1

    def settle(self):
        self.eng.wait_ge(self.sem, self.base + self.k)

    def link(self, ins):
        self.mark(ins)
        self.settle()


def build_layer(nc, x, c, w_ada, b_ada, w_in, b_in, conv_w, conv_b, mlstm_norm_w, w_out, ln1_w, ln1_b,
                peer_wq, peer_subkeys, peer_u, peer_v, ln2_w, ln2_b, out, alpha):
    with ExitStack() as ctx:
        def at(name, shape, offset, dt=F32):
            return nc.alloc_sbuf_tensor_at(name, shape, dt, offset=offset)

        def sem(name):
            return ctx.enter_context(nc.semaphore(name))

        KB = 1024
        base = (nc.sbuf_base + 31) // 32 * 32
        raw = [at(f"raw{s}", [P, 4, CH], base + 8 * KB * s) for s in range(SLABS)]
        o_split = base + 32 * KB
        w_hi = [at(f"w_hi{i}", [P, 4, CH], o_split + 8 * KB * i, F32R) for i in range(2)]
        w_lo = [at(f"w_lo{i}", [P, 4, CH], o_split + 16 * KB + 8 * KB * i, F32R) for i in range(2)]
        o_u = o_split + 32 * KB
        u_hi = at("u_hi", [P, KD, T], o_u, F32R)
        u_lo = at("u_lo", [P, KD, T], o_u + 32 * KB, F32R)

        o_const = [o_u + 64 * KB]

        def const(name, shape, dt=F32):
            t = at(name, shape, o_const[0], dt)
            n = 4
            for m in shape[1:]:
                n *= m
            o_const[0] += (n + 31) // 32 * 32
            return t

        ident = const("ident", [P, P])
        ones = const("ones", [P, P])
        iota = const("iota", [P, P])
        mask_fwd = const("mask_fwd", [P, P])
        mask_bwd = const("mask_bwd", [P, P])
        cond = const("cond", [P, KD])
        b_ada_c = const("b_ada_c", [P, 6 * KD])
        mod = const("mod", [P, 6 * KD])
        vec_c = const("vec_c", [P, 64])
        CONV_W, CONV_B = 32, 56
        gate_b = const("gate_b", [P, 1])
        stat = const("stat", [P, NT, 4, 6])
        mv = const("mv", [P, 4 * NT, 2])
        rstd = const("rstd", [P, 4 * NT])
        shift_n = const("shift_n", [P, NT])
        a_col = const("a_col", [P, 2, NT, HEADS])
        em_col = const("em_col", [P, 2, NT, HEADS])
        den = const("den", [P, 2, 2])
        step_hi = const("step_hi", [P, G_SLOTS, G_TOK], F32R)
        step_lo = const("step_lo", [P, G_SLOTS, G_TOK])
        W1 = o_const[0]
        H0 = W1 + 33024

        xz = at("xz", [P, NT, D], H0)
        u_f = [at(f"u_f{i}", [P, T], W1 + 16 * KB + 2 * KB * i) for i in range(4)]
        c_rows = at("c_rows", [KD, P], W1 + 24 * KB)
        c_sig = at("c_sig", [KD, P], W1 + 25 * KB)
        ada_rows = at("ada_rows", [6 * KD, P], W1 + 26 * KB)
        vec_rows = at("vec_rows", [64, P], W1 + 27 * KB)
        qk = at("qk", [P, 2, HEADS, T], W1)
        v_aug = at("v_aug", [P, NT, HEADS, DV + 2], W1 + 16 * KB)
        h_sum = at("h_sum", [P, NT, HEADS, DV], H0)
        g_hi = at("g_hi", [P, KD, P], o_split + 8 * KB, F32R)
        g_lo = at("g_lo", [P, KD, P], o_split + 24 * KB, F32R)
        gate_t = at("gate_t", [HEADS, 4, T], H0 + 16 * KB)
        g_raw = at("g_raw", [P, KD, 16], W1 + 8 * KB)
        prob = [at(f"prob{d}", [P, NT, T], H0 + (16 + 18 * d) * KB) for d in range(2)]
        v_bias = at("v_bias", [P, 2 * CH], H0 + 16 * KB)
        g_M = at("g_M", [HEADS, 2, T], H0 + 24 * KB)
        g_b = at("g_b", [HEADS, 2, T], H0 + 28 * KB)
        norm_row = at("norm_row", [P, HEADS * DV], H0 + 24 * KB)
        sel = at("sel", [HEADS, HEADS, P], H0 + 32 * KB)
        yc_hi = at("yc_hi", [P, 8, T], W1, F32R)
        yc_lo = at("yc_lo", [P, 8, T], W1 + 16 * KB, F32R)
        conv_h = at("conv_h", [P, MT, T], H0 + 16 * KB)
        conv_c = at("conv_c", [P, MT, T + 2], H0 + 24 * KB)
        o_sig = at("o_sig", [P, 4, CH], H0 + 16 * KB)
        o_bias = at("o_bias", [P, 2 * CH], H0 + 28 * KB)
        ada_acc = [at("ada_acc", [P, 4, CH], H0 + 34 * KB), at("ada_acc1", [P, 4, CH], W1)]
        assert H0 + 42 * KB + 96 <= nc.sbuf_usable_end, (H0 + 42 * KB, nc.sbuf_usable_end)
        g1_row = at("g1_row", [P, D], o_u + 16 * KB)
        ln1w_row = at("ln1w_row", [P, D], o_u + 24 * KB)
        ln1b_row = at("ln1b_row", [P, D], o_u + 48 * KB)
        diag = at("diag", [P, 4, P], o_u + 56 * KB)
        sk_raw = at("sk_raw", [P, 2 * PH, P], W1)
        sk_t = at("sk_t", [P, 2 * PH, P], H0 + 34 * KB)
        q_t = at("q_t", [P, 2 * PH, T], W1)
        scores = at("scores", [P, NT, 2 * PH, NK], H0)
        pick = [W1]

        def scratch(name, shape, dt=F32):
            t = at(name, shape, pick[0], dt)
            n = 4
            for m in shape[1:]:
                n *= m
            pick[0] += (n + 31) // 32 * 32
            return t

        ws = scratch("ws", [P, 2, NK])
        ws2 = scratch("ws2", [P, 2, NK])
        top_s = scratch("top_s", [P, 2, TOPK])
        top_i = scratch("top_i", [P, 2, TOPK], U32)
        top_f = scratch("top_f", [P, 2, TOPK])
        cand = scratch("cand", [P, TOPK, TOPK])
        cand2 = scratch("cand2", [P, TOPK, TOPK])
        best_s = scratch("best_s", [P, TOPK])
        best_c = scratch("best_c", [P, TOPK], U32)
        best_j = scratch("best_j", [P, 2, TOPK], U32)
        best_f = scratch("best_f", [P, 2, TOPK])
        hot = scratch("hot", [P, 2, TOPK, TOPK])
        neg_max = scratch("neg_max", [P, PH])
        g_exp = scratch("g_exp", [P, PH, TOPK])
        g_sum = scratch("g_sum", [P, PH])
        g_inv = scratch("g_inv", [P, PH])
        picks = scratch("picks", [P, 3, PH, TOPK])
        G_BATCH = 64
        STEPS_AT = [(9, 13, KD)] + [(5, 10, KD)] * 3 + [(10, KD)] * 2 + [(), ()]
        STEPS = G_BATCH // G_TOK
        assert sum(len(at_k) for at_k in STEPS_AT) == STEPS
        gates_sb = at("gates_sb", [P, NK, G_BATCH], W1)
        hot2 = [at(f"hot2_{i}", [P, G_TOK, NK], H0 + 8 * KB * i, F32R) for i in range(G_SLOTS)]
        hot1 = [at(f"hot1_{i}", [P, G_TOK, 2, NK], H0 + 8 * KB * i + 2 * KB, F32R) for i in range(G_SLOTS)]
        one_hot1 = [at(f"one_hot1_{i}", [P, G_TOK, NK], H0 + 8 * KB * i + 6 * KB) for i in range(G_SLOTS)]
        h_stage = [at(f"h_stage{i}", [P, T], H0 + (32 + 2 * i) * KB) for i in range(2)]
        by_pick = at("by_pick", [P, 3, T + 2 * G_TOK], H0 + 36 * KB)
        a_hi = [at(f"a_hi{i}", [P, 4, T], o_u + 8 * KB * i, F32R) for i in range(2)]
        a_lo = [at(f"a_lo{i}", [P, 4, T], o_u + 16 * KB + 8 * KB * i, F32R) for i in range(2)]
        h_in = [at(f"h_in{i}", [P, 4, T], H0 + 8 * KB * i) for i in range(2)]
        g_in = [at(f"g_in{i}", [P, 4, T], H0 + 16 * KB + 8 * KB * i) for i in range(2)]
        y_acc = at("y_acc", [P, NT, D], W1)
        x1 = at("x1", [P, NT, D], o_u + 32 * KB)
        g2_row = at("g2_row", [P, D], H0 + 34 * KB)
        ln2w_row = at("ln2w_row", [P, D], H0)
        ln2b_row = at("ln2b_row", [P, D], H0 + 16 * KB)

        ps = ctx.enter_context(nc.psum_tensor("ps", [P, 8, CH], F32))

        def batch_slice(q):
            return gates_sb[:, :, q * G_TOK:(q + 1) * G_TOK].rearrange("p a t -> p t a")

        def step_part(s):
            return ps[:, 6:8, :].rearrange("p b (t s a) -> p (b t) s a", s=2, a=NK)[:, :, s, :]

        x1_dram = nc.dram_tensor("x1_scratch", [T, D], F32, kind="Internal").ap()
        h_dram = nc.dram_tensor("h_scratch", [NE, T], F32, kind="Internal").ap()
        g_dram = nc.dram_tensor("g_scratch", [NE, T], F32, kind="Internal").ap()

        x_v = x.rearrange("b (n p) d -> p (b n) d", p=P)
        out_v = out.rearrange("b (n p) d -> p (b n) d", p=P)
        x1_v = x1_dram.rearrange("(n p) d -> p n d", p=P)
        ada_v = w_ada[0].rearrange("(k p) n -> p k n", p=P)
        win_v = w_in[0].rearrange("(k p) n -> p k n", p=P)
        wout_v = w_out[0].rearrange("(k p) n -> p k n", p=P)
        wq_v = peer_wq[0].rearrange("(k p) n -> p k n", p=P)
        pu_v = peer_u[0].rearrange("(e p) (k n) -> p e k n", p=P, n=CH)
        pv_v = peer_v[0].rearrange("(e p) n -> p e n", p=P)
        h_v = h_dram.rearrange("(e p) t -> p e t", p=P)
        g_v = g_dram.rearrange("(e p) t -> p e t", p=P)

        def row(v, lo, n):
            return v[0, lo:lo + n].partition_broadcast(P)

        c_in = sem("c_in")
        small_in = sem("small_in")
        g_raw_in = sem("g_raw_in")
        cond_turned = sem("cond_turned")
        norm_asked = sem("norm_asked")
        centred = sem("centred")
        x_in = sem("x_in")
        rows_in = sem("rows_in")
        slab_in = [sem(f"slab_in{s}") for s in range(SLABS)]
        const_made = sem("const_made")
        silu_made = sem("silu_made")
        first_turned = sem("first_turned")
        cond_ready = sem("cond_ready")
        x_normal = sem("x_normal")
        sqrt_asked = sem("sqrt_asked")
        sqrt_made = sem("sqrt_made")
        x_turned = sem("x_turned")
        mod_ready = sem("mod_ready")
        uf_made = sem("uf_made")
        uhi_made = sem("uhi_made")
        ulo_made = sem("ulo_made")
        ada_read = sem("ada_read")
        ada_half = sem("ada_half")
        ada_added = sem("ada_added")
        ada_reduced = sem("ada_reduced")
        ada_kept = sem("ada_kept")
        hi_made = sem("hi_made")
        lo_made = sem("lo_made")
        slab_used = sem("slab_used")
        tile_done = sem("tile_done")
        bank_free = sem("bank_free")
        gates_zero = sem("gates_zero")
        gates_hi = sem("gates_hi")
        gates_lo = sem("gates_lo")
        gate_b_in = sem("gate_b_in")
        norm_in = sem("norm_in")
        y_zero = sem("y_zero")
        gates_proj = sem("gates_proj")
        gate_step = sem("gate_step")
        gate_act = sem("gate_act")
        gates_turned = sem("gates_turned")
        cols_kept = sem("cols_kept")
        s_made = sem("s_made")
        m_made = sem("m_made")
        e_asked = sem("e_asked")
        e_made = sem("e_made")
        p_made = sem("p_made")
        hd_out = sem("hd_out")
        hd_kept = sem("hd_kept")
        conv_done = sem("conv_done")
        yhi_made = sem("yhi_made")
        ylo_made = sem("ylo_made")
        o_added = sem("o_added")
        o_sigd = sem("o_sigd")
        y_gated = sem("y_gated")
        y_turned = sem("y_turned")
        ym_hi = sem("ym_hi")
        ym_lo = sem("ym_lo")
        diag_made = sem("diag_made")
        row_made = sem("row_made")
        row_kept = sem("row_kept")
        x1_made = sem("x1_made")
        x1_out = sem("x1_out")
        sk_turned = sem("sk_turned")
        sk_kept = sem("sk_kept")
        sc_made = sem("sc_made")
        sc_kept = sem("sc_kept")
        u_turned = sem("u_turned")
        eu_hi = sem("eu_hi")
        eu_lo = sem("eu_lo")
        u_done = sem("u_done")
        h_made = sem("h_made")
        h_out = [sem(f"h_out{i}") for i in range(2)]
        gexp_asked = sem("gexp_asked")
        gexp_made = sem("gexp_made")
        picked = sem("picked")
        pick_turned = sem("pick_turned")
        pick_kept = sem("pick_kept")
        one_hot_made = sem("one_hot_made")
        hot_made = sem("hot_made")
        hot_lo_made = sem("hot_lo_made")
        g_done = sem("g_done")
        g_hi_kept = sem("g_hi_kept")
        g_kept = sem("g_kept")
        g_out = sem("g_out")
        batch_out = sem("batch_out")
        hg_in = [sem(f"hg_in{i}") for i in range(2)]
        a_mul = sem("a_mul")
        ahi_made = sem("ahi_made")
        alo_made = sem("alo_made")
        v_done = sem("v_done")
        v_free = sem("v_free")
        x1_back = sem("x1_back")
        out_made = sem("out_made")
        out_sent = sem("out_sent")
        dve_order = sem("dve_order")
        paced = sem("paced")
        act_order = sem("act_order")
        pool_order = sem("pool_order")

        NC = 20
        NB = ET // 4

        block = ctx.enter_context(nc.Block())

        @block.sync
        def _(sp):
            def load(s, src):
                sp.dma_start(raw[s][:, :, :], src).then_inc(slab_in[s], 16)

            sp.dma_start(c_rows[:, :], c.rearrange("b (k p) -> (b k) p", p=P)).then_inc(c_in, 16)
            for s in range(SLABS):
                load(s, ada_v[:, 4 * s:4 * s + 4, 0:CH])
            for n in range(NT):
                sp.dma_start(xz[:, n, :], x_v[:, n, :]).then_inc(x_in, 16)
            with sp.Fori(1, ADA_FIRST, 1) as g:
                for s in range(SLABS):
                    sp.wait_ge(ada_read, g * 4 + (s - 3))
                    load(s, ada_v[:, 4 * s:4 * s + 4, bass.ds(g * CH, CH)])

            def projection(j, src, col, ada):
                for s in range(SLABS):
                    sp.wait_ge(ada_read, j * 4 + (4 * ADA_FIRST - 4 + s + 1))
                    load(s, src[:, 4 * s:4 * s + 4, bass.ds(col, CH)])
                for s in range(SLABS):
                    sp.wait_ge(lo_made, j * 4 + (s + 1))
                    load(s, ada_v[:, 4 * s:4 * s + 4, bass.ds(ada * CH, CH)])

            with sp.Fori(0, 4, 1) as i:
                projection(i, win_v, (i + Q_CH) * CH, i + ADA_FIRST)
            with sp.Fori(0, 2, 1) as i:
                for r, first in enumerate((HIN_CH, GC_CH, GB_CH)):
                    projection(i * 3 + (J_CONV + r), win_v, (i + first) * CH, i * 3 + (J_CONV + r + ADA_FIRST))
            with sp.Fori(0, 2, 1) as i:
                projection(i + J_O, win_v, (i + O_CH) * CH, i + (J_O + ADA_FIRST))
            with sp.Fori(0, 4, 1) as i:
                projection(i + J_OUT, wout_v, i * CH, i + (J_OUT + ADA_FIRST))
            for s in range(SLABS):
                sp.wait_ge(ada_read, 4 * ADA_ALL - 4 + s + 1)
                load(s, wq_v[:, 4 * s:4 * s + 4, 0:CH])
            with sp.Fori(1, 4, 1) as i:
                for s in range(SLABS):
                    sp.wait_ge(lo_made, i * 4 + (4 * (J_WQ - 1) + s + 1))
                    load(s, wq_v[:, 4 * s:4 * s + 4, bass.ds(i * CH, CH)])
            for s in range(SLABS):
                sp.wait_ge(lo_made, 4 * (NC - 1) + s + 1)
                load(s, pu_v[:, s, :, :])
            with sp.Fori(1, NB, 1) as b:
                for s in range(SLABS):
                    sp.wait_ge(u_turned, b * 8 + (2 * s - 6))
                    load(s, pu_v[:, b * 4 + s, :, :])

            def load_hg(b, i, stored):
                if stored is not None:
                    sp.wait_ge(alo_made, stored)
                sp.dma_start(h_in[i][:, :, :], h_v[:, bass.ds(b * 4, 4), :]).then_inc(hg_in[i], 16)
                sp.dma_start(g_in[i][:, :, :], g_v[:, bass.ds(b * 4, 4), :]).then_inc(hg_in[i], 16)

            for par in range(2):
                sp.wait_ge(h_out[par], 16 * 48)
            sp.wait_ge(g_out, 32 * T // G_BATCH)
            sp.wait_ge(hot_made, T // G_TOK + 2)
            sp.wait_ge(hot_lo_made, T // G_TOK + 2)
            load_hg(0, 0, None)
            load_hg(1, 1, None)
            for s in range(SLABS):
                sp.wait_ge(u_turned, 2 * (ET - 4 + s + 1))
                load(s, pv_v[:, 0:4, s * CH:s * CH + CH])
            for s in range(SLABS):
                sp.wait_ge(lo_made, 4 * NC + s + 1)
                load(s, pv_v[:, 4:8, s * CH:s * CH + CH])
            with sp.Fori(1, NB // 2, 1) as r:
                for i in range(2):
                    for par in range(2):
                        sp.wait_ge(h_out[par], r * 64 + (32 * i + 32))
                    load_hg(r * 2 + i, i, r * 2 + (i - 1))
                    for s in range(SLABS):
                        sp.wait_ge(lo_made, r * 8 + (4 * i + 4 * NC - 4 + s + 1))
                        load(s, pv_v[:, bass.ds((r * 2 + i) * 4, 4), s * CH:s * CH + CH])
            for n in range(NT):
                sp.wait_ge(out_made, n + 1)
                sp.dma_start(out_v[:, n, :], x1[:, n, :]).then_inc(out_sent, 16)
            sp.wait_ge(out_sent, 16 * NT)
            sp.wait_ge(x1_out, 16 * NT)

        @block.gpsimd
        def _(pool):
            order = Tally(pool, pool_order)
            order.mark(pool.memset(ident[:, :], 0.0))
            order.mark(pool.memset(ones[:, :], 1.0))
            order.mark(pool.memset(sel[:, :, :], 0.0))
            order.mark(pool.memset(gate_b[:, :], 0.0))
            order.mark(pool.memset(g_hi[:, :, :].bitcast(F32), 0.0))
            order.mark(pool.memset(g_lo[:, :, :].bitcast(F32), 0.0))
            order.settle()
            order.mark(pool.affine_select(out=ident[:, :], in_=ident[:, :], compare_op=ALU.not_equal, fill=1.0,
                                          base=0, pattern=[[-1, P]], channel_multiplier=1))
            order.mark(pool.affine_select(out=mask_fwd[:, :], in_=ones[:, :], compare_op=ALU.is_ge, fill=0.0,
                                          base=0, pattern=[[1, P]], channel_multiplier=-1))
            order.mark(pool.affine_select(out=mask_bwd[:, :], in_=ones[:, :], compare_op=ALU.is_ge, fill=0.0,
                                          base=0, pattern=[[-1, P]], channel_multiplier=1))
            order.mark(pool.affine_select(out=sel[:, :, :], in_=sel[:, :, :], compare_op=ALU.not_equal, fill=1.0,
                                          base=0, pattern=[[-1, HEADS], [0, P]], channel_multiplier=1))
            order.mark(pool.iota(iota[:, :], [[1, P]], base=0, channel_multiplier=0,
                                 allow_small_or_imprecise_dtypes=True))
            order.settle()
            pool.sem_inc(const_made, 1)
            pool.sem_inc(gates_zero, 1)
            for g in range(4):
                pool.dma_start(gate_b[32 * g:32 * g + HEADS, :],
                               b_in[0, GATE_COL + HEADS * g:GATE_COL + HEADS * (g + 1)].unsqueeze(1)
                               ).then_inc(gate_b_in, 16)

            def ada_add(a, acc):
                pool.wait_ge(ada_read, a * 4 + 4)
                pool.tensor_tensor(acc[:, 0:2, :], acc[:, 0:2, :], acc[:, 2:4, :], ALU.add).then_inc(ada_half, 1)
                pool.wait_ge(ada_half, a + 1)
                pool.tensor_tensor(acc[:, 0, :], acc[:, 0, :], acc[:, 1, :], ALU.add).then_inc(ada_added, 1)

            with pool.Fori(0, ADA_FIRST // 2, 1) as i:
                for k in range(2):
                    ada_add(i * 2 + k, ada_acc[k])
            with pool.Fori(ADA_FIRST, ADA_FIRST + J_CONV, 1) as a:
                ada_add(a, ada_acc[0])
            with pool.Fori(0, 2, 1) as i:
                for r in range(3):
                    ada_add(i * 3 + (ADA_FIRST + J_CONV + r), ada_acc[0])
                for m in range(MT):
                    pool.wait_ge(yhi_made, i * MT + (m + 1))
                    pool.tensor_tensor(yc_lo[:, i * MT + m, :], conv_h[:, m, :],
                                       yc_hi[:, i * MT + m, :].bitcast(F32), ALU.subtract).then_inc(ylo_made, 1)
            with pool.Fori(ADA_FIRST + J_O, ADA_ALL, 1) as a:
                ada_add(a, ada_acc[0])

            def store_h(i, par, stage=0):
                pool.wait_ge(h_made, i + 1)
                pool.dma_start(h_v[:, i, :], h_stage[stage][:, :]).then_inc(h_out[par], 16)

            with pool.Fori(0, 16, 1) as i:
                for par in range(2):
                    store_h(i * 2 + par, par)

            def store_gates(b):
                pool.wait_ge(g_kept, b * STEPS + (STEPS + 1))
                for h in range(2):
                    keys = slice(h * NK // 2, (h + 1) * NK // 2)
                    pool.dma_start(g_dram.rearrange("(a b) t -> b a t", b=P)[:, keys, bass.ds(b * G_BATCH, G_BATCH)],
                                   gates_sb[:, keys, :]).then_inc(g_out, 16)

            def step_rows(b, q):
                i = q % G_SLOTS
                pool.wait_ge(one_hot_made, b * STEPS + (q + 1))
                pool.tensor_tensor(hot1[i][:, :, 1, :], one_hot1[i][:, :, :],
                                   step_lo[:, i, :].unsqueeze(2).to_broadcast([P, G_TOK, NK]), ALU.mult
                                   ).then_inc(hot_lo_made, 1)

            step_rows(0, 0)
            step_rows(0, 1)
            with pool.Fori(0, T // G_BATCH, 1) as b:
                q = 0
                for i in range(8):
                    for _k in STEPS_AT[i]:
                        step_rows(b, q + 2)
                        q += 1
                    store_h(b * 8 + (32 + i), i % 2, i % 2)
                    if i == 5:
                        store_gates(b)
                pool.wait_ge(g_out, b * 32 + 32)
                pool.sem_inc(batch_out, 1)
            pool.wait_ge(g_out, 32 * T // G_BATCH)
            pool.memset(y_acc[:, :, :], 0.0).then_inc(y_zero, 1)
            with pool.Fori(0, 16, 1) as i:
                for par in range(2):
                    store_h(i * 2 + (96 + par), par)

        @block.scalar
        def _(act):
            order = Tally(act, act_order)
            act.dma_start(ada_rows[:, :], b_ada[0].rearrange("(k p) -> k p", p=P)).then_inc(small_in, 16)
            act.dma_start(vec_rows[0:32, :], b_in[0, 0:32 * P].rearrange("(k p) -> k p", p=P)).then_inc(small_in, 16)
            act.dma_start(vec_rows[32:56, :], conv_w[0].rearrange("w (k p) -> (w k) p", p=P)).then_inc(small_in, 16)
            act.dma_start(vec_rows[56:64, :], conv_b[0].rearrange("(k p) -> k p", p=P)).then_inc(small_in, 16)
            act.dma_start(g_raw[:, :, :], win_v[:, :, GATE_COL:GATE_COL + 16]).then_inc(g_raw_in, 16)
            act.wait_ge(c_in, 16)
            act.activation(c_sig[:, :], c_rows[:, :], ACT.Sigmoid).then_inc(silu_made, 1)

            def root(n, width):
                act.wait_ge(sqrt_asked, n)
                act.activation(rstd[:, 0:width], rstd[:, 0:width], ACT.Sqrt).then_inc(sqrt_made, 1)

            def normal(tiles, asked):
                act.wait_ge(norm_asked, asked)
                for n in tiles:
                    act.activation(xz[:, n, :], xz[:, n, :], ACT.Identity, scale=rstd[:, n:n + 1],
                                   bias=shift_n[:, n:n + 1]).then_inc(x_normal, 1)

            def split_u(r, scale, shift):
                act.wait_ge(mod_ready, r + 1)
                with act.Fori(0, KD // 4, 1) as i:
                    order.loop(i, 2)
                    for k in range(4):
                        if k % 2:
                            act.wait_ge(x_turned, i * 4 + (KD * r + k + 1))
                            act.wait_ge(ulo_made, i * 4 + (KD * r + k + 1))
                            order.link(act.activation(u_f[k][:, :], ps[:, 4 + k, :], ACT.Identity,
                                                      scale=mod[:, bass.ds(i * 4 + (scale + k), 1)],
                                                      bias=mod[:, bass.ds(i * 4 + (shift + k), 1)]))
                        else:
                            act.wait_ge(uf_made, i * 2 + (KD // 2 * r + k // 2 + 1))
                        act.activation(u_hi[:, i * 4 + k, :], u_f[k][:, :], ACT.Copy).then_inc(uhi_made, 1)
                    order.end(KD // 4)

            def hi(s, loaded, used, count):
                act.wait_ge(slab_in[s], loaded)
                act.wait_ge(used, count)
                act.activation(w_hi[s % 2][:, :, :], raw[s][:, :, :], ACT.Copy).then_inc(hi_made, 1)

            def chunk(j, loaded, loaded_next, beside=None):
                hi(1, loaded, tile_done, 1 + j * 4)
                if beside:
                    beside()
                hi(2, loaded, slab_used, j * 3 + 1)
                hi(3, loaded, slab_used, j * 3 + 2)
                if loaded_next is not None:
                    hi(0, loaded_next, slab_used, j * 3 + 3)

            def paired(j, beside=None):
                chunk(j, j * 32 + 16 * (ADA_FIRST + 1), j * 32 + 16 * (ADA_FIRST + 3), beside)

            act.wait_ge(g_raw_in, 16)
            act.wait_ge(gates_zero, 1)
            for g in range(4):
                act.activation(g_hi[:, :, 32 * g:32 * g + HEADS], g_raw[:, :, HEADS * g:HEADS * (g + 1)], ACT.Copy
                               ).then_inc(gates_hi, 1)
            root(1, NT)
            normal(range(NT), 1)
            split_u(0, SC1, SH1)
            act.wait_ge(slab_in[0], 16 * (ADA_FIRST + 1))
            act.activation(w_hi[0][:, :, :], raw[0][:, :, :], ACT.Copy).then_inc(hi_made, 1)
            def gates():
                act.wait_ge(gate_step, 1)
                order.link(act.activation(g_M[:, :, :], gate_t[:, 1::2, :], ACT.Abs))
                order.link(act.activation(g_M[:, :, :], g_M[:, :, :], ACT.Exp, scale=-1.0))
                act.activation(g_M[:, :, :], g_M[:, :, :], ACT.Ln, bias=1.0).then_inc(gate_act, 1)
                act.wait_ge(gate_step, 2)
                act.activation(g_b[:, :, :], g_b[:, :, :], ACT.Exp, scale=-1.0).then_inc(gate_act, 1)

            act.wait_ge(gates_proj, 1)
            paired(0, gates)
            paired(1)
            act.wait_ge(cols_kept, 1)
            act.dma_start(v_bias[:, :], row(b_in, V_CH * CH, 2 * CH)).then_inc(rows_in, 16)
            with act.Fori(J_V, J_CONV, 1) as i:
                paired(i)
            for n in range(2 * HEADS):
                for st in range(NT):
                    act.wait_ge(e_asked, NT * n + st + 1)
                    lo_c, hi_c = (st * P, T) if n % 2 == 0 else (0, (st + 1) * P)
                    act.activation(prob[n % 2][:, st, lo_c:hi_c], prob[n % 2][:, st, lo_c:hi_c], ACT.Exp, scale=-1.0
                                   ).then_inc(e_made, 1)
            root(2, 4 * NT)
            with act.Fori(0, 2, 1) as i:
                for r in range(3):
                    paired(i * 3 + (J_CONV + r))
                for m in range(MT):
                    act.wait_ge(conv_done, i * MT + (m + 1))
                    act.activation(yc_hi[:, i * MT + m, :], conv_h[:, m, :], ACT.Copy).then_inc(yhi_made, 1)
            act.wait_ge(ylo_made, 12)
            act.dma_start(o_bias[:, :], row(b_in, O_CH * CH, 2 * CH)).then_inc(rows_in, 16)
            act.dma_start(norm_row[:, :], row(mlstm_norm_w, 0, HEADS * DV)).then_inc(norm_in, 16)
            with act.Fori(0, 2, 1) as i:
                paired(i + J_O)
                for t in range(NT):
                    act.wait_ge(o_added, i * NT + (t + 1))
                    act.activation(o_sig[:, t, :], o_sig[:, t, :], ACT.Sigmoid).then_inc(o_sigd, 1)
            for k in range(8):
                act.wait_ge(y_turned, k + 1)
                act.activation(u_hi[:, k, :], ps[:, 4 + k % 4, :], ACT.Copy).then_inc(ym_hi, 1)
            act.dma_start(ln1w_row[:, :], row(ln1_w, 0, D)).then_inc(rows_in, 16)
            act.dma_start(ln1b_row[:, :], row(ln1_b, 0, D)).then_inc(rows_in, 16)
            for n in range(NT):
                act.dma_start(xz[:, n, :], x_v[:, n, :]).then_inc(x_in, 16)
            with act.Fori(0, 3, 1) as i:
                paired(i + J_OUT)
            first_wq = 16 * (ADA_FIRST + 2 * J_WQ + 1)
            chunk(J_WQ - 1, first_wq - 32, first_wq)
            act.wait_ge(tile_done, 1 + 4 * J_WQ)
            act.dma_start(sk_raw[:, :, :], peer_subkeys[0].rearrange("h s n k -> n (h s) k")).then_inc(small_in, 16)
            root(3, NT)
            for n in range(NT):
                act.wait_ge(x1_made, n + 1)
                act.dma_start(x1_v[:, n, :], xz[:, n, :]).then_inc(x1_out, 16)
            root(4, NT)
            act.wait_ge(x1_out, 16 * NT)
            normal(range(2, NT), 2)
            split_u(1, SC2, SH2)
            with act.Fori(0, 3, 1) as i:
                chunk(i + J_WQ, i * 16 + first_wq, i * 16 + (first_wq + 16))
            chunk(NC - 1, first_wq + 48, None)

            def turn_hi(i, par):
                for h in range(2):
                    act.wait_ge(u_turned, i * 2 + (h + 1))
                    act.activation(w_hi[par][:, 2 * h:2 * h + 2, :], ps[:, 2 * h:2 * h + 2, :], ACT.Copy
                                   ).then_inc(eu_hi, 1)

            def gelu(i, par, stage=0):
                act.wait_ge(u_done, i + 1)
                act.activation(h_stage[stage][:, :], ps[:, 4 + par, :], ACT.Gelu).then_inc(h_made, 1)

            def stored(half, par):
                act.wait_ge(h_out[par], half * 16 + 16)

            act.wait_ge(tile_done, 1 + 4 * NC)
            turn_hi(0, 0)
            turn_hi(1, 1)
            act.sem_inc(gexp_made, 1)
            with act.Fori(0, NT, 1) as r:
                for h in range(PH):
                    gelu(r * 8 + h, h % 2)
                    act.wait_ge(gexp_asked, r * 8 + (h + 1))
                    act.activation(g_exp[:, h, :], best_s[:, :], ACT.Exp, bias=neg_max[:, h:h + 1],
                                   accum_out=g_sum[:, h:h + 1]).then_inc(gexp_made, 1)
                    turn_hi(r * 8 + (h + 2), h % 2)
                    stored(r * 4 + h // 2, h % 2)


            def keep_gates(b, q):
                act.wait_ge(g_done, b * STEPS + (q + 1 + G_SLOTS))
                if q == 0:
                    act.wait_ge(batch_out, b + 1)
                act.activation(batch_slice(q), step_part(0), ACT.Copy).then_inc(g_hi_kept, 1)

            with act.Fori(0, T // G_BATCH, 1) as b:
                q = 0
                for n in range(8):
                    for k in STEPS_AT[n]:
                        if k < KD:
                            keep_gates(b, q)
                            q += 1
                    gelu(b * 8 + (32 + n), n % 2, n % 2)
                    if KD in STEPS_AT[n]:
                        keep_gates(b, q)
                        q += 1
                    turn_hi(b * 8 + (34 + n), n % 2)
                    stored(b * 4 + (31 + n) // 2, (31 + n) % 2)
            with act.Fori(0, 15, 1) as r:
                for n in range(2):
                    gelu(r * 2 + (96 + n), n)
                    turn_hi(r * 2 + (98 + n), n)
                    stored(r + 48, n)
            gelu(ET - 2, 0)
            stored(ET // 2 - 1, 0)

            def v_hi(s, loaded, done):
                act.wait_ge(slab_in[s], loaded)
                if done is not None:
                    act.wait_ge(v_done, 1 + done)
                act.activation(w_hi[s % 2][:, :, :], raw[s][:, :, :], ACT.Copy).then_inc(hi_made, 1)

            def a_split(b, par, done):
                act.wait_ge(a_mul, b + 1)
                if done is not None:
                    act.wait_ge(v_done, 1 + done)
                act.activation(a_hi[par][:, :, :], h_in[par][:, :, :], ACT.Copy).then_inc(ahi_made, 1)

            def v_block(b, par, last):
                for dc in range(SLABS):
                    if dc < 3:
                        v_hi(dc + 1, b * 16 + 16 * 77, b * 16 + 4 * dc)
                    elif not last:
                        v_hi(0, b * 16 + 16 * 78, b * 16 + 12)
                    if dc == 1 and not last:
                        a_split(b + 1, 1 - par, b * 16)

            v_hi(0, 16 * 77, None)
            act.wait_ge(u_done, ET)
            a_split(0, 0, None)
            gelu(ET - 1, 1)
            act.dma_start(x1[:, :, :], x1_v).then_inc(x1_back, 16)
            with act.Fori(0, NB // 2 - 1, 1) as r:
                v_block(r * 2, 0, False)
                v_block(r * 2 + 1, 1, False)
            v_block(NB - 2, 0, False)
            act.wait_ge(alo_made, NB - 1)
            act.dma_start(ln2w_row[:, :], row(ln2_w, 0, D)).then_inc(rows_in, 16)
            act.dma_start(ln2b_row[:, :], row(ln2_b, 0, D)).then_inc(rows_in, 16)
            v_block(NB - 1, 1, True)
            root(5, NT)

        @block.vector
        def _(dve):
            order = Tally(dve, dve_order)
            dve.sem_inc(bank_free, 3)
            dve.sem_inc(v_free, 8)
            for counted_from_one in (ada_kept, pick_kept, g_kept, batch_out):
                dve.sem_inc(counted_from_one, 1)
            dve.sem_inc(ulo_made, 4)
            dve.sem_inc(ylo_made, 4)

            def root(n, width):
                order.settle()
                dve.tensor_scalar(rstd[:, 0:width], mv[:, 0:width, 1], LN_EPS, None, ALU.add).then_inc(sqrt_asked, 1)
                dve.wait_ge(sqrt_made, n)
                order.link(dve.reciprocal(rstd[:, 0:width], rstd[:, 0:width]))

            def row_stats(n):
                for q in range(4):
                    order.mark(dve.bn_stats(stat[:, n, q, :], xz[:, n, q * CH:(q + 1) * CH]))
                order.settle()
                order.mark(dve.bn_aggr(mv[:, n, :], stat[:, n, :, :]))

            def normal(n):
                return dve.tensor_scalar(xz[:, n, :], xz[:, n, :], mv[:, n, 0:1], rstd[:, n:n + 1],
                                         ALU.subtract, ALU.mult)

            def ask_normal():
                dve.scalar_tensor_tensor(shift_n[:, :], mv[:, 0:NT, 0], -1.0, rstd[:, 0:NT], ALU.mult, ALU.mult
                                         ).then_inc(norm_asked, 1)

            def affine(z, w_row, b_row, done, made):
                for n in range(NT):
                    dve.scalar_tensor_tensor(z[:, n, :], z[:, n, :], mv[:, n, 0:1], w_row[:, :],
                                             ALU.subtract, ALU.mult).then_inc(centred, 1)
                    dve.wait_ge(centred, done + n + 1)
                    dve.scalar_tensor_tensor(z[:, n, :], z[:, n, :], rstd[:, n:n + 1], b_row[:, :],
                                             ALU.mult, ALU.add).then_inc(made, 1)

            def split_u(r, scale, shift):
                with dve.Fori(0, KD // 4, 1) as i:
                    for k in (0, 2):
                        dve.wait_ge(x_turned, i * 4 + (KD * r + k + 1))
                        if k == 0:
                            dve.wait_ge(ulo_made, i * 4 + (KD * r + 4))
                        dve.tensor_scalar(u_f[k][:, :], ps[:, 4 + k, :], mod[:, bass.ds(i * 4 + (scale + k), 1)],
                                          mod[:, bass.ds(i * 4 + (shift + k), 1)], ALU.mult, ALU.add
                                          ).then_inc(uf_made, 1)
                    for k in range(4):
                        dve.wait_ge(uhi_made, i * 4 + (KD * r + k + 1))
                        dve.tensor_tensor(u_lo[:, i * 4 + k, :], u_f[k][:, :], u_hi[:, i * 4 + k, :].bitcast(F32),
                                          ALU.subtract).then_inc(ulo_made, 1)

            def lo(s, n):
                dve.wait_ge(hi_made, n)
                dve.tensor_tensor(w_lo[s % 2][:, :, :], raw[s][:, :, :], w_hi[s % 2][:, :, :].bitcast(F32),
                                  ALU.subtract).then_inc(lo_made, 1)

            def ada_chunk(a, loaded, acc, reduced):
                if reduced is not None:
                    dve.wait_ge(ada_reduced, reduced)
                for s in range(SLABS):
                    dve.wait_ge(slab_in[s], loaded)
                    if s:
                        dve.wait_ge(ada_read, a * 4 + s)
                    for k in range(4):
                        w, m = raw[s][:, k, :], cond[:, 4 * s + k:4 * s + k + 1]
                        if s == 0:
                            ins = dve.tensor_scalar(acc[:, k, :], w, m, None, ALU.mult)
                        else:
                            ins = dve.scalar_tensor_tensor(acc[:, k, :], w, m, acc[:, k, :],
                                                           ALU.mult, ALU.add)
                    ins.then_inc(ada_read, 1)

            def ada_keep(a):
                dve.wait_ge(ada_reduced, a + 1)
                dve.tensor_tensor(mod[:, bass.ds(a * 4, 4)], ps[:, 6, 0:4], b_ada_c[:, bass.ds(a * 4, 4)],
                                  ALU.add).then_inc(ada_kept, 1)

            def chunk(j, read_bank, beside={}):
                for s in range(1, SLABS):
                    lo(s, j * 4 + (s + 1))
                    if s in beside:
                        beside[s]()
                ada_chunk(j + ADA_FIRST, j * 32 + 16 * (ADA_FIRST + 2), ada_acc[0], j + ADA_FIRST)
                lo(0, j * 4 + 5)
                for m in range(MT):
                    dve.wait_ge(tile_done, 1 + j * 4 + (m + 1))
                    read_bank(m)
                ada_keep(j + ADA_FIRST)

            dve.wait_ge(silu_made, 1)
            dve.tensor_tensor(c_sig[:, :], c_rows[:, :], c_sig[:, :], ALU.mult).then_inc(cond_ready, 1)
            dve.wait_ge(cond_turned, 1)
            order.link(dve.tensor_copy(cond[:, :], ps[:, 0, 0:KD]))
            ada_chunk(0, 16, ada_acc[0], None)
            dve.wait_ge(first_turned, 1)
            order.mark(dve.tensor_copy(b_ada_c[:, :], ps[:, 7, 128:128 + 6 * KD]))
            order.mark(dve.tensor_copy(vec_c[:, :], ps[:, 7, 256:256 + 64]))
            order.settle()
            for g in range(4):
                dve.wait_ge(gates_hi, g + 1)
                dve.tensor_tensor(g_lo[:, :, 32 * g:32 * g + HEADS], g_raw[:, :, HEADS * g:HEADS * (g + 1)],
                                  g_hi[:, :, 32 * g:32 * g + HEADS].bitcast(F32), ALU.subtract).then_inc(gates_lo, 1)
            dve.wait_ge(x_in, 16 * NT)
            for n in range(NT):
                row_stats(n)
            root(1, NT)
            ask_normal()
            ada_chunk(1, 32, ada_acc[1], None)
            ada_keep(0)
            with dve.Fori(1, ADA_FIRST // 2, 1) as i:
                for k in range(2):
                    ada_chunk(i * 2 + k, i * 32 + 16 * (k + 1), ada_acc[k], i * 2 + (k - 1))
                    ada_keep(i * 2 + (k - 1))
            ada_keep(ADA_FIRST - 1)
            dve.wait_ge(ada_kept, 1 + ADA_FIRST)
            order.link(dve.tensor_scalar(mod[:, SC1:SC1 + KD], mod[:, SC1:SC1 + KD], 1.0, None, ALU.add))
            dve.sem_inc(mod_ready, 1)
            split_u(0, SC1, SH1)
            dve.wait_ge(ulo_made, 4 + KD)
            order.link(dve.memset(v_aug[:, :, :, DV:DV + 2], 1.0))
            lo(0, 1)
            def gates():
                dve.wait_ge(gate_b_in, 64)
                for g in range(4):
                    order.mark(dve.tensor_scalar(gate_t[:, g, :], ps[32 * g:32 * g + HEADS, 3, :],
                                                 gate_b[32 * g:32 * g + HEADS, :], None, ALU.add))
                order.settle()
                dve.sem_inc(bank_free, 1)
                dve.sem_inc(gate_step, 1)
                dve.wait_ge(gate_act, 1)
                f, i_g = gate_t[:, 1::2, :], gate_t[:, 0::2, :]
                order.link(dve.scalar_tensor_tensor(f, f, 0.0, g_M[:, :, :], ALU.min, ALU.subtract))
                f0, f1 = gate_t[:, 1, :], gate_t[:, 3, :]
                order.mark(dve.tensor_tensor_scan(g_b[:, 0, :], f0, f0, 0.0, ALU.add, ALU.min))
                order.mark(dve.tensor_tensor_scan(g_b[:, 1, ::-1], f1[:, ::-1], f1[:, ::-1], 0.0, ALU.add, ALU.min))
                order.settle()
                order.link(dve.tensor_tensor(i_g, i_g, g_b[:, :, :], ALU.subtract))
                a0, a1 = gate_t[:, 0, :], gate_t[:, 2, :]
                order.mark(dve.tensor_tensor_scan(g_M[:, 0, :], a0, a0, 0.0, ALU.max, ALU.max))
                order.mark(dve.tensor_tensor_scan(g_M[:, 1, ::-1], a1[:, ::-1], a1[:, ::-1], 0.0, ALU.max, ALU.max))
                order.settle()
                dve.tensor_tensor(g_b[:, :, :], g_b[:, :, :], g_M[:, :, :], ALU.add).then_inc(gate_step, 1)

            dve.wait_ge(gates_proj, 1)
            for i in range(2):
                def keep_qk(m):
                    dve.tensor_scalar(qk[:, i, m, :], ps[:, m, :], vec_c[:, bass.ds(i * MT + (Q_CH * MT + m), 1)],
                                      None, ALU.add).then_inc(bank_free, 1)
                chunk(i, keep_qk, {1: gates} if i == 0 else {})
            dve.wait_ge(gates_turned, 1)
            order.mark(dve.tensor_copy(a_col[:, :, :, :].rearrange("p d t h -> p (d t h)"), ps[:, 7, 0:32]))
            order.mark(dve.tensor_copy(em_col[:, :, :, :].rearrange("p d t h -> p (d t h)"), ps[:, 7, 32:64]))
            order.settle()
            dve.sem_inc(cols_kept, 1)
            dve.wait_ge(rows_in, 16)
            with dve.Fori(0, 2, 1) as i:
                def keep_v(t):
                    dve.tensor_tensor(v_aug[:, t, bass.ds(i * 2, 2), 0:DV],
                                      ps[:, t, :].rearrange("p (h v) -> p h v", h=2),
                                      v_bias[:, bass.ds(i * CH, CH)].rearrange("p (h v) -> p h v", h=2),
                                      ALU.add).then_inc(bank_free, 1)
                chunk(i + J_V, keep_v)
            dve.wait_ge(bank_free, 4 * J_CONV + 4)

            def live(d, st):
                return slice(st * P, T) if d == 0 else slice(0, (st + 1) * P)

            def exponents(n):
                h, d = n // 2, n % 2
                dve.wait_ge(m_made, h + 1)
                if n >= 2:
                    dve.wait_ge(hd_out, NT * (n - 1))
                for st in range(NT):
                    dve.tensor_scalar(prob[d][:, st, live(d, st)], ps[:, 4 + d, live(d, st)],
                                      a_col[:, d, st, h:h + 1], 0.0, ALU.subtract, ALU.max).then_inc(e_asked, 1)

            def weights(n):
                h, d = n // 2, n % 2
                for st in range(NT):
                    dve.wait_ge(e_made, NT * n + st + 1)
                    own = prob[d][:, st, st * P:(st + 1) * P]
                    order.mark(dve.tensor_tensor(own, own, (mask_fwd, mask_bwd)[d][:, :], ALU.mult))
                order.settle()
                for st in range(NT):
                    dve.wait_ge(s_made, NT * h + st + 1)
                    w = prob[d][:, st, live(d, st)]
                    dve.scalar_tensor_tensor(w, ps[:, st, live(d, st)], DK ** -0.5, w, ALU.mult, ALU.mult
                                             ).then_inc(p_made, 1)

            def outputs(n):
                h, d = n // 2, n % 2
                for k, t in enumerate(reversed(range(NT)) if d == 0 else range(NT)):
                    b = 6 + k % 2
                    dve.wait_ge(hd_out, NT * n + k + 1)
                    order.link(dve.tensor_scalar(den[:, k % 2, 0:1], ps[:, b, DV:DV + 1], -1.0,
                                                 em_col[:, d, t, h:h + 1], ALU.mult, ALU.max))
                    order.link(dve.tensor_tensor(den[:, k % 2, 0:1], ps[:, b, DV:DV + 1], den[:, k % 2, 0:1],
                                                 ALU.max))
                    order.link(dve.reciprocal(den[:, k % 2, 1:2], den[:, k % 2, 0:1]))
                    if d == 0:
                        dve.tensor_scalar(h_sum[:, t, h, :], ps[:, b, 0:DV], den[:, k % 2, 1:2], None, ALU.mult
                                          ).then_inc(hd_kept, 1)
                    else:
                        dve.scalar_tensor_tensor(h_sum[:, t, h, :], ps[:, b, 0:DV], den[:, k % 2, 1:2],
                                                 h_sum[:, t, h, :], ALU.mult, ALU.add).then_inc(hd_kept, 1)

            exponents(0)
            exponents(1)
            weights(0)
            for h in range(HEADS):
                weights(2 * h + 1)
                outputs(2 * h)
                if h < HEADS - 1:
                    exponents(2 * h + 2)
                outputs(2 * h + 1)
                if h < HEADS - 1:
                    weights(2 * h + 2)
                    exponents(2 * h + 3)
            dve.wait_ge(hd_kept, 8 * NT)
            for t in range(NT):
                for h in range(HEADS):
                    order.mark(dve.bn_stats(stat[:, t, h, :], h_sum[:, t, h, :]))
            order.settle()
            for t in range(NT):
                for h in range(HEADS):
                    order.mark(dve.bn_aggr(mv[:, 4 * t + h, :], stat[:, t, h, :]))
            root(2, 4 * NT)
            order.mark(dve.memset(conv_c[:, :, 0:1], 0.0))
            order.mark(dve.memset(conv_c[:, :, T + 1:T + 2], 0.0))
            order.settle()

            with dve.Fori(0, 2, 1) as i:
                order.loop(i, 3 * MT)

                def col(first, m):
                    return vec_c[:, bass.ds(i * MT + (first + m), 1)]

                def keep_h(m):
                    dve.wait_ge(ylo_made, i * MT + MT)
                    dve.tensor_scalar(conv_h[:, m, :], ps[:, m, :], col(HIN_CH * MT, m), None, ALU.add
                                      ).then_inc(bank_free, 1)

                def keep_c(m):
                    dve.scalar_tensor_tensor(conv_c[:, m, 1:T + 1], ps[:, m, :], col(GC_CH * MT, m),
                                             conv_h[:, m, :], ALU.add, ALU.mult).then_inc(bank_free, 1)

                def taps():
                    for k in range(3):
                        for m in range(MT):
                            src = conv_c[:, m, k:k + T]
                            if k == 0:
                                order.mark(dve.tensor_scalar(conv_h[:, m, :], src, col(CONV_W, m), col(CONV_B, m),
                                                             ALU.mult, ALU.add))
                            else:
                                order.mark(dve.scalar_tensor_tensor(conv_h[:, m, :], src, col(CONV_W + 8 * k, m),
                                                                    conv_h[:, m, :], ALU.mult, ALU.add))
                        order.settle()

                def keep_y(m):
                    dve.scalar_tensor_tensor(conv_h[:, m, :], ps[:, m, :], col(GB_CH * MT, m), conv_h[:, m, :],
                                             ALU.add, ALU.mult).then_inc(conv_done, 1)

                chunk(i * 3 + J_CONV, keep_h)
                dve.wait_ge(bank_free, i * 12 + (4 * J_CONV + 4 + 4))
                chunk(i * 3 + (J_CONV + 1), keep_c)
                dve.wait_ge(bank_free, i * 12 + (4 * J_CONV + 8 + 4))
                chunk(i * 3 + (J_CONV + 2), keep_y, {1: taps})
                dve.wait_ge(conv_done, i * MT + MT)
                dve.sem_inc(bank_free, 4)
                order.end(2)

            dve.wait_ge(rows_in, 32)
            dve.wait_ge(ylo_made, 12)
            dve.wait_ge(norm_in, 16)
            with dve.Fori(0, 2, 1) as i:
                order.loop(i, 2 * NT)

                def head(t, h):
                    return (h_sum[:, t, bass.ds(i * 2 + h, 1), :].rearrange("p h v -> p (h v)"),
                            bass.ds(i * 2 + (4 * t + h), 1))

                def centre():
                    for t in range(NT):
                        for h in range(2):
                            hs, q = head(t, h)
                            order.mark(dve.scalar_tensor_tensor(hs, hs, mv[:, q, 0:1].rearrange("p a b -> p (a b)"),
                                                                norm_row[:, bass.ds(i * 2 * DV + h * DV, DV)],
                                                                ALU.subtract, ALU.mult))

                def keep_o(t):
                    dve.tensor_tensor(o_sig[:, t, :], ps[:, t, :], o_bias[:, bass.ds(i * CH, CH)], ALU.add
                                      ).then_inc(o_added, 1)
                chunk(i + J_O, keep_o, {1: centre})
                order.settle()
                dve.wait_ge(o_added, i * NT + NT)
                dve.sem_inc(bank_free, 4)
                for t in range(NT):
                    dve.wait_ge(o_sigd, i * NT + (t + 1))
                    for h in range(2):
                        hs, q = head(t, h)
                        dve.scalar_tensor_tensor(hs, hs, rstd[:, q], o_sig[:, t, h * DV:(h + 1) * DV],
                                                 ALU.mult, ALU.mult).then_inc(y_gated, 1)
                order.end(2)
            for k in range(8):
                dve.wait_ge(ym_hi, k + 1)
                dve.tensor_tensor(u_lo[:, k, :], ps[:, 4 + k % 4, :], u_hi[:, k, :].bitcast(F32), ALU.subtract
                                  ).then_inc(ym_lo, 1)

            def spread_diag(col, tiles, q):
                w = len(tiles)
                for m in range(w):
                    order.mark(dve.tensor_scalar(tiles[m], ident[:, :], mod[:, bass.ds(q * w + (col + m), 1)], None,
                                                 ALU.mult))
                order.settle()
                dve.sem_inc(diag_made, 1)

            def spread_keep(dst, w, q, made):
                dve.wait_ge(row_made, made)
                dve.tensor_copy(dst[:, bass.ds(q * (w * P), w * P)], ps[:, 7, 0:w * P]).then_inc(row_kept, 1)

            with dve.Fori(0, 4, 1) as i:
                order.loop(i, 2 * NT + 4)

                def spread_g1():
                    spread_diag(G1, [diag[:, m, :] for m in range(4)], i)

                def keep_g1():
                    spread_keep(g1_row, 4, i, i + 1)
                    dve.wait_ge(row_kept, i + 2)
                    dve.wait_ge(x_in, 32 * NT)

                def keep_z(t):
                    order.link(dve.tensor_tensor(ps[:, t, :], ps[:, t, :], g1_row[:, bass.ds(i * CH, CH)], ALU.mult))
                    z = xz[:, t, bass.ds(i * CH, CH)]
                    dve.scalar_tensor_tensor(z, z, alpha, ps[:, t, :], ALU.mult, ALU.add).then_inc(bank_free, 1)

                chunk(i + J_OUT, keep_z, {1: spread_g1, 2: keep_g1})
                dve.wait_ge(bank_free, i * 4 + (4 * J_OUT + 8))
                for t in range(NT):
                    order.mark(dve.bn_stats(stat[:, t, bass.ds(i, 1), :].rearrange("p a b -> p (a b)"),
                                            xz[:, t, bass.ds(i * CH, CH)]))
                order.settle()
                order.end(4)
            dve.wait_ge(bank_free, 4 * J_WQ + 4)
            dve.wait_ge(ada_reduced, ADA_ALL)
            for q in range(4):
                dve.wait_ge(sk_turned, q + 1)
                dve.tensor_copy(sk_t[:, 4 * q:4 * q + 4, :], ps[:, q, :].rearrange("p (a b) -> p a b", a=4)
                                ).then_inc(sk_kept, 1)
            for n in range(NT):
                order.mark(dve.bn_aggr(mv[:, n, :], stat[:, n, :, :]))
            root(3, NT)
            dve.wait_ge(rows_in, 64)
            affine(xz, ln1w_row, ln1b_row, 0, x1_made)
            for n in range(NT):
                dve.wait_ge(x1_made, n + 1)
                row_stats(n)
            root(4, NT)
            ask_normal()
            dve.wait_ge(x1_out, 16 * NT)
            for n in range(2):
                normal(n).then_inc(x_normal, 1)
            dve.wait_ge(ada_kept, 1 + ADA_ALL)
            order.link(dve.tensor_scalar(mod[:, SC2:SC2 + KD], mod[:, SC2:SC2 + KD], 1.0, None, ALU.add))
            dve.sem_inc(mod_ready, 1)
            split_u(1, SC2, SH2)
            dve.wait_ge(ulo_made, 4 + 2 * KD)

            def q_chunk(i, last):
                for s in range(1, SLABS):
                    lo(s, i * 4 + (4 * J_WQ + s + 1))
                if not last:
                    lo(0, i * 4 + (4 * J_WQ + 5))
                for m in range(MT):
                    dve.wait_ge(tile_done, 1 + i * 4 + (4 * J_WQ + m + 1))
                    dve.tensor_copy(q_t[:, i * MT + m, :], ps[:, m, :]).then_inc(bank_free, 1)

            with dve.Fori(0, 3, 1) as i:
                q_chunk(i, False)
            q_chunk(3, True)
            with dve.Fori(0, NT, 1) as t:
                for g in range(4):
                    dve.wait_ge(sc_made, t * 4 + (g + 1))
                    dve.tensor_copy(scores[:, t, 4 * g:4 * g + 4, :], ps[:, 4 + g, :].rearrange("p (a b) -> p a b", a=4)
                                    ).then_inc(sc_kept, 1)

            def turn_lo(i, par):
                for h in range(2):
                    dve.wait_ge(eu_hi, i * 2 + (h + 1))
                    dve.tensor_tensor(w_lo[par][:, 2 * h:2 * h + 2, :], ps[:, 2 * h:2 * h + 2, :],
                                      w_hi[par][:, 2 * h:2 * h + 2, :].bitcast(F32), ALU.subtract).then_inc(eu_lo, 1)

            def pick(t, h, meanwhile=None):
                dve.wait_ge(gexp_made, t * 8 + (h + 1))
                order.link(dve.tensor_copy(ws[:, :, :], scores[:, t, 2 * h:2 * h + 2, :]))
                dve.sem_inc(paced, 1)
                for half, src in ((0, ws), (8, ws2)):
                    for s in range(2):
                        order.mark(dve.max(top_s[:, s, half:half + 8], src[:, s, :]))
                    order.settle()
                    dve.sem_inc(paced, 1)
                    for s in range(2):
                        order.mark(dve.max_index(top_i[:, s, half:half + 8], top_s[:, s, half:half + 8], src[:, s, :]))
                    if half == 0:
                        for s in range(2):
                            order.mark(dve.match_replace(ws2[:, s, :], top_s[:, s, 0:8], ws[:, s, :], LOWEST))
                    order.settle()
                    dve.sem_inc(paced, 1)
                order.mark(dve.tensor_copy(top_f[:, :, :], top_i[:, :, :]))
                order.link(dve.tensor_tensor(cand[:, :, :], top_s[:, 0, :].unsqueeze(2).to_broadcast([P, TOPK, TOPK]),
                                             top_s[:, 1, :].unsqueeze(1).to_broadcast([P, TOPK, TOPK]), ALU.add))
                flat, flat2 = (v[:, :, :].rearrange("p a b -> p (a b)") for v in (cand, cand2))
                dve.sem_inc(paced, 1)
                order.link(dve.max(best_s[:, 0:8], flat))
                dve.sem_inc(paced, 1)
                order.mark(dve.max_index(best_c[:, 0:8], best_s[:, 0:8], flat))
                order.link(dve.match_replace(flat2, best_s[:, 0:8], flat, LOWEST))
                dve.sem_inc(paced, 1)
                order.link(dve.max(best_s[:, 8:16], flat2))
                dve.sem_inc(paced, 1)
                order.mark(dve.max_index(best_c[:, 8:16], best_s[:, 8:16], flat2))
                dve.tensor_scalar(neg_max[:, h:h + 1], best_s[:, 0:1], -1.0, None, ALU.mult).then_inc(gexp_asked, 1)
                order.settle()
                order.mark(dve.tensor_scalar(best_j[:, 0, :], best_c[:, :], 4, None, ALU.logical_shift_right))
                order.link(dve.tensor_scalar(best_j[:, 1, :], best_c[:, :], 15, None, ALU.bitwise_and))
                order.link(dve.tensor_copy(best_f[:, :, :], best_j[:, :, :]))
                for s in range(2):
                    order.mark(dve.tensor_tensor(hot[:, s, :, :],
                                                 best_f[:, s, :].unsqueeze(2).to_broadcast([P, TOPK, TOPK]),
                                                 iota[:, 0:TOPK].unsqueeze(1).to_broadcast([P, TOPK, TOPK]),
                                                 ALU.is_equal))
                order.settle()
                for s in range(2):
                    order.mark(dve.tensor_tensor(hot[:, s, :, :], hot[:, s, :, :],
                                                 top_f[:, s, :].unsqueeze(1).to_broadcast([P, TOPK, TOPK]), ALU.mult))
                order.settle()
                if meanwhile:
                    meanwhile()
                for s in range(2):
                    order.mark(dve.tensor_reduce(picks[:, s, h, :], hot[:, s, :, :], AX_X, ALU.add))

            def step_rows(b, q):
                tok = bass.ds(b * G_BATCH + q * G_TOK, G_TOK)
                i = q % G_SLOTS
                shape = [P, G_TOK, NK]
                keys = iota[:, :].unsqueeze(1).to_broadcast(shape)
                dve.wait_ge(g_done, b * STEPS + (q + 1))
                order.mark(dve.tensor_copy(step_hi[:, i, :], by_pick[:, 2, tok]))
                order.mark(dve.tensor_tensor(one_hot1[i][:, :, :], by_pick[:, 0, tok].unsqueeze(2).to_broadcast(shape),
                                             keys, ALU.is_equal))
                order.settle()
                dve.tensor_tensor(step_lo[:, i, :], by_pick[:, 2, tok], step_hi[:, i, :].bitcast(F32),
                                  ALU.subtract).then_inc(one_hot_made, 1)
                order.mark(dve.tensor_tensor(hot2[i][:, :, :], by_pick[:, 1, tok].unsqueeze(2).to_broadcast(shape),
                                             keys, ALU.is_equal))
                dve.tensor_tensor(hot1[i][:, :, 0, :], one_hot1[i][:, :, :],
                                  step_hi[:, i, :].bitcast(F32).unsqueeze(2).to_broadcast(shape), ALU.mult
                                  ).then_inc(hot_made, 1)

            def keep_gates(b, q):
                dve.wait_ge(g_hi_kept, b * STEPS + (q + 1))
                dve.tensor_tensor(batch_slice(q), batch_slice(q), step_part(1), ALU.add).then_inc(g_kept, 1)

            turn_lo(0, 0)
            def keep_picks(r):
                dve.wait_ge(pick_turned, r + 1)
                order.link(dve.tensor_copy(by_pick[:, :, bass.ds(r * P, P)],
                                           ps[:, 6, 0:3 * P].rearrange("p (c t) -> p c t", c=3)))
                dve.sem_inc(pick_kept, 1)

            def pick_tile(r, meanwhile=None):
                for h in range(PH):
                    turn_lo(r * 8 + (h + 1), (h + 1) % 2)
                    pick(r, h, meanwhile if h == 0 else None)
                dve.wait_ge(gexp_made, r * 8 + (PH + 1))
                order.link(dve.reciprocal(g_inv[:, :], g_sum[:, :]))
                order.mark(dve.tensor_tensor(picks[:, 2, :, :], g_exp[:, :, :],
                                             g_inv[:, :].unsqueeze(2).to_broadcast([P, PH, TOPK]), ALU.mult))
                order.settle()
                dve.sem_inc(picked, 1)

            pick_tile(0)
            with dve.Fori(0, NT - 1, 1) as r:
                order.loop(r, PH * 27 + 3)
                pick_tile(r + 1, lambda: keep_picks(r))
                order.end(NT - 1)
            keep_picks(NT - 1)
            order.link(dve.memset(by_pick[:, :, T:T + 2 * G_TOK], 0.0))
            step_rows(0, 0)
            step_rows(0, 1)
            with dve.Fori(0, T // G_BATCH, 1) as b:
                order.loop(b, 3 * STEPS)
                q = 0
                for n in range(8):
                    turn_lo(b * 8 + (33 + n), (n + 1) % 2)
                    for _k in STEPS_AT[n]:
                        step_rows(b, q + 2)
                        keep_gates(b, q)
                        q += 1
                order.end(T // G_BATCH)
            dve.wait_ge(g_done, G_SLOTS + T // G_TOK)
            def spread_g2(q):
                spread_diag(G2, [mask_fwd[:, :], mask_bwd[:, :]], q)

            with dve.Fori(0, 7, 1) as r:
                order.loop(r, 2)
                for n in range(4):
                    turn_lo(r * 4 + (97 + n), (n + 1) % 2)
                    if n == 0:
                        spread_g2(r)
                    if n == 1:
                        dve.wait_ge(h_out[1], 16 * 48)
                        spread_keep(g2_row, 2, r, r + 5)
                order.end(7)
            turn_lo(ET - 3, 1)
            spread_g2(7)
            turn_lo(ET - 2, 0)
            spread_keep(g2_row, 2, 7, 12)
            turn_lo(ET - 1, 1)

            def gated(b, par):
                dve.wait_ge(hg_in[par], (b >> 1) * 32 + 32 if isinstance(b, int) else b * 16 + 32 - 16 * par)
                dve.tensor_tensor(h_in[par][:, :, :], h_in[par][:, :, :], g_in[par][:, :, :], ALU.mult
                                  ).then_inc(a_mul, 1)

            def gated_lo(b, par):
                dve.wait_ge(ahi_made, b + 1)
                dve.tensor_tensor(a_lo[par][:, :, :], h_in[par][:, :, :], a_hi[par][:, :, :].bitcast(F32),
                                  ALU.subtract).then_inc(alo_made, 1)

            def v_block(b, par, last):
                for dc in range(SLABS):
                    if dc < 3 or not last:
                        lo((dc + 1) % 4, b * 4 + (4 * NC + dc + 2))
                    if dc == 0 and not last:
                        gated(b + 1, 1 - par)
                    if dc == 1 and not last:
                        gated_lo(b + 1, 1 - par)
                    for t in range(NT):
                        dve.wait_ge(v_done, 1 + b * 16 + (4 * dc + t + 1))
                        y = y_acc[:, t, dc * CH:(dc + 1) * CH]
                        dve.tensor_tensor(y, y, ps[:, (4 * dc + t) % 8, :], ALU.add).then_inc(v_free, 1)

            gated(0, 0)
            lo(0, 4 * NC + 1)
            gated_lo(0, 0)
            dve.wait_ge(y_zero, 1)
            with dve.Fori(0, NB // 2 - 1, 1) as r:
                v_block(r * 2, 0, False)
                v_block(r * 2 + 1, 1, False)
            v_block(NB - 2, 0, False)
            dve.wait_ge(x1_back, 16)
            dve.wait_ge(row_kept, 13)
            for dc in range(SLABS):
                if dc < 3:
                    lo(dc + 1, 4 * NC + 4 * (NB - 1) + dc + 2)
                cols = slice(dc * CH, (dc + 1) * CH)
                for t in range(NT):
                    dve.wait_ge(v_done, 16 * (NB - 1) + 4 * dc + t + 2)
                    dve.tensor_tensor(y_acc[:, t, cols], y_acc[:, t, cols], ps[:, (4 * dc + t) % 8, :], ALU.add
                                      ).then_inc(v_free, 1)
                dve.wait_ge(v_free, 8 + 16 * (NB - 1) + 4 * dc + NT)
                for t in range(NT):
                    order.mark(dve.tensor_tensor(y_acc[:, t, cols], y_acc[:, t, cols], g2_row[:, cols], ALU.mult))
                order.settle()
                for t in range(NT):
                    order.mark(dve.scalar_tensor_tensor(x1[:, t, cols], x1[:, t, cols], alpha, y_acc[:, t, cols],
                                                        ALU.mult, ALU.add))
                order.settle()
                for t in range(NT):
                    order.mark(dve.bn_stats(stat[:, t, dc, :], x1[:, t, cols]))
            order.settle()
            for n in range(NT):
                order.mark(dve.bn_aggr(mv[:, n, :], stat[:, n, :, :]))
            root(5, NT)
            dve.wait_ge(rows_in, 96)
            affine(x1, ln2w_row, ln2b_row, NT, out_made)

        @block.tensor
        def _(pe):
            for counted_from_one in (tile_done, v_done, row_kept):
                pe.sem_inc(counted_from_one, 1)
            pe.sem_inc(g_done, G_SLOTS)
            def ada_reduce(a, acc=ada_acc[0]):
                pe.wait_ge(ada_added, a + 1)
                pe.wait_ge(ada_kept, 1 + a)
                for m in range(4):
                    mm = pe.matmul(ps[:, 6, m:m + 1], acc[:, 0, m * P:(m + 1) * P], ones[:, 0:1],
                                   start=True, stop=True)
                mm.then_inc(ada_reduced, 1)

            def turn_x(r):
                pe.wait_ge(x_normal, NT * (r + 1))
                pe.wait_ge(ada_kept, 1 + (ADA_FIRST if r == 0 else ADA_ALL))
                for k in range(KD):
                    if k >= 4:
                        pe.wait_ge(uhi_made, KD * r + k - 3)
                        if k % 2 == 0:
                            pe.wait_ge(uf_made, KD // 2 * r + k // 2 - 1)
                    for n in range(NT):
                        mm = pe.transpose(ps[:, 4 + k % 4, n * P:(n + 1) * P], xz[:, n, k * P:(k + 1) * P],
                                          ident[:, :])
                    mm.then_inc(x_turned, 1)

            def three(bank, stat_hi, stat_lo, mov_hi, mov_lo, first, last):
                pe.matmul(bank, stat_hi, mov_hi, start=first, stop=False)
                pe.matmul(bank, stat_hi, mov_lo, start=False, stop=False)
                return pe.matmul(bank, stat_lo, mov_hi, start=False, stop=last)

            def u_tile(k):
                return u_hi[:, k, :], u_lo[:, k, :]

            def y_tile(k):
                if k < 8:
                    return yc_hi[:, k, :], yc_lo[:, k, :]
                return u_hi[:, k - 8, :], u_lo[:, k - 8, :]

            def chunk(j, feature_major, tile=u_tile, split=None, midway=None):
                for s in range(SLABS):
                    if s == 2 and midway:
                        midway()
                    if split is not None:
                        pe.wait_ge(ulo_made, split + 4 * (s + 1))
                    pe.wait_ge(lo_made, j * 4 + (s + 1))
                    wh, wl = w_hi[s % 2], w_lo[s % 2]
                    for m in range(MT):
                        if s == 0:
                            pe.wait_ge(bank_free, j * 4 + (m + 1))
                        own = slice(m * P, (m + 1) * P)
                        for k in range(4):
                            uh, ul = tile(4 * s + k)
                            first, last = s == 0 and k == 0, s == 3 and k == 3
                            if feature_major:
                                mm = three(ps[:, m, :], wh[:, k, own], wl[:, k, own], uh, ul, first, last)
                            else:
                                mm = three(ps[:, m, :], uh[:, own], ul[:, own], wh[:, k, :], wl[:, k, :], first, last)
                        if s == 3:
                            mm.then_inc(tile_done, 1)
                    if s < 3:
                        mm.then_inc(slab_used, 1)

            pe.wait_ge(const_made, 1)
            pe.wait_ge(cond_ready, 1)
            pe.transpose(ps[:, 0, 0:KD], c_sig[:, :], ident[0:KD, 0:KD]).then_inc(cond_turned, 1)
            pe.wait_ge(small_in, 64)
            pe.transpose(ps[:, 7, 128:128 + 6 * KD], ada_rows[:, :], ident[0:6 * KD, 0:6 * KD])
            pe.transpose(ps[:, 7, 256:256 + 64], vec_rows[:, :], ident[0:64, 0:64]).then_inc(first_turned, 1)
            with pe.Fori(0, ADA_FIRST // 2, 1) as i:
                for k in range(2):
                    ada_reduce(i * 2 + k, ada_acc[k])
            turn_x(0)
            pe.wait_ge(gates_lo, 4)
            for k in range(KD):
                pe.wait_ge(ulo_made, 4 + k + 1)
                mm = three(ps[:, 3, :], g_hi[:, k, :], g_lo[:, k, :], *u_tile(k), k == 0, k == KD - 1)
            mm.then_inc(gates_proj, 1)
            with pe.Fori(0, 2, 1) as i:
                chunk(i, True)
                ada_reduce(i + ADA_FIRST)
            pe.wait_ge(gate_step, 2)
            pe.wait_ge(gate_act, 2)
            for d in range(2):
                for t in range(NT):
                    c0 = (d * NT + t) * HEADS
                    pe.transpose(ps[:, 7, c0:c0 + HEADS], gate_t[:, 2 * d, t * P:(t + 1) * P],
                                 ident[0:HEADS, 0:HEADS])
                    mm = pe.transpose(ps[:, 7, 32 + c0:32 + c0 + HEADS], g_b[:, d, t * P:(t + 1) * P],
                                      ident[0:HEADS, 0:HEADS])
            mm.then_inc(gates_turned, 1)
            with pe.Fori(0, 2, 1) as i:
                chunk(i + J_V, False)
                ada_reduce(i + (ADA_FIRST + J_V))
            pe.wait_ge(ada_kept, 1 + ADA_FIRST + J_CONV)
            pe.wait_ge(bank_free, 4 * J_CONV + 4)
            def head_inputs(h):
                if h:
                    pe.wait_ge(e_asked, 2 * NT * h)
                for d in range(2):
                    mm = pe.matmul(ps[:, 4 + d, :], sel[:, h, :], g_M[:, d, :], start=True, stop=True)
                mm.then_inc(m_made, 1)
                if h:
                    pe.wait_ge(p_made, 2 * NT * h)
                for st in range(NT):
                    pe.matmul(ps[:, st, :], qk[:, 1, h, st * P:(st + 1) * P], qk[:, 0, h, :], start=True, stop=True
                              ).then_inc(s_made, 1)

            def head_outputs(n):
                h, d = n // 2, n % 2
                pe.wait_ge(p_made, NT * (n + 1))
                for k, t in enumerate(reversed(range(NT)) if d == 0 else range(NT)):
                    if NT * n + k >= 2:
                        pe.wait_ge(hd_kept, NT * n + k - 1)
                    sts = list(range(t + 1)) if d == 0 else list(range(t, NT))
                    for st in sts:
                        mm = pe.matmul(ps[:, 6 + k % 2, 0:DV + 1], prob[d][:, st, t * P:(t + 1) * P],
                                       v_aug[:, st, h, 0:DV + 1], start=st == sts[0], stop=st == sts[-1])
                    mm.then_inc(hd_out, 1)

            head_inputs(0)
            for h in range(HEADS):
                head_outputs(2 * h)
                if h < HEADS - 1:
                    head_inputs(h + 1)
                head_outputs(2 * h + 1)
            pe.wait_ge(hd_kept, 8 * NT)
            with pe.Fori(0, 2, 1) as i:
                for r in range(3):
                    chunk(i * 3 + (J_CONV + r), True)
                    ada_reduce(i * 3 + (ADA_FIRST + J_CONV + r))
            with pe.Fori(0, 2, 1) as i:
                chunk(i + J_O, False)
                ada_reduce(i + (ADA_FIRST + J_O))
            pe.wait_ge(y_gated, 4 * NT)
            pe.wait_ge(ada_kept, 1 + ADA_FIRST + J_OUT)
            for k in range(8):
                if k >= 4:
                    pe.wait_ge(ym_lo, k - 3)
                for t in range(NT):
                    mm = pe.transpose(ps[:, 4 + k % 4, t * P:(t + 1) * P],
                                      h_sum[:, t, k // 2, (k % 2) * P:(k % 2 + 1) * P], ident[:, :])
                mm.then_inc(y_turned, 1)

            def spread(tiles, made):
                pe.wait_ge(diag_made, made)
                pe.wait_ge(row_kept, made)
                for m in range(len(tiles)):
                    mm = pe.matmul(ps[:, 7, m * P:(m + 1) * P], ones[:, :], tiles[m], start=True, stop=True)
                mm.then_inc(row_made, 1)

            pe.wait_ge(ym_lo, 8)
            pe.wait_ge(ylo_made, 12)
            with pe.Fori(0, 4, 1) as i:
                chunk(i + J_OUT, False, y_tile, midway=lambda: spread([diag[:, m, :] for m in range(4)], i + 1))
                ada_reduce(i + (ADA_FIRST + J_OUT))
            pe.wait_ge(bank_free, 4 * J_WQ + 4)
            pe.wait_ge(small_in, 80)
            for q in range(4):
                for m in range(4):
                    mm = pe.transpose(ps[:, q, m * P:(m + 1) * P], sk_raw[:, 4 * q + m, :], ident[:, :])
                mm.then_inc(sk_turned, 1)
            turn_x(1)
            pe.wait_ge(sk_kept, 4)
            with pe.Fori(0, 4, 1) as i:
                chunk(i + J_WQ, True, split=4 + KD)
            pe.wait_ge(bank_free, 4 * NC + 4)
            for t in range(NT):
                for g in range(4):
                    if t:
                        pe.wait_ge(sc_kept, 4 * (t - 1) + g + 1)
                    for m in range(4):
                        mm = pe.matmul(ps[:, 4 + g, m * P:(m + 1) * P], q_t[:, 4 * g + m, t * P:(t + 1) * P],
                                       sk_t[:, 4 * g + m, :], start=True, stop=True)
                    mm.then_inc(sc_made, 1)
            pe.wait_ge(sc_kept, 16)

            def turn_u(i, slot, loaded, read):
                pe.wait_ge(slab_in[slot], loaded)
                for h in range(2):
                    if read is not None:
                        pe.wait_ge(eu_lo, read + h)
                    for k in range(8 * h, 8 * h + 8):
                        own = slice((k % 4) * P, (k % 4 + 1) * P)
                        mm = pe.transpose(ps[:, k // 4, own], raw[slot][:, k // 4, own], ident[:, :])
                    mm.then_inc(u_turned, 1)

            def u_products(i, par, between={}):
                pe.wait_ge(eu_lo, i * 2 + 2)
                for k in range(KD):
                    if k in between:
                        between[k]()
                    own = slice((k % 4) * P, (k % 4 + 1) * P)
                    mm = three(ps[:, 4 + par, :], w_hi[par][:, k // 4, own], w_lo[par][:, k // 4, own], *u_tile(k),
                               k == 0, k == KD - 1)
                mm.then_inc(u_done, 1)

            def u_step(i, n, loaded, between={}):
                turn_u(i + 1, (n + 1) % 4, loaded, i * 2 + 1)
                u_products(i, n % 2, between)
                if KD in between:
                    between[KD]()

            def step_products(b, q):
                pe.wait_ge(hot_made, b * STEPS + (q + 1))
                pe.wait_ge(hot_lo_made, b * STEPS + (q + 1))
                pe.wait_ge(g_kept, b * STEPS + (q + 1))
                for t in range(G_TOK):
                    mm = pe.matmul(ps[:, 6 + t // 2, (t % 2) * 2 * NK:(t % 2 + 1) * 2 * NK],
                                   hot2[q % G_SLOTS][:, t, :],
                                   hot1[q % G_SLOTS][:, t, :, :].rearrange("p s a -> p (s a)"), start=True, stop=True)
                mm.then_inc(g_done, 1)

            turn_u(0, 0, 16 * 45, None)
            def turn_picks(r):
                pe.wait_ge(picked, r + 1)
                pe.wait_ge(pick_kept, 1 + r)
                for c in range(3):
                    mm = pe.transpose(ps[:, 6, c * P:(c + 1) * P], picks[:, c, :, :].rearrange("p h k -> p (h k)"),
                                      ident[:, :])
                mm.then_inc(pick_turned, 1)

            for n in range(8):
                u_step(n, n, 16 * (45 + (n + 1) // 4))
            with pe.Fori(0, NT - 1, 1) as r:
                for n in range(8):
                    u_step(r * 8 + (8 + n), n, r * 32 + 16 * (47 + (n + 1) // 4),
                           {KD // 2: lambda: turn_picks(r)} if n == 0 else {})
            turn_picks(NT - 1)
            pe.wait_ge(pick_kept, 1 + NT)
            with pe.Fori(0, T // G_BATCH, 1) as b:
                for n in range(8):
                    first = sum(len(at_k) for at_k in STEPS_AT[:n])
                    u_step(b * 8 + (32 + n), n, b * 32 + 16 * (53 + (n + 1) // 4),
                           {k: lambda q=first + j: step_products(b, q) for j, k in enumerate(STEPS_AT[n])})
            pe.wait_ge(g_kept, 1 + T // G_TOK)

            def spread_g2(made):
                spread([mask_fwd[:, :], mask_bwd[:, :]], made)

            with pe.Fori(0, 7, 1) as r:
                for n in range(4):
                    u_step(r * 4 + (96 + n), n, r * 16 + 16 * (69 + (n + 1) // 4),
                           {KD // 2: lambda: spread_g2(r + 5)} if n == 1 else {})
            for n in range(3):
                u_step(124 + n, n, 16 * 76, {KD // 2: lambda: spread_g2(12)} if n == 1 else {})
            u_products(ET - 1, 1)

            def v_block(b, par):
                pe.wait_ge(alo_made, b + 1)
                for dc in range(SLABS):
                    pe.wait_ge(lo_made, b * 4 + (4 * NC + dc + 1))
                    for t in range(NT):
                        pe.wait_ge(v_free, b * 16 + (4 * dc + t + 1))
                        own = slice(t * P, (t + 1) * P)
                        for e in range(4):
                            mm = three(ps[:, (4 * dc + t) % 8, :], a_hi[par][:, e, own], a_lo[par][:, e, own],
                                       w_hi[dc % 2][:, e, :], w_lo[dc % 2][:, e, :], e == 0, e == 3)
                        mm.then_inc(v_done, 1)

            pe.wait_ge(h_made, ET)
            with pe.Fori(0, NB // 2, 1) as r:
                for i in range(2):
                    v_block(r * 2 + i, i)


_INS = ['x', 'c', 'w_ada', 'b_ada', 'w_in', 'b_in', 'conv_w', 'conv_b', 'mlstm_norm_w', 'w_out', 'ln1_w', 'ln1_b',
        'peer_wq', 'peer_subkeys', 'peer_u', 'peer_v', 'ln2_w', 'ln2_b']
_OUT = (1, T, D)


def kernel(**inputs):
    import concourse.bacc as _bacc
    from concourse.bass_utils import run_bass_kernel_spmd as _run

    nc = _bacc.Bacc("TRN2", target_bir_lowering=False, num_devices=1)
    arrays, args = {}, []
    for name in _INS:
        a = np.ascontiguousarray(inputs[name])
        arrays[f"in_{name}_dram"] = a
        args.append(nc.dram_tensor(f"in_{name}_dram", a.shape, mybir.dt.from_np(a.dtype), kind="ExternalInput").ap())
    args.append(nc.dram_tensor("out_dram", _OUT, F32, kind="ExternalOutput").ap())
    build_layer(nc, *args, alpha=2.0 ** 0.25)
    r = _run(nc, [arrays], core_ids=[0])
    return r.results[0]["out_dram"]
```
